# Optimizing a Trainium2 kernel written in Bass

```python
import math
import jax, jax.numpy as jnp
from jax import lax
import numpy as np

D_MODEL = 1024
BATCH = 1
SEQ = 128
DEPTH = 1
DEC_BATCH = 1
DEC_SEQ = 512
PAST_LEN = 128

GRID_W = 64
D_MIX = D_MODEL
D_HY = D_MIX // 2
D_RET = D_MIX - D_HY
N_RET_HEADS = 4
RET_DK = D_RET // N_RET_HEADS
RET_DV = D_RET // N_RET_HEADS
RET_CHUNK = 128
ROPE_BASE = 10000.0
HY_ORDER = 2
HY_SHORT = 3
HY_EMB = 33
HY_BANDS = (HY_EMB - 1) // 2
HY_FILT_W = 64
HY_DECAY_TARGET = 1e-2
HY_FAST_PCT = 0.3
HY_SLOW_PCT = 1.5
D_IN = 3 * D_HY + 4 * D_RET
N_KEYS = 128
N_EXPERTS = N_KEYS * N_KEYS
PEER_HEADS = 8
PEER_TOPK = 16
PEER_DQ = 256
PEER_BLOCK = 128
N_MOD = 6

kernel_name = 'hyena_retnet_peer_hybrid_step'

F32 = jnp.float32

def _rmsnorm(x, g, eps=1e-6):
    xf = x.astype(F32)
    y = xf * lax.rsqrt(jnp.mean(xf * xf, axis=-1, keepdims=True) + eps)
    return (y * g.astype(F32)).astype(x.dtype)

def _modulate(h, shift, scale):
    return h * (1.0 + scale[:, None, :]) + shift[:, None, :]

def _short_conv(u, w, b):
    L = u.shape[1]
    pad = HY_SHORT // 2
    up = jnp.pad(u, ((0, 0), (pad, HY_SHORT - 1 - pad), (0, 0)))
    out = b
    for j in range(HY_SHORT):
        out = out + up[:, j:j + L] * w[j]
    return out

def _hyena_filters(L, w1, b1, w2, b2, w3, b3, w4, freq):
    t = jnp.linspace(0.0, 1.0, L, dtype=F32)[:, None]
    w = 2.0 * math.pi * jnp.arange(L, dtype=F32)[:, None] / L
    f = jnp.linspace(1e-4, HY_BANDS - 1, HY_BANDS, dtype=F32)[None, :]
    z = jnp.concatenate([t, jnp.cos(f * w), -jnp.sin(f * w)], axis=-1).astype(w1.dtype)
    h = jnp.sin(freq * (z @ w1 + b1))
    h = jnp.sin(freq * (h @ w2 + b2))
    h = jnp.sin(freq * (h @ w3 + b3))
    h = (h @ w4).astype(F32).reshape(L, 2, HY_ORDER, D_HY)
    min_decay = math.log(HY_DECAY_TARGET) / HY_SLOW_PCT
    max_decay = math.log(HY_DECAY_TARGET) / HY_FAST_PCT
    deltas = jnp.abs(jnp.linspace(min_decay, max_decay, D_HY, dtype=F32))
    window = jnp.exp(-t * deltas[None, :])
    h = h * window[:, None, None, :]
    h_fwd, h_bwd = h[:, 0], h[:, 1]
    return jnp.concatenate([h_fwd, jnp.zeros((1, HY_ORDER, D_HY), F32), h_bwd[1:][::-1]], axis=0)

def _long_conv(u, k, bias):
    L = u.shape[1]
    uf = jnp.fft.rfft(u.astype(F32), n=2 * L, axis=1)
    kf = jnp.fft.rfft(k, n=2 * L, axis=0)
    y = jnp.fft.irfft(uf * kf[None], n=2 * L, axis=1)[:, :L]
    return (y + u.astype(F32) * bias.astype(F32)).astype(u.dtype)

def _hyena_mixer(p, conv_w, conv_b, w1, b1, w2, b2, w3, b3, w4, freq, fbias):
    L = p.shape[1]
    u = _short_conv(p, conv_w, conv_b)
    v, x1, x2 = jnp.split(u, 3, axis=-1)
    k = _hyena_filters(L, w1, b1, w2, b2, w3, b3, w4, freq)
    z = x1 * _long_conv(v, k[:, 0], fbias[0])
    z = x2 * _long_conv(z, k[:, 1], fbias[1])
    return z

def _axial_rope(x):
    L = x.shape[2]
    rows = L // GRID_W
    r, c = jnp.meshgrid(jnp.arange(rows, dtype=F32), jnp.arange(GRID_W, dtype=F32), indexing='ij')
    r = r.reshape(-1)
    c = c.reshape(-1)
    nf = RET_DK // 4
    inv = ROPE_BASE ** (-jnp.arange(nf, dtype=F32) / nf)
    ang = jnp.concatenate([r[:, None] * inv, c[:, None] * inv], axis=-1)
    cos = jnp.concatenate([jnp.cos(ang), jnp.cos(ang)], axis=-1)
    sin = jnp.concatenate([jnp.sin(ang), jnp.sin(ang)], axis=-1)
    half = RET_DK // 2
    rot = jnp.concatenate([-x[..., half:], x[..., :half]], axis=-1)
    return x * cos + rot * sin

def _retention_chunkwise(q, k, v, log_gamma, state0):
    B, H, L, dk = q.shape
    dv = v.shape[-1]
    C = RET_CHUNK
    n = L // C
    lg = log_gamma.astype(F32)
    pos = jnp.arange(C, dtype=F32)
    diff = pos[:, None] - pos[None, :]
    decay_mask = jnp.where(diff[None] >= 0, jnp.exp(jnp.maximum(diff, 0.0)[None] * lg[:, None, None]), 0.0)
    xi = jnp.exp((pos[None, :] + 1.0) * lg[:, None])
    zeta = jnp.exp((C - 1.0 - pos[None, :]) * lg[:, None])
    chunk_decay = jnp.exp(C * lg)
    qc = q.reshape(B, H, n, C, dk)
    kc = k.reshape(B, H, n, C, dk)
    vc = v.reshape(B, H, n, C, dv)
    scores = jnp.einsum('bhcnd,bhcmd->bhcnm', qc, kc) * decay_mask[None, :, None]
    intra = jnp.einsum('bhcnm,bhcme->bhcne', scores, vc)
    kz = kc * zeta[None, :, None, :, None]

    def step(S, xs):
        q_i, kz_i, v_i = xs
        cross = jnp.einsum('bhnd,bhde->bhne', q_i, S) * xi[None, :, :, None]
        S = S * chunk_decay[None, :, None, None] + jnp.einsum('bhmd,bhme->bhde', kz_i, v_i)
        return S, cross

    xs = (jnp.moveaxis(qc, 2, 0), jnp.moveaxis(kz, 2, 0), jnp.moveaxis(vc, 2, 0))
    S_final, cross = lax.scan(step, state0.astype(F32), xs)
    out = (intra + jnp.moveaxis(cross, 0, 2)).reshape(B, H, L, dv)
    return out, S_final

def _retention_mixer(q, k, v, g, decay_f, decay_b, s0_f, s0_b, norm_g, latent):
    B, L, _ = q.shape

    def heads(t):
        return t.reshape(B, L, N_RET_HEADS, -1).transpose(0, 2, 1, 3).astype(F32)

    qh, kh, vh = heads(q), heads(k), heads(v)
    if latent:
        qh = _axial_rope(qh)
        kh = _axial_rope(kh)
    kh = kh * (RET_DK ** -0.5)
    lg_f = -jnp.exp(decay_f.astype(F32))
    lg_b = -jnp.exp(decay_b.astype(F32))
    o_f, S_f = _retention_chunkwise(qh, kh, vh, lg_f, s0_f)
    o_b, S_b = _retention_chunkwise(qh[:, :, ::-1], kh[:, :, ::-1], vh[:, :, ::-1], lg_b, s0_b)
    o = (o_f + o_b[:, :, ::-1]).transpose(0, 2, 1, 3)
    o = _rmsnorm(o, norm_g.reshape(N_RET_HEADS, RET_DV)).reshape(B, L, D_RET).astype(q.dtype)
    o = o * jax.nn.silu(g)
    return o, S_f.astype(q.dtype), S_b.astype(q.dtype)

def _peer(h, w_q, sub_keys, u_tab, v_tab):
    B, L, D = h.shape
    T = B * L
    hf = h.reshape(T, D)
    q = (hf @ w_q).reshape(T, PEER_HEADS, 2, PEER_DQ // 2).astype(F32)
    s = jnp.einsum('thpd,hpkd->thpk', q, sub_keys.astype(F32))
    v1, i1 = lax.top_k(s[:, :, 0], PEER_TOPK)
    v2, i2 = lax.top_k(s[:, :, 1], PEER_TOPK)
    cand = (v1[..., :, None] + v2[..., None, :]).reshape(T, PEER_HEADS, PEER_TOPK * PEER_TOPK)
    cidx = (i1[..., :, None] * N_KEYS + i2[..., None, :]).reshape(T, PEER_HEADS, PEER_TOPK * PEER_TOPK)
    top_s, pos = lax.top_k(cand, PEER_TOPK)
    idx = jnp.take_along_axis(cidx, pos, axis=-1).reshape(T, PEER_HEADS * PEER_TOPK)
    gates = jax.nn.softmax(top_s, axis=-1).reshape(T, PEER_HEADS * PEER_TOPK).astype(h.dtype)
    nb = T // PEER_BLOCK

    def block(args):
        xb, ib, gb = args
        u = jnp.take(u_tab, ib, axis=0)
        a = jax.nn.gelu(jnp.einsum('td,tkd->tk', xb, u))
        ve = jnp.take(v_tab, ib, axis=0)
        return jnp.einsum('tk,tkd->td', gb * a, ve)

    out = lax.map(block, (hf.reshape(nb, PEER_BLOCK, D), idx.reshape(nb, PEER_BLOCK, -1), gates.reshape(nb, PEER_BLOCK, -1)))
    return out.reshape(B, L, D)

def _trunk_layer(x, cond, s0_f, s0_b, latent, w_ada, b_ada, norm1_g, w_in, hy_conv_w, hy_conv_b,
                 hy_w1, hy_b1, hy_w2, hy_b2, hy_w3, hy_b3, hy_w4, hy_freq, hy_bias, hy_norm_g,
                 ret_decay_fwd, ret_decay_bwd, ret_norm_g, w_out, norm2_g, peer_wq, peer_keys, peer_u, peer_v):
    mod = jax.nn.silu(cond) @ w_ada + b_ada
    sh1, sc1, gt1, sh2, sc2, gt2 = jnp.split(mod, N_MOD, axis=-1)
    h = _modulate(_rmsnorm(x, norm1_g), sh1, sc1)
    p = h @ w_in
    hy_in = p[..., :3 * D_HY]
    rq, rk, rv, rg = jnp.split(p[..., 3 * D_HY:], 4, axis=-1)
    y_hy = _hyena_mixer(hy_in, hy_conv_w, hy_conv_b, hy_w1, hy_b1, hy_w2, hy_b2, hy_w3, hy_b3, hy_w4, hy_freq, hy_bias)
    y_ret, S_f, S_b = _retention_mixer(rq, rk, rv, rg, ret_decay_fwd, ret_decay_bwd, s0_f, s0_b, ret_norm_g, latent)
    y = jnp.concatenate([_rmsnorm(y_hy, hy_norm_g), y_ret], axis=-1) @ w_out
    x = x + gt1[:, None, :] * y
    h2 = _modulate(_rmsnorm(x, norm2_g), sh2, sc2)
    x = x + gt2[:, None, :] * _peer(h2, peer_wq, peer_keys, peer_u, peer_v)
    return x, S_f, S_b

def setup_inputs(seed: int = 0) -> dict:
    key = jax.random.key(seed)
    ks = iter(jax.random.split(key, 48))

    def nrm(shape, scale):
        return jax.random.normal(next(ks), shape, F32) * scale

    heads = jnp.arange(N_RET_HEADS, dtype=F32)
    decay0 = jnp.log(-jnp.log(1.0 - 2.0 ** (-5.0 - heads)))
    st = (DEC_BATCH, DEPTH, N_RET_HEADS, RET_DK, RET_DV)
    return {
        'x_prompt': nrm((BATCH, SEQ, D_MODEL), 1.0),
        'x_sample': nrm((DEC_BATCH, DEC_SEQ, D_MODEL), 1.0),
        'state_ret_fwd': nrm(st, 1.0),
        'state_ret_bwd': nrm(st, 1.0),
        'c': nrm((DEC_BATCH, D_MODEL), 1.0),
        'c_ctx': nrm((D_MODEL,), 1.0),
        'w_ada': nrm((DEPTH, D_MODEL, N_MOD * D_MODEL), D_MODEL ** -0.5),
        'b_ada': nrm((DEPTH, N_MOD * D_MODEL), 0.01),
        'norm1_g': 1.0 + nrm((DEPTH, D_MODEL), 0.01),
        'w_in': nrm((DEPTH, D_MODEL, D_IN), D_MODEL ** -0.5),
        'hy_conv_w': nrm((DEPTH, HY_SHORT, 3 * D_HY), HY_SHORT ** -0.5),
        'hy_conv_b': nrm((DEPTH, 3 * D_HY), 0.01),
        'hy_w1': nrm((DEPTH, HY_EMB, HY_FILT_W), HY_EMB ** -0.5),
        'hy_b1': nrm((DEPTH, HY_FILT_W), 0.01),
        'hy_w2': nrm((DEPTH, HY_FILT_W, HY_FILT_W), HY_FILT_W ** -0.5),
        'hy_b2': nrm((DEPTH, HY_FILT_W), 0.01),
        'hy_w3': nrm((DEPTH, HY_FILT_W, HY_FILT_W), HY_FILT_W ** -0.5),
        'hy_b3': nrm((DEPTH, HY_FILT_W), 0.01),
        'hy_w4': nrm((DEPTH, HY_FILT_W, 2 * HY_ORDER * D_HY), 0.1 * HY_FILT_W ** -0.5),
        'hy_freq': 1.0 + nrm((DEPTH, HY_FILT_W), 0.01),
        'hy_bias': nrm((DEPTH, HY_ORDER, D_HY), 0.1),
        'hy_norm_g': 1.0 + nrm((DEPTH, D_HY), 0.01),
        'ret_decay_fwd': decay0[None, :] + nrm((DEPTH, N_RET_HEADS), 0.01),
        'ret_decay_bwd': decay0[None, :] + nrm((DEPTH, N_RET_HEADS), 0.01),
        'ret_norm_g': 1.0 + nrm((DEPTH, D_RET), 0.01),
        'w_out': nrm((DEPTH, D_MIX, D_MODEL), D_MIX ** -0.5),
        'norm2_g': 1.0 + nrm((DEPTH, D_MODEL), 0.01),
        'peer_wq': nrm((DEPTH, D_MODEL, PEER_HEADS * PEER_DQ), D_MODEL ** -0.5),
        'peer_keys': nrm((DEPTH, PEER_HEADS, 2, N_KEYS, PEER_DQ // 2), (PEER_DQ // 2) ** -0.5),
        'peer_u': nrm((DEPTH, N_EXPERTS, D_MODEL), D_MODEL ** -0.5),
        'peer_v': nrm((DEPTH, N_EXPERTS, D_MODEL), 0.5),
        'final_g': 1.0 + nrm((D_MODEL,), 0.01),
    }

def reference(x_prompt, x_sample, state_ret_fwd, state_ret_bwd, c, c_ctx, w_ada, b_ada, norm1_g, w_in,
              hy_conv_w, hy_conv_b, hy_w1, hy_b1, hy_w2, hy_b2, hy_w3, hy_b3, hy_w4, hy_freq, hy_bias,
              hy_norm_g, ret_decay_fwd, ret_decay_bwd, ret_norm_g, w_out, norm2_g, peer_wq, peer_keys,
              peer_u, peer_v, final_g):
    B_ctx = x_prompt.shape[0]
    x_ctx = x_prompt
    x_lat = x_sample
    cond_ctx = c_ctx[None, :]
    zero_state = jnp.zeros((B_ctx, N_RET_HEADS, RET_DK, RET_DV), x_prompt.dtype)
    new_f, new_b = [], []
    for l in range(DEPTH):
        lw = (w_ada[l], b_ada[l], norm1_g[l], w_in[l], hy_conv_w[l], hy_conv_b[l], hy_w1[l], hy_b1[l],
              hy_w2[l], hy_b2[l], hy_w3[l], hy_b3[l], hy_w4[l], hy_freq[l], hy_bias[l], hy_norm_g[l],
              ret_decay_fwd[l], ret_decay_bwd[l], ret_norm_g[l], w_out[l], norm2_g[l], peer_wq[l],
              peer_keys[l], peer_u[l], peer_v[l])
        x_ctx, S_f, S_b = _trunk_layer(x_ctx, cond_ctx, zero_state, zero_state, False, *lw)
        new_f.append(S_f)
        new_b.append(S_b)
        x_lat, _, _ = _trunk_layer(x_lat, c, state_ret_fwd[:, l], state_ret_bwd[:, l], True, *lw)
    y_prompt = _rmsnorm(x_ctx, final_g)
    y_sample = _rmsnorm(x_lat, final_g)
    new_state_ret_fwd = jnp.stack(new_f, axis=1)
    new_state_ret_bwd = jnp.stack(new_b, axis=1)
    return (y_prompt, y_sample, new_state_ret_fwd, new_state_ret_bwd)


_drawn_inputs = setup_inputs


def setup_inputs(seed=0):
    import zlib

    import numpy as np

    out = dict(_drawn_inputs(seed))
    spreads = {}
    factors = {'norm1_g': 8.733,
     'hy_conv_b': 96.095,
     'hy_freq': 2.965,
     'hy_norm_g': 200.0,
     'ret_norm_g': 128.978,
     'norm2_g': 128.915,
     'final_g': 200.0,
     'hy_b3': 3.35,
     'state_ret_fwd': 8.0,
     'state_ret_bwd': 8.0}
    for name, (base, spread) in spreads.items():
        noise = np.random.default_rng([zlib.crc32(name.encode()), seed]).standard_normal(out[name].shape)
        drawn = base * np.exp(spread * noise) if base else spread * noise
        out[name] = __import__('jax').numpy.asarray(drawn.astype(out[name].dtype))
    for name, factor in factors.items():
        out[name] = (out[name] * factor).astype(out[name].dtype)
    return out
```

```python
from contextlib import ExitStack
import math

import numpy as np
import concourse.bass as bass
from concourse import mybir

F32 = mybir.dt.float32
U32 = mybir.dt.uint32
ALU = mybir.AluOpType
ACT = mybir.ActivationFunctionType
AX = mybir.AxisListType

P = 128
D = 1024
KD = D // P
NLAT = 512
NB = 5
NT = NB * P
HY = 512
NH = 4
GRID_W = 64
PH = 8
TOPK = 16
NKEYS = 128
NEXP = NKEYS * NKEYS
EPS = 1e-6
NADA = 12
NWSLOT = 3
USLOTS = 8
VSLOTS = 8
DSLOTS = 4
MAGIC = 12582912.0
TWO_PI_PARTS = (6.28125, 0.0019350051879882812, 3.0199159819e-07)
PI_SAFE = 3.1415925
FLOAT_LOW = -3.0e38


def shape_constants():
    f8 = np.float64
    out = {}
    out["ident"] = np.eye(P)
    for name, L in (("lat", NLAT), ("ctx", P)):
        t = np.arange(L, dtype=f8)
        ang = 2.0 * np.pi * ((t[:, None] * t[None, :]) % (2 * L)) / (2 * L)
        c, s = np.cos(ang), np.sin(ang)
        s[:, 0] = (-1.0) ** t
        nt = L // P
        out["dft_" + name] = np.concatenate([
            m.reshape(nt, P, L).transpose(1, 0, 2).reshape(P, nt * L) for m in (c, s, s.T)], axis=1)
    feats, wins = [], []
    for L in (P, NLAT):
        t = np.linspace(0.0, 1.0, L, dtype=np.float32)[:, None]
        w = (np.float32(2.0 * math.pi) * np.arange(L, dtype=np.float32)[:, None] / np.float32(L)).astype(np.float32)
        f = np.linspace(1e-4, 15, 16, dtype=np.float32)[None, :]
        fw = (f * w).astype(np.float32)
        feats.append(np.concatenate([t, np.cos(fw), -np.sin(fw)], axis=-1))
        lo, hi = math.log(1e-2) / 1.5, math.log(1e-2) / 0.3
        deltas = np.abs(np.linspace(lo, hi, HY, dtype=np.float32))
        wins.append(np.exp(-t * deltas[None, :]))
    out["feat_t"] = np.concatenate(feats, axis=0).T
    win = np.concatenate(wins, axis=0).reshape(NB, P, HY)
    out["window"] = win.transpose(1, 0, 2).reshape(P, NB * HY)
    t = np.arange(NLAT)
    inv = (10000.0 ** (-np.arange(32, dtype=np.float32) / np.float32(32))).astype(np.float32)
    ang = np.concatenate([(t // GRID_W).astype(np.float32)[:, None] * inv,
                          (t % GRID_W).astype(np.float32)[:, None] * inv], axis=1)
    rope = np.stack([np.cos(ang), np.sin(ang)], axis=1).reshape(4, P, 2, 64)
    out["rope"] = rope.transpose(1, 2, 0, 3).reshape(P, 2 * 4 * 64)
    m, n = np.arange(P)[:, None], np.arange(P)[None, :]
    out["dist"] = np.concatenate([np.maximum(n - m, 0), np.maximum(m - n, 0), n >= m, m >= n], axis=1)
    cols = np.zeros((P, 8))
    i = np.arange(P)
    cols[:, 0], cols[:, 1], cols[:, 2], cols[:, 3] = i + 1, 127 - i, 128 - i, i
    for j, L in ((4, P), (6, NLAT)):
        cols[:, j] = np.where(i == 0, 1.0 / (2 * L), 2.0 / (2 * L))
        cols[:, j + 1] = np.where(i == 0, 0.0, 2.0 / (2 * L))
    out["cols"] = cols
    out["iota16"] = np.tile(np.arange(TOPK)[None, :], (P, 1))
    return {k: np.ascontiguousarray(v.astype(np.float32)) for k, v in out.items()}


def build_trunk_layer(nc, io):
    ctx = ExitStack()
    with ctx:
        def sb(name, shape, dt=F32):
            return ctx.enter_context(nc.sbuf_tensor(name, shape, dt))

        def sem(name):
            return ctx.enter_context(nc.semaphore(name))

        bank = [ctx.enter_context(nc.psum_tensor(f"bank{i}", [P, 512], F32)) for i in range(8)]

        X = sb("X", [P, NB, D])
        HA = sb("HA", [P, NB * D])
        W = sb("W", [P, NWSLOT * KD * 512])
        DA = sb("DA", [P, 6 * D])
        RA = sb("RA", [P, 15 * D])
        TA = sb("TA", [P, 6 * D])

        ident = sb("ident", [P, P])
        cols = sb("cols", [P, 8])
        iota16 = sb("iota16", [P, TOPK])
        rope = sb("rope", [P, 2, 4, 64])
        mask = sb("mask", [P, NH, P])
        hid = sb("hid", [64, NT])
        hidp = sb("peer_small", [P, 96])
        sml = sb("sml", [P, 256])

        wslot = [W[:, i * KD * 512:(i + 1) * KD * 512].rearrange("p (k n) -> p k n", k=KD) for i in range(NWSLOT)]

        def seg(area, lo, n, pat=None, **kw):
            v = area[:, lo:lo + n]
            return v.rearrange(pat, **kw) if pat else v

        silu_c = sml[:, 0:16]
        convc = sml[:, 16:64]
        bfcol = sml[0:64, 64:68]
        decay = sml[:, 68:76]
        lg = sml[:, 76:84]
        xi = sml[:, 84:92]
        zeta = sml[:, 92:100]
        chunkdec = sml[:, 100:108]
        ss1, var1, sd1, rs1 = (sml[:, 108 + 5 * i:113 + 5 * i] for i in range(4))
        sso, varo, sdo, rso = (sml[:, 128 + 4 * i:132 + 4 * i] for i in range(4))
        ssy, vary, sdy, rsy = (sml[:, 144 + 5 * i:149 + 5 * i] for i in range(4))
        ss2, var2, sd2, rs2 = (sml[:, 164 + 5 * i:169 + 5 * i] for i in range(4))
        ssf, varf, sdf, rsf = (sml[:, 184 + 5 * i:189 + 5 * i] for i in range(4))

        feat = TA[0:33, 0:NT]
        arg = TA[0:64, NT:2 * NT]
        turns = TA[0:64, 2 * NT:3 * NT]
        ef = seg(TA, 2048, 512, "p (h n) -> p h n", h=NH)
        eb = seg(TA, 2560, 512, "p (h n) -> p h n", h=NH)
        dist = seg(TA, 4096, 512, "p (a n) -> p a n", a=4)
        wf1 = TA[0:33, 4608:4672]
        wf2 = TA[0:64, 4672:4736]
        wf3 = TA[0:64, 4736:4800]
        condrows = TA[0:16, 4800:4928]
        convrows = TA[0:48, 4928:5056]
        modrow = RA[0:2, 0:6 * D]
        bada = RA[0:2, 6 * D:12 * D]
        grow = RA[0:2, 12 * D:14 * D]
        mod1 = [(seg(DA, 2 * c * D, D), seg(DA, (2 * c + 1) * D, D)) for c in range(2)]
        hbuf = [seg(TA, 0, D), seg(TA, D, D)]
        ropt1 = seg(TA, 2048, 512, "p (h a c) -> p h a c", h=NH, a=2)
        ropt2 = seg(TA, 2560, 512, "p (h a c) -> p h a c", h=NH, a=2)
        junk1 = seg(TA, 3072, D)
        hT = seg(HA, 0, NB * D, "p (k t) -> p k t", k=KD)
        qT = seg(RA, 0, 2560, "p (h t) -> p h t", h=NH)
        kT = seg(RA, 2560, 2560, "p (h t) -> p h t", h=NH)
        kt = seg(RA, 5120, 2560, "p (b n) -> p b n", b=NB)
        vt = seg(RA, 7680, 2560, "p (b n) -> p b n", b=NB)
        gg = seg(RA, 10240, 2560, "p (b n) -> p b n", b=NB)
        qt = seg(RA, 12800, 2560, "p (b n) -> p b n", b=NB)
        yret = qt
        retg = seg(TA, 4096, 512)
        Sf = [seg(TA, i * 512, 512) for i in range(4)]
        Sb = [seg(TA, (4 + i) * 512, 512) for i in range(4)]
        kz = [seg(TA, 4096, 512), seg(TA, 4608, 512)]
        stout = seg(TA, 5120, 1024, "p (a n) -> p a n", a=2)
        sm = [seg(DA, 0, 512), seg(DA, 512, 512)]
        ob = [seg(DA, 1024, 512), seg(DA, 1536, 512)]
        junko = seg(DA, 2048, 512)
        uT = [seg(TA, i * NT, NT) for i in range(3)]
        U = seg(RA, 0, 7680, "p (b j n) -> p b j n", b=NB, j=3)
        XF = X[:, :, :].rearrange("p b d -> p (b d)")
        window = seg(XF, 0, NB * HY, "p (b n) -> p b n", b=NB)
        w4 = XF[0:64, NB * HY:NB * HY + 4 * HY]
        dftc = seg(XF, 4608, 3 * P, "p (m t n) -> p m t n", m=3, t=1)
        dftl = seg(DA, 0, 6 * D, "p (m t n) -> p m t n", m=3, t=4)
        Ps = [seg(TA, 0, 512), seg(TA, 512, 512)]
        Qs = [seg(TA, 1024, 512), seg(TA, 1536, 512)]
        Pn = seg(TA, 2048, 512)
        tt4 = [seg(TA, 2560 + 512 * i, 512) for i in range(4)]
        fbias = TA[0:1, 4608:4608 + 2 * HY]
        he = seg(RA, 7680, 2048, "p (t n) -> p t n", t=4)
        ho = seg(RA, 9728, 2048, "p (t n) -> p t n", t=4)
        Rr = seg(HA, 0, 2048, "p (t n) -> p t n", t=4)
        Ri = seg(HA, 2048, 2048, "p (t n) -> p t n", t=4)
        mod2 = [(seg(DA, 3 * c * D, D), seg(DA, (3 * c + 1) * D, D), seg(DA, (3 * c + 2) * D, D)) for c in range(2)]
        yT = [seg(TA, i * D, D, "p (k t) -> p k t", k=KD) for i in range(2)]
        junk2 = seg(TA, 2048, D)
        hyg = seg(TA, 3072, 512)
        gy = [seg(TA, 3584, 512), seg(TA, 4096, 512)]
        H2 = seg(HA, 0, NB * D, "p (b d) -> p b d", b=NB)
        h2T = seg(RA, 7680, 5120, "p (k t) -> p k t", k=KD)
        keyraw = seg(DA, 0, 2048, "p (i d) -> p i d", i=16)
        keysT = seg(RA, 0, 2048, "p (i n) -> p i n", i=16)
        qTb = [seg(TA, i * NT, NT) for i in range(2)]
        sc = [seg(TA, 1280 + i * 1280, 1280, "p (b a n) -> p b a n", b=NB, a=2) for i in range(2)]
        topv = seg(TA, 3840, 160, "p (b a k) -> p b a k", b=NB, a=2)
        topi = seg(TA, 4000, 160, "p (b a k) -> p b a k", b=NB, a=2).bitcast(U32)
        topif = seg(TA, 4160, 160, "p (b a k) -> p b a k", b=NB, a=2)
        pairv = seg(TA, 4320, 80, "p (b k) -> p b k", b=NB)
        pairp = seg(TA, 4400, 80).bitcast(U32)
        posa = seg(TA, 4480, 80).bitcast(U32)
        posb = seg(TA, 4560, 80).bitcast(U32)
        posaf = seg(TA, 4640, 80)
        posbf = seg(TA, 4720, 80)
        sel1 = seg(TA, 4800, 80)
        sel2 = seg(TA, 4880, 80)
        gsum = seg(TA, 4960, 40)
        grec = seg(TA, 5000, 40)
        cand = seg(DA, 3072, 1280, "p (b i j) -> p b i j", b=NB, i=16)
        onehot = seg(DA, 4352, 1280)
        IDX = seg(RA, 12800, 640, "p (b h k) -> p b h k", b=NB, h=PH).bitcast(U32)
        GATE = seg(RA, 13440, 640, "p (b h k) -> p b h k", b=NB, h=PH)
        uslot = [seg(W, i * D, D) for i in range(USLOTS)]
        vslot = [seg(RA, i * D, D) for i in range(VSLOTS)]
        moe = seg(TA, 0, NB * D, "p (b d) -> p b d", b=NB)
        h2cur = seg(TA, 5120, D)
        gt2 = [seg(DA, 0, D), seg(DA, D, D)]
        fing = seg(DA, 2 * D, D)
        junku = [seg(DA, 3 * D, D), seg(DA, 5 * D, D)]
        diag = [seg(DA, 4096 + i * P, P) for i in range(DSLOTS)]
        zero = seg(DA, 4608, 512)
        dots = [seg(sml, 210, TOPK), seg(sml, 226, TOPK)]
        gelu = [seg(hidp, 16 * i, TOPK) for i in range(2)]
        wgt = [seg(hidp, 32 + 16 * i, TOPK) for i in range(2)]
        idxc = [seg(hidp, 64 + 16 * i, TOPK).bitcast(U32) for i in range(2)]

        T_COND, T_CONV, T_MLP = 0, 1, 2
        T_MOD = T_MLP + 6
        T_HT = T_MOD + NADA
        T_QKVG = T_HT + 2 * NB
        T_QK = T_QKVG + 4 * NB
        T_KV = T_QK + 2 * NB
        KV = [(0, 0), (0, 1), (1, 0), (2, 0), (3, 0), (4, 1), (3, 1), (2, 1)]
        T_RET = T_KV + len(KV)

        def t_score(b):
            return T_RET + (0 if b == 0 else 2 + 4 * (b - 1))

        def t_cross(b, d):
            return t_score(b) + 1 + d

        def t_intra(b):
            return t_score(b) + (1 if b == 0 else 3)

        T_HY = T_RET + 2 + 4 * 4

        def t_proj(i, part):
            return T_HY + (0 if i == 0 else 4 * i - 2) + part

        def t_uback(i, part):
            return T_HY + (4 * i + 4 if i < 11 else 46) + part

        T_CONVL = T_HY + 48
        SEGS = [(0, 1), (1, 4)]

        def conv_base(s, o):
            return T_CONVL + (o * 8 if s == 0 else 16 + o * 29)

        def t_filt(s, o, t, d):
            return conv_base(s, o) + 2 * t + d

        def t_freq(s, o, f, j):
            return conv_base(s, o) + 2 * SEGS[s][1] + (j if f == 0 else 1 + 4 * f + j)

        def t_inv(s, o, t):
            return conv_base(s, o) + 6 * SEGS[s][1] + 1 + t

        T_OUT = T_CONVL + 74

        def t_yT(b, j):
            return T_OUT + (0 if b == 0 else 6 * b - 2) + j

        def t_y(b, j):
            return t_yT(b, 0) + 2 + j

        def t_h2T(b, j):
            return T_OUT + 6 * (b + 1) - 2 + (4 if b < 4 else 0) + j

        T_KEYS = T_OUT + 30
        T_WQ = T_KEYS + 4

        def t_q(i, part):
            return T_WQ + (0 if i == 0 else 4 * i - 2) + part

        def t_s(i, part):
            return T_WQ + (4 * i + 4 if i < 15 else 62) + part

        T_PEER = T_WQ + 64

        bank_filled = [sem(f"bank_filled{i}") for i in range(8)]
        bank_freed = [sem(f"bank_freed{i}") for i in range(8)]

        def free_bank(pe, t):
            if t >= 8:
                pe.wait_ge(bank_freed[t % 8], t // 8)
            return bank[t % 8]

        def filled(eng, t):
            eng.wait_ge(bank_filled[t % 8], t // 8 + 1)
            return bank[t % 8]

        def readout(eng, t):
            eng.wait_ge(bank_freed[t % 8], t // 8 + 1)

        names = """c_loaded conv_loaded mlp_loaded const_loaded decay_loaded ada_bias_loaded x_loaded x_again
            arg_ready sin_done lg_ready decays_ready masks_ready mod_ready mod_stored mod1_loaded retg_loaded
            ss1_ready var1_ready sd1_ready h_ready rope_ready gate_ready state_loaded kz_ready state_ready
            stout_ready o_ready sso_ready varo_ready sdo_ready yret_ready conv_center dft_loaded filt_loaded
            bias_loaded filt_ready ps_scaled spectrum_ready z_ready mod2_loaded hyg_loaded ssy_ready vary_ready sdy_ready
            yhy_ready x1_ready ss2_ready var2_ready sd2_ready h2_ready keys_loaded scores_out topk_done pair_ready exp_done
            gates_ready mod3_loaded weights_used idx_ready gelu_ready wgt_ready diag_ready acc_filled acc_free
            vrow_used urow_used pool_go zero_ready ssf_ready varf_ready sdf_ready y_ready stored states_stored dve_chain act_chain
            norm2_started""".split()
        s = {n: sem(n) for n in names}
        w_full = [sem(f"w_full{i}") for i in range(NWSLOT)]
        urow_full = [sem(f"urow_full{i}") for i in range(USLOTS)]
        vrow_full = [sem(f"vrow_full{i}") for i in range(VSLOTS)]

        wtiles = [(io["w_ada"], n * 512) for n in range(NADA)]
        W_QKVG = len(wtiles)
        wtiles += [(io["w_in"], 3 * HY + n * 512) for n in range(4)]
        W_HY = len(wtiles)
        wtiles += [(io["w_in"], n * 512) for n in range(3)]
        W_OUT = len(wtiles)
        wtiles += [(io["w_out"], n * 512) for n in range(2)]
        W_Q = len(wtiles)
        wtiles += [(io["peer_wq"], n * 512) for n in range(4)]

        def weight(pe, n):
            pe.wait_ge(w_full[n % NWSLOT], 16 * (n // NWSLOT + 1))
            return wslot[n % NWSLOT]

        block = ctx.enter_context(nc.Block())

        @block.sync
        def _(sp):
            sp.dma_start(condrows, io["conds"]).then_inc(s["c_loaded"], 16)
            sp.dma_start(ident[:, :], io["ident"]).then_inc(s["c_loaded"], 16)
            for i in range(NWSLOT):
                src, lo = wtiles[i]
                sp.dma_start(wslot[i], src[:, lo:lo + 512].rearrange("(k p) n -> p k n", p=P)).then_inc(w_full[i], 16)
            for n in range(NWSLOT, len(wtiles)):
                src, lo = wtiles[n]
                sp.wait_ge(s["weights_used"], n - NWSLOT + 1)
                sp.dma_start(wslot[n % NWSLOT], src[:, lo:lo + 512].rearrange("(k p) n -> p k n", p=P)).then_inc(
                    w_full[n % NWSLOT], 16)
            for b in range(NB):
                sp.wait_ge(s["y_ready"], b + 1)
                dst = io["y_prompt"] if b == 0 else io["y_sample"][(b - 1) * P:b * P, :]
                sp.dma_start(dst, moe[:, b, :]).then_inc(s["stored"], 16)
            sp.wait_ge(s["stored"], 16 * NB)

        @block.gpsimd
        def _(g):
            g.dma_start(convrows, io["conv_rows"]).then_inc(s["conv_loaded"], 16)
            for dst, name in ((feat, "feat_t"), (wf1, "hy_w1"), (wf2, "hy_w2"), (wf3, "hy_w3")):
                g.dma_start(dst, io[name]).then_inc(s["mlp_loaded"], 16)
            for j, name in enumerate(("hy_b1", "hy_b2", "hy_b3", "hy_freq")):
                g.dma_start(bfcol[:, j:j + 1], io[name]).then_inc(s["mlp_loaded"], 16)
            g.dma_start(dist, io["dist"].rearrange("p (a n) -> p a n", a=4)).then_inc(s["decay_loaded"], 16)
            g.dma_start(cols[:, :], io["cols"]).then_inc(s["decay_loaded"], 16)
            g.dma_start(decay[:, 0:4], io["ret_decay_fwd"].to_broadcast([P, NH])).then_inc(s["decay_loaded"], 16)
            g.dma_start(decay[:, 4:8], io["ret_decay_bwd"].to_broadcast([P, NH])).then_inc(s["decay_loaded"], 16)
            g.dma_start(bada, io["b_ada"].to_broadcast([2, 6 * D])).then_inc(s["ada_bias_loaded"], 16)
            g.dma_start(grow[:, 0:D], io["norm1_g"].to_broadcast([2, D])).then_inc(s["ada_bias_loaded"], 16)
            g.dma_start(grow[:, D:2 * D], io["norm2_g"].to_broadcast([2, D])).then_inc(s["ada_bias_loaded"], 16)
            g.dma_start(X[:, 0, :], io["x_prompt"]).then_inc(s["x_loaded"], 16)
            g.dma_start(X[:, 1:NB, :], io["x_sample"].rearrange("(b p) d -> p b d", p=P)).then_inc(s["x_loaded"], 16)
            g.dma_start(rope[:, :, :, :], io["rope"].rearrange("p (a b c) -> p a b c", a=2, b=4)).then_inc(s["const_loaded"], 16)
            g.dma_start(iota16[:, :], io["iota16"]).then_inc(s["const_loaded"], 16)
            g.wait_ge(s["mod_ready"], 1)
            g.dma_start(io["mod_scratch"], modrow).then_inc(s["mod_stored"], 16)
            g.wait_ge(s["mod_stored"], 16)

            def spread(dst, c, j, done):
                g.dma_start(dst, io["mod_scratch"][c:c + 1, j * D:(j + 1) * D].to_broadcast([P, D])).then_inc(s[done], 16)

            for c in range(2):
                spread(mod1[c][0], c, 1, "mod1_loaded")
                spread(mod1[c][1], c, 0, "mod1_loaded")
            g.wait_ge(s["masks_ready"], 1)
            g.dma_start(retg, io["ret_norm_g"].to_broadcast([P, HY])).then_inc(s["retg_loaded"], 16)
            for b in range(NB):
                for j in range(2):
                    filled(g, T_HT + 2 * b + j)
            g.dma_start(Sf[0].rearrange("p (h e) -> p h e", h=NH), io["state_ret_fwd"]).then_inc(s["state_loaded"], 16)
            g.wait_ge(s["rope_ready"], 8)
            g.wait_ge(s["h_ready"], NB)
            g.dma_start(Sb[3].rearrange("p (h e) -> p h e", h=NH), io["state_ret_bwd"]).then_inc(s["state_loaded"], 16)
            g.dma_start(window, io["window"].rearrange("p (b n) -> p b n", b=NB)).then_inc(s["filt_loaded"], 16)
            g.dma_start(w4, io["hy_w4"]).then_inc(s["filt_loaded"], 16)
            g.dma_start(dftc, io["dft_ctx"].rearrange("p (m t n) -> p m t n", m=3, t=1)).then_inc(s["filt_loaded"], 16)
            g.wait_ge(s["stout_ready"], 2)
            for d, name in ((0, "new_fwd"), (1, "new_bwd")):
                g.dma_start(io[name], stout[:, d, :].rearrange("p (h e) -> p h e", h=NH)).then_inc(s["states_stored"], 16)
            g.wait_ge(s["yret_ready"], NB)
            g.dma_start(dftl, io["dft_lat"].rearrange("p (m t n) -> p m t n", m=3, t=4)).then_inc(s["dft_loaded"], 16)
            g.wait_ge(s["states_stored"], 32)
            g.dma_start(fbias, io["hy_bias"]).then_inc(s["bias_loaded"], 16)
            for t in range(4):
                filled(g, t_inv(1, 1, t))
            for c in range(2):
                for i, j in enumerate((2, 4, 3)):
                    spread(mod2[c][i], c, j, "mod2_loaded")
            g.wait_ge(s["z_ready"], 10)
            g.dma_start(hyg, io["hy_norm_g"].to_broadcast([P, HY])).then_inc(s["hyg_loaded"], 16)
            g.dma_start(X[:, 0, :], io["x_prompt"]).then_inc(s["x_again"], 16)
            g.dma_start(X[:, 1:NB, :], io["x_sample"].rearrange("(b p) d -> p b d", p=P)).then_inc(s["x_again"], 16)
            g.wait_ge(s["h2_ready"], 1)
            g.dma_start(keyraw, io["peer_keys"].rearrange("i n d -> n i d")).then_inc(s["keys_loaded"], 16)
            g.wait_ge(s["topk_done"], PH)
            spread(gt2[0], 0, 5, "mod3_loaded")
            spread(gt2[1], 1, 5, "mod3_loaded")
            g.dma_start(fing, io["final_g"].to_broadcast([P, D])).then_inc(s["mod3_loaded"], 16)

            g.wait_ge(s["weights_used"], len(wtiles))
            with g.Fori(0, NB) as b:
                with g.Fori(0, PH // 2) as hp:
                    for par in range(2):
                        chunk = b * PH + hp * 2 + par
                        g.wait_ge(s["idx_ready"], chunk + 1)
                        for k in range(TOPK):
                            g.wait_ge(s["urow_used"], chunk * TOPK + k + 1)
                            g.sem_inc(s["pool_go"], 1)
                            g.indirect_dma_start(out=uslot[k % USLOTS], out_offset=None, in_=io["peer_u"],
                                                 in_offset=bass.IndirectOffsetOnAxis(ap=idxc[par][:, k:k + 1], axis=0)
                                                 ).then_inc(urow_full[k % USLOTS], 16)
                        for k in range(TOPK):
                            g.wait_ge(s["vrow_used"], chunk * TOPK + TOPK + k + 1)
                            g.sem_inc(s["pool_go"], 1)
                            g.indirect_dma_start(out=vslot[k % VSLOTS], out_offset=None, in_=io["peer_v"],
                                                 in_offset=bass.IndirectOffsetOnAxis(ap=idxc[par][:, k:k + 1], axis=0)
                                                 ).then_inc(vrow_full[k % VSLOTS], 16)

        @block.scalar
        def _(act):
            A = nc.scalar

            def copy_out(t, out, src):
                A.copy(out, src).then_inc(bank_freed[t % 8], 1)

            chain = [0]

            def link(ins):
                chain[0] += 1
                ins.then_inc(s["act_chain"], 1)
                act.wait_ge(s["act_chain"], chain[0])

            ps = filled(act, T_COND)
            A.activation(silu_c, ps[:, 0:16], ACT.Silu).then_inc(bank_freed[T_COND % 8], 1)
            ps = filled(act, T_CONV)
            copy_out(T_CONV, convc, ps[:, 0:48])
            for layer in range(3):
                for i, (lo, n) in enumerate(((0, P), (P, NLAT))):
                    act.wait_ge(s["arg_ready"], 2 * layer + i + 1)
                    A.activation(hid[:, lo:lo + n], arg[:, lo:lo + n], ACT.Sin).then_inc(s["sin_done"], 1)
            act.wait_ge(s["decay_loaded"], 64)
            link(A.activation(decay, decay, ACT.Exp))
            act.wait_ge(s["lg_ready"], 1)
            for h in range(NH):
                A.activation(ef[:, h, :], dist[:, 0, :], ACT.Exp, scale=lg[:, h:h + 1])
                A.activation(eb[:, h, :], dist[:, 1, :], ACT.Exp, scale=lg[:, 4 + h:5 + h])
            A.activation(xi[:, 0:4], lg[:, 0:4], ACT.Exp, scale=cols[:, 0:1])
            A.activation(zeta[:, 0:4], lg[:, 0:4], ACT.Exp, scale=cols[:, 1:2])
            A.activation(xi[:, 4:8], lg[:, 4:8], ACT.Exp, scale=cols[:, 2:3])
            A.activation(zeta[:, 4:8], lg[:, 4:8], ACT.Exp, scale=cols[:, 3:4])
            A.activation(chunkdec, lg, ACT.Exp, scale=float(P)).then_inc(s["decays_ready"], 1)
            act.wait_ge(s["x_loaded"], 32)
            for b in range(NB):
                link(A.activation(junk1, X[:, b, :], ACT.Square, accum_out=ss1[:, b:b + 1]))
            act.sem_inc(s["ss1_ready"], 1)
            act.wait_ge(s["var1_ready"], 1)
            A.activation(sd1, var1, ACT.Sqrt).then_inc(s["sd1_ready"], 1)
            for b in range(NB):
                for j in range(2):
                    t = T_HT + 2 * b + j
                    ps = filled(act, t)
                    copy_out(t, hT[:, 4 * j:4 * j + 4, b * P:(b + 1) * P], ps[:, :].rearrange("p (k t) -> p k t", k=4))
            t = T_QKVG
            copy_out(t, qt[:, 0, :], filled(act, t)[:, :])
            t = T_QKVG + NB
            copy_out(t, kt[:, 0, :], filled(act, t)[:, :])
            for b in range(NB):
                t = T_QKVG + 2 * NB + b
                copy_out(t, vt[:, b, :], filled(act, t)[:, :])
            for b in range(NB):
                t = T_QKVG + 3 * NB + b
                ps = filled(act, t)
                A.activation(gg[:, b, :], ps[:, :], ACT.Silu).then_inc(bank_freed[t % 8], 1)
            for j, dst in enumerate((qT, kT)):
                for b in range(NB):
                    t = T_QK + j * NB + b
                    ps = filled(act, t)
                    copy_out(t, dst[:, :, b * P:(b + 1) * P], ps[:, :].rearrange("p (h t) -> p h t", h=NH))
            for b in range(NB):
                if b >= 2:
                    act.wait_ge(s["yret_ready"], b - 1)
                copy_out(t_intra(b), ob[b % 2], filled(act, t_intra(b))[:, :])
                act.wait_ge(s["o_ready"], b + 1)
                for h in range(NH):
                    ins = A.activation(junko[:, h * P:(h + 1) * P], ob[b % 2][:, h * P:(h + 1) * P], ACT.Square,
                                       accum_out=sso[:, h:h + 1])
                ins.then_inc(s["sso_ready"], 1)
                act.wait_ge(s["varo_ready"], b + 1)
                A.activation(sdo, varo, ACT.Sqrt).then_inc(s["sdo_ready"], 1)
            def rows_out(i):
                for part in range(2):
                    t = t_uback(i, part)
                    ps = filled(act, t)
                    j, c = i // 4, (i % 4) * P
                    if part == 0:
                        copy_out(t, U[:, 1:NB, j, c:c + P], ps[:, :].rearrange("p (b n) -> p b n", b=4))
                    else:
                        copy_out(t, U[:, 0, j, c:c + P], ps[:, 0:P])

            act.wait_ge(s["stout_ready"], 2)
            act.wait_ge(s["yret_ready"], NB)
            for i in range(12):
                if i >= 3:
                    filled(act, t_uback(i - 3, 1))
                for part, lo, n in ((0, P, NLAT), (1, 0, P)):
                    ps = filled(act, t_proj(i, part))
                    A.activation(uT[i % 3][:, lo:lo + n], ps[:, 0:n], ACT.Identity, bias=convc[:, 36 + i:37 + i],
                                 scale=convc[:, 12 + i:13 + i]).then_inc(s["conv_center"], 1)
                if i >= 1:
                    rows_out(i - 1)
            rows_out(11)
            n_freq = 0
            for sg, (b0, nt) in enumerate(SEGS):
                cp, cq = (cols[:, 4 + 2 * sg:5 + 2 * sg], cols[:, 5 + 2 * sg:6 + 2 * sg])
                wgt2 = 2.0 / (2 * nt * P)
                for o in range(2):
                    for f in range(nt):
                        if n_freq >= 2:
                            act.wait_ge(s["spectrum_ready"], n_freq - 1)
                        if f == 0 and n_freq >= 1:
                            act.wait_ge(s["spectrum_ready"], n_freq)
                        i = n_freq % 2
                        ps = filled(act, t_freq(sg, o, f, 0))
                        if f == 0:
                            link(A.activation(Pn, ps[:, :], ACT.Copy, scale=cp))
                        A.activation(Ps[i], ps[:, :], ACT.Copy, scale=cp if f == 0 else wgt2).then_inc(
                            bank_freed[t_freq(sg, o, f, 0) % 8], 1)
                        ps = filled(act, t_freq(sg, o, f, 1))
                        A.activation(Qs[i], ps[:, :], ACT.Copy, scale=cq if f == 0 else wgt2).then_inc(
                            bank_freed[t_freq(sg, o, f, 1) % 8], 1)
                        if f == 0:
                            t = t_freq(sg, o, 0, 4)
                            ps = filled(act, t)
                            A.activation(Pn[0:1, :], ps[0:1, :], ACT.Copy, scale=0.5 * wgt2).then_inc(bank_freed[t % 8], 1)
                        n_freq += 1
            act.wait_ge(s["z_ready"], 10)
            for b in range(NB):
                link(A.activation(junk2[:, 0:512], U[:, b, 0, :], ACT.Square, accum_out=ssy[:, b:b + 1]))
            act.sem_inc(s["ssy_ready"], 1)
            act.wait_ge(s["vary_ready"], 1)
            A.activation(sdy, vary, ACT.Sqrt).then_inc(s["sdy_ready"], 1)

            def h2T_out(b):
                for j in range(2):
                    t = t_h2T(b, j)
                    ps = filled(act, t)
                    copy_out(t, h2T[:, 4 * j:4 * j + 4, b * P:(b + 1) * P], ps[:, :].rearrange("p (k t) -> p k t", k=4))

            for b in range(NB):
                for j in range(2):
                    t = t_yT(b, j)
                    if b >= 2:
                        filled(act, t_y(b - 2, 1))
                    ps = filled(act, t)
                    copy_out(t, yT[b % 2][:, 4 * j:4 * j + 4, :], ps[:, :].rearrange("p (k t) -> p k t", k=4))
                act.wait_ge(s["x1_ready"], b + 1)
                A.activation(junk2, X[:, b, :], ACT.Square, accum_out=ss2[:, b:b + 1]).then_inc(s["ss2_ready"], 1)
                act.wait_ge(s["var2_ready"], b + 1)
                A.activation(sd2[:, b:b + 1], var2[:, b:b + 1], ACT.Sqrt).then_inc(s["sd2_ready"], 1)
                if b >= 1:
                    h2T_out(b - 1)
            h2T_out(NB - 1)
            for i in range(4):
                t = T_KEYS + i
                copy_out(t, keysT[:, 4 * i:4 * i + 4, :], filled(act, t)[:, :].rearrange("p (i n) -> p i n", i=4))

            def scores_out(i):
                hd, half = i // 2, i % 2
                if half == 0 and hd >= 2:
                    act.wait_ge(s["topk_done"], hd - 1)
                t = t_s(i, 0)
                copy_out(t, sc[hd % 2][:, 1:NB, half, :], filled(act, t)[:, :].rearrange("p (b n) -> p b n", b=4))
                t = t_s(i, 1)
                copy_out(t, sc[hd % 2][:, 0, half, :], filled(act, t)[:, 0:P])

            act.wait_ge(s["h2_ready"], NB)
            for i in range(16):
                if i >= 2:
                    filled(act, t_s(i - 2, 1))
                t = t_q(i, 0)
                copy_out(t, qTb[i % 2][:, P:NT], filled(act, t)[:, :])
                t = t_q(i, 1)
                copy_out(t, qTb[i % 2][:, 0:P], filled(act, t)[:, 0:P])
                if i >= 1:
                    scores_out(i - 1)
            scores_out(15)
            act.wait_ge(s["pair_ready"], PH)
            gflat = GATE[:, :, :, :].rearrange("p b h k -> p (b h k)")
            A.activation(gflat, gflat, ACT.Exp).then_inc(s["exp_done"], 1)

            act.wait_ge(s["zero_ready"], 1)
            with act.Fori(0, NB) as b:
                with act.Fori(0, PH // 2) as hp:
                    for par in range(2):
                        chunk = b * PH + hp * 2 + par
                        act.wait_ge(s["urow_used"], chunk * TOPK + USLOTS + TOPK)
                        A.activation(gelu[par], dots[par], ACT.Gelu_apprx_tanh).then_inc(s["gelu_ready"], 1)
                        act.wait_ge(s["wgt_ready"], chunk + 1)
                        for k in range(TOPK):
                            act.wait_ge(s["vrow_used"], chunk * TOPK + TOPK + k + 1 + VSLOTS - DSLOTS)
                            A.activation(diag[k % DSLOTS], ident[:, :], ACT.Copy, scale=wgt[par][:, k:k + 1]).then_inc(
                                s["diag_ready"], 1)
                act.wait_ge(s["acc_filled"], b + 1)
                act.sem_inc(s["act_chain"], 1)
                for j in range(2):
                    ins = A.copy(moe[:, bass.ds(b, 1), j * 512:(j + 1) * 512], bank[j][:, :].unsqueeze(1))
                ins.then_inc(s["acc_free"], 1)
            for b in range(NB):
                act.wait_ge(s["norm2_started"], b + 1)
                A.activation(junku[b % 2], X[:, b, :], ACT.Square, accum_out=ssf[:, b:b + 1]).then_inc(s["ssf_ready"], 1)
                act.wait_ge(s["varf_ready"], b + 1)
                A.activation(sdf[:, b:b + 1], varf[:, b:b + 1], ACT.Sqrt).then_inc(s["sdf_ready"], 1)

        @block.vector
        def _(dve):
            V = nc.vector
            chain = [0]

            def link(ins):
                chain[0] += 1
                ins.then_inc(s["dve_chain"], 1)
                dve.wait_ge(s["dve_chain"], chain[0])

            def frees(ins, t):
                ins.then_inc(bank_freed[t % 8], 1)

            def inverse_root(ss, var, sd, rs, n, got, said, sd_done, count):
                dve.wait_ge(s[got], count)
                V.tensor_scalar(var, ss, 1.0 / n, EPS, ALU.mult, ALU.add).then_inc(s[said], 1)
                dve.wait_ge(s[sd_done], count)
                link(V.reciprocal(rs, sd))

            for layer in range(3):
                for i, (lo, n) in enumerate(((0, P), (P, NLAT))):
                    t = T_MLP + 2 * layer + i
                    if t == T_MLP:
                        dve.wait_ge(s["mlp_loaded"], 128)
                    ps = filled(dve, t)
                    a, k = arg[:, lo:lo + n], turns[:, lo:lo + n]
                    frees(V.tensor_scalar(a, ps[0:64, 0:n], bfcol[:, layer:layer + 1], bfcol[:, 3:4], ALU.add, ALU.mult), t)
                    readout(dve, t)
                    link(V.tensor_scalar(k, a, 1.0 / (2.0 * math.pi), MAGIC, ALU.mult, ALU.add))
                    link(V.tensor_scalar(k, k, MAGIC, None, ALU.subtract))
                    for part in TWO_PI_PARTS:
                        link(V.scalar_tensor_tensor(a, k, -part, a, ALU.mult, ALU.add))
                    V.tensor_scalar(a, a, PI_SAFE, -PI_SAFE, ALU.min, ALU.max).then_inc(s["arg_ready"], 1)
            dve.wait_ge(s["act_chain"], 1)
            V.tensor_scalar(lg, decay, -1.0, None, ALU.mult).then_inc(s["lg_ready"], 1)
            dve.wait_ge(s["decays_ready"], 1)
            V.tensor_tensor(ef, ef, dist[:, 2, :].unsqueeze(1).to_broadcast([P, NH, P]), ALU.mult)
            V.tensor_scalar(zeta, zeta, P ** -0.5, None, ALU.mult)
            link(V.tensor_tensor(eb, eb, dist[:, 3, :].unsqueeze(1).to_broadcast([P, NH, P]), ALU.mult))
            link(V.tensor_tensor(mask[:, :, :], ef, eb, ALU.add))
            V.tensor_scalar(mask[:, :, :], mask[:, :, :], P ** -0.5, None, ALU.mult).then_inc(s["masks_ready"], 1)
            dve.wait_ge(s["ada_bias_loaded"], 48)
            for n in range(NADA):
                ps = filled(dve, T_MOD + n)
                frees(V.tensor_tensor(modrow[:, n * 512:(n + 1) * 512], ps[0:2, :], bada[:, n * 512:(n + 1) * 512], ALU.add),
                      T_MOD + n)
            for n in range(NADA):
                readout(dve, T_MOD + n)
            m = modrow[:, D:2 * D]
            link(V.scalar_tensor_tensor(m, m, 1.0, grow[:, 0:D], ALU.add, ALU.mult))
            m = modrow[:, 4 * D:5 * D]
            V.scalar_tensor_tensor(m, m, 1.0, grow[:, D:2 * D], ALU.add, ALU.mult).then_inc(s["mod_ready"], 1)
            inverse_root(ss1, var1, sd1, rs1, D, "ss1_ready", "var1_ready", "sd1_ready", 1)
            dve.wait_ge(s["mod1_loaded"], 64)
            for b in range(NB):
                scale, shift = mod1[min(b, 1)]
                if b >= 2:
                    filled(dve, T_HT + 2 * (b - 2) + 1)
                link(V.scalar_tensor_tensor(hbuf[b % 2], X[:, b, :], rs1[:, b:b + 1], scale, ALU.mult, ALU.mult))
                V.tensor_tensor(hbuf[b % 2], hbuf[b % 2], shift, ALU.add).then_inc(s["h_ready"], 1)
            dve.wait_ge(s["const_loaded"], 32)
            for j, dst in enumerate((qt, kt)):
                for b in range(1, NB):
                    t = T_QKVG + j * NB + b
                    ps = filled(dve, t)[:, :].rearrange("p (h a c) -> p h a c", h=NH, a=2)
                    out = dst[:, b, :].rearrange("p (h a c) -> p h a c", h=NH, a=2)
                    cos = rope[:, 0, b - 1, :].unsqueeze(1).to_broadcast([P, NH, 64])
                    sin = rope[:, 1, b - 1, :].unsqueeze(1).to_broadcast([P, NH, 64])
                    for a in range(2):
                        V.tensor_tensor(ropt1[:, :, a, :], ps[:, :, a, :], cos, ALU.mult)
                    V.tensor_tensor(ropt2[:, :, 0, :], ps[:, :, 1, :], sin, ALU.mult)
                    frees(V.tensor_tensor(ropt2[:, :, 1, :], ps[:, :, 0, :], sin, ALU.mult), t)
                    readout(dve, t)
                    V.tensor_tensor(out[:, :, 0, :], ropt1[:, :, 0, :], ropt2[:, :, 0, :], ALU.subtract)
                    V.tensor_tensor(out[:, :, 1, :], ropt1[:, :, 1, :], ropt2[:, :, 1, :], ALU.add).then_inc(s["rope_ready"], 1)
                    dve.wait_ge(s["rope_ready"], 4 * j + b)
            dve.wait_ge(s["retg_loaded"], 16)
            for b in range(NB):
                readout(dve, T_QKVG + 3 * NB + b)
                V.tensor_tensor(gg[:, b, :], gg[:, b, :], retg, ALU.mult).then_inc(s["gate_ready"], 1)
            dve.wait_ge(s["gate_ready"], NB)
            dve.wait_ge(s["rope_ready"], 8)
            dve.wait_ge(s["state_loaded"], 32)
            readout(dve, T_QKVG + NB)

            def state(i):
                b, d = KV[i]
                t = T_KV + i
                ps = filled(dve, t)
                if b == 0:
                    V.tensor_copy(stout[:, d, :], ps[:, :]).then_inc(s["stout_ready"], 1)
                    dve.wait_ge(s["stout_ready"], i + 1)
                    dve.sem_inc(bank_freed[t % 8], 1)
                    return
                old, new = (Sf[b - 1], Sf[b]) if d == 0 else (Sb[b - 1], Sb[b - 2])
                for h in range(NH):
                    c = slice(h * P, (h + 1) * P)
                    ins = V.scalar_tensor_tensor(new[:, c], old[:, c], chunkdec[:, 4 * d + h:4 * d + h + 1], ps[:, c],
                                                 ALU.mult, ALU.add)
                frees(ins, t)
                readout(dve, t)

            for i, (b, d) in enumerate(KV):
                if i >= 2:
                    filled(dve, T_KV + i - 2)
                V.tensor_tensor(kz[i % 2].rearrange("p (h e) -> p h e", h=NH), kt[:, b, :].rearrange("p (h e) -> p h e", h=NH),
                                zeta[:, 4 * d:4 * d + 4].unsqueeze(2).to_broadcast([P, NH, P]), ALU.mult).then_inc(s["kz_ready"], 1)
                if i >= 1:
                    state(i - 1)
            state(len(KV) - 1)
            for b in range(NB):
                t = t_score(b)
                if b >= 2:
                    filled(dve, t_intra(b - 2))
                frees(V.tensor_tensor(sm[b % 2], filled(dve, t)[:, :], mask[:, :, :].rearrange("p h n -> p (h n)"), ALU.mult), t)
                o = ob[b % 2]
                readout(dve, t_intra(b))
                if b == 0:
                    dve.sem_inc(s["o_ready"], 1)
                else:
                    for d in range(2):
                        t = t_cross(b, d)
                        ps = filled(dve, t)
                        for h in range(NH):
                            c = slice(h * P, (h + 1) * P)
                            ins = V.scalar_tensor_tensor(o[:, c], ps[:, c], xi[:, 4 * d + h:4 * d + h + 1], o[:, c], ALU.mult, ALU.add)
                        frees(ins, t)
                        readout(dve, t)
                    dve.sem_inc(s["o_ready"], 1)
                inverse_root(sso, varo, sdo, rso, P, "sso_ready", "varo_ready", "sdo_ready", b + 1)
                for h in range(NH):
                    c = slice(h * P, (h + 1) * P)
                    ins = V.scalar_tensor_tensor(yret[:, b, c], o[:, c], rso[:, h:h + 1], gg[:, b, c], ALU.mult, ALU.mult)
                ins.then_inc(s["yret_ready"], 1)
            for i in range(12):
                u = uT[i % 3]
                w0, w2 = convc[:, i:i + 1], convc[:, 24 + i:25 + i]
                dve.wait_ge(s["conv_center"], 2 * i + 2)
                pl, pc = filled(dve, t_proj(i, 0)), filled(dve, t_proj(i, 1))
                V.scalar_tensor_tensor(u[:, P + 1:NT], pl[:, 0:NLAT - 1], w0, u[:, P + 1:NT], ALU.mult, ALU.add)
                link(V.scalar_tensor_tensor(u[:, 1:P], pc[:, 0:P - 1], w0, u[:, 1:P], ALU.mult, ALU.add))
                frees(V.scalar_tensor_tensor(u[:, P:NT - 1], pl[:, 1:NLAT], w2, u[:, P:NT - 1], ALU.mult, ALU.add), t_proj(i, 0))
                frees(V.scalar_tensor_tensor(u[:, 0:P - 1], pc[:, 1:P], w2, u[:, 0:P - 1], ALU.mult, ALU.add), t_proj(i, 1))
            dve.wait_ge(s["filt_loaded"], 48)
            dve.wait_ge(s["bias_loaded"], 16)
            for i in range(12):
                for part in range(2):
                    readout(dve, t_uback(i, part))
            n_freq = n_filt = 0
            for sg, (b0, nt) in enumerate(SEGS):
                for o in range(2):
                    for t in range(nt):
                        hf, hb = tt4[2 * (t % 2)], tt4[2 * (t % 2) + 1]
                        tf, tb = t_filt(sg, o, t, 0), t_filt(sg, o, t, 1)
                        if n_filt >= 2:
                            dve.wait_ge(s["filt_ready"], n_filt - 1)
                        n_filt += 1
                        frees(V.tensor_tensor(hf, filled(dve, tf)[:, :], window[:, b0 + t, :], ALU.mult), tf)
                        frees(V.tensor_tensor(hb, filled(dve, tb)[:, :], window[:, b0 + t, :], ALU.mult), tb)
                        readout(dve, tf)
                        readout(dve, tb)
                        if t == 0:
                            V.tensor_tensor(hf[0:1, :], hf[0:1, :], fbias[:, o * HY:(o + 1) * HY], ALU.add)
                            link(V.memset(hb[0:1, :], 0.0))
                        V.tensor_tensor(he[:, t, :], hf, hb, ALU.add)
                        V.tensor_tensor(ho[:, t, :], hf, hb, ALU.subtract).then_inc(s["filt_ready"], 1)
                    for f in range(nt):
                        i = n_freq % 2
                        readout(dve, t_freq(sg, o, f, 0))
                        readout(dve, t_freq(sg, o, f, 1))
                        if f == 0:
                            readout(dve, t_freq(sg, o, 0, 4))
                        if f == 0:
                            dve.wait_ge(s["filt_ready"], n_filt)
                        else:
                            dve.wait_ge(s["spectrum_ready"], n_freq)
                        a, bb = filled(dve, t_freq(sg, o, f, 2)), filled(dve, t_freq(sg, o, f, 3))
                        V.tensor_tensor(tt4[0], a[:, :], Ps[i], ALU.mult)
                        V.tensor_tensor(tt4[1], bb[:, :], Qs[i], ALU.mult)
                        frees(V.tensor_tensor(tt4[2], a[:, :], Qs[i], ALU.mult), t_freq(sg, o, f, 2))
                        frees(V.tensor_tensor(tt4[3], bb[:, :], Pn if f == 0 else Ps[i], ALU.mult), t_freq(sg, o, f, 3))
                        readout(dve, t_freq(sg, o, f, 3))
                        readout(dve, t_freq(sg, o, f, 2))
                        V.tensor_tensor(Rr[:, f, :], tt4[0], tt4[1], ALU.subtract)
                        V.tensor_tensor(Ri[:, f, :], tt4[2], tt4[3], ALU.add).then_inc(s["spectrum_ready"], 1)
                        n_freq += 1
                    for t in range(nt):
                        ti = t_inv(sg, o, t)
                        ps = filled(dve, ti)
                        V.tensor_tensor(U[:, b0 + t, 0, :], ps[:, :], U[:, b0 + t, 1 + o, :], ALU.mult).then_inc(s["z_ready"], 1)
                        dve.wait_ge(s["z_ready"], {0: o + 1, 1: 2 + 4 * o + t + 1}[sg])
                        dve.sem_inc(bank_freed[ti % 8], 1)
            inverse_root(ssy, vary, sdy, rsy, HY, "ssy_ready", "vary_ready", "sdy_ready", 1)
            dve.wait_ge(s["hyg_loaded"], 16)
            for b in range(NB):
                V.scalar_tensor_tensor(U[:, b, 0, :], U[:, b, 0, :], rsy[:, b:b + 1], hyg, ALU.mult, ALU.mult).then_inc(
                    s["yhy_ready"], 1)
            dve.wait_ge(s["mod2_loaded"], 96)
            dve.wait_ge(s["x_again"], 32)
            for b in range(NB):
                g1, scale, shift = mod2[min(b, 1)]
                for j in range(2):
                    c = slice(j * 512, (j + 1) * 512)
                    t = t_y(b, j)
                    frees(V.tensor_tensor(gy[j], filled(dve, t)[:, :], g1[:, c], ALU.mult), t)
                    readout(dve, t)
                    ins = V.tensor_tensor(X[:, b, c], X[:, b, c], gy[j], ALU.add)
                    if j == 0:
                        link(ins)
                    else:
                        ins.then_inc(s["x1_ready"], 1)
                inverse_root(ss2[:, b:b + 1], var2[:, b:b + 1], sd2[:, b:b + 1], rs2[:, b:b + 1], D,
                             "ss2_ready", "var2_ready", "sd2_ready", b + 1)
                link(V.scalar_tensor_tensor(H2[:, b, :], X[:, b, :], rs2[:, b:b + 1], scale, ALU.mult, ALU.mult))
                V.tensor_tensor(H2[:, b, :], H2[:, b, :], shift, ALU.add).then_inc(s["h2_ready"], 1)
            for i in range(4):
                filled(dve, T_KEYS + i)
            filled(dve, t_h2T(NB - 1, 1))
            dve.wait_ge(s["h2_ready"], NB)
            for hd in range(PH):
                S = sc[hd % 2]
                for i in (2 * hd, 2 * hd + 1):
                    readout(dve, t_s(i, 0))
                    readout(dve, t_s(i, 1))
                halves = [(b, a) for b in range(NB) for a in range(2)]

                def sixteen_best(vals, outv, outi):
                    n = len(vals)
                    for j in range(n):
                        ins = V.max(outv[j][:, 0:8], vals[j])
                    link(ins)
                    for j in range(n):
                        ins = V.max_index(outi[j][:, 0:8], outv[j][:, 0:8], vals[j])
                    link(ins)
                    for j in range(n):
                        ins = V.match_replace(vals[j], outv[j][:, 0:8], vals[j], FLOAT_LOW)
                    link(ins)
                    for j in range(n):
                        ins = V.max(outv[j][:, 8:16], vals[j])
                    link(ins)
                    for j in range(n):
                        ins = V.max_index(outi[j][:, 8:16], outv[j][:, 8:16], vals[j])
                    return ins

                link(sixteen_best([S[:, b, a, :] for b, a in halves], [topv[:, b, a, :] for b, a in halves],
                                  [topi[:, b, a, :] for b, a in halves]))
                V.tensor_copy(topif, topi)
                link(V.tensor_tensor(cand, topv[:, :, 0, :].unsqueeze(3).to_broadcast([P, NB, 16, 16]),
                                     topv[:, :, 1, :].unsqueeze(2).to_broadcast([P, NB, 16, 16]), ALU.add))
                pp = pairp.rearrange("p (b k) -> p b k", b=NB)
                link(sixteen_best([cand[:, b, :, :].rearrange("p i j -> p (i j)") for b in range(NB)],
                                  [pairv[:, b, :] for b in range(NB)], [pp[:, b, :] for b in range(NB)]))
                V.tensor_scalar(posa, pairp, 4, None, ALU.logical_shift_right)
                link(V.tensor_scalar(posb, pairp, 15, None, ALU.bitwise_and))
                V.tensor_copy(posaf, posa)
                link(V.tensor_copy(posbf, posb))
                for half, pos, sel in ((0, posaf, sel1), (1, posbf, sel2)):
                    oh = onehot.rearrange("p (q j) -> p q j", j=TOPK)
                    link(V.tensor_tensor(oh, pos.unsqueeze(2).to_broadcast([P, 80, TOPK]),
                                         iota16[:, :].unsqueeze(1).to_broadcast([P, 80, TOPK]), ALU.is_equal))
                    oh4 = onehot.rearrange("p (b q j) -> p b q j", b=NB, j=TOPK)
                    link(V.tensor_tensor(oh4, oh4, topif[:, :, half, :].unsqueeze(2).to_broadcast([P, NB, TOPK, TOPK]), ALU.mult))
                    link(V.tensor_reduce(sel, oh, AX.X, ALU.add))
                V.scalar_tensor_tensor(IDX[:, :, hd, :], sel1.rearrange("p (b k) -> p b k", b=NB), float(NKEYS),
                                       sel2.rearrange("p (b k) -> p b k", b=NB), ALU.mult, ALU.add).then_inc(s["topk_done"], 1)
                V.tensor_tensor(GATE[:, :, hd, :], pairv, pairv[:, :, 0:1].to_broadcast([P, NB, TOPK]),
                                ALU.subtract).then_inc(s["pair_ready"], 1)
            dve.wait_ge(s["exp_done"], 1)
            gh = GATE[:, :, :, :].rearrange("p b h k -> p (b h) k")
            link(V.tensor_reduce(gsum, gh, AX.X, ALU.add))
            link(V.reciprocal(grec, gsum))
            V.tensor_tensor(gh, gh, grec.unsqueeze(2).to_broadcast([P, NB * PH, TOPK]), ALU.mult).then_inc(s["gates_ready"], 1)
            link(V.memset(zero, 0.0))
            filled(dve, t_s(15, 1))
            dve.wait_ge(s["gates_ready"], 1)
            dve.sem_inc(s["zero_ready"], 1)
            dve.sem_inc(s["urow_used"], USLOTS)
            dve.sem_inc(s["acc_free"], 1)
            chain_base = chain[0]
            IDXF = IDX.rearrange("p b h k -> p (b h k)")
            GATEF = GATE.rearrange("p b h k -> p (b h k)")
            H2F = H2.rearrange("p b d -> p (b d)")
            with dve.Fori(0, NB) as b:
                V.tensor_copy(h2cur, H2F[:, bass.ds(b * D, D)]).then_inc(s["dve_chain"], 1)
                dve.wait_ge(s["dve_chain"], chain_base + 1 + b)
                dve.sem_inc(s["pool_go"], 1)
                with dve.Fori(0, PH // 2) as hp:
                    for par in range(2):
                        chunk = b * PH + hp * 2 + par
                        dve.wait_ge(s["vrow_used"], chunk * TOPK + VSLOTS)
                        dve.sem_inc(s["pool_go"], 1)
                        V.tensor_copy(idxc[par], IDXF[:, bass.ds((b * PH + hp * 2 + par) * TOPK, TOPK)]).then_inc(s["idx_ready"], 1)
                        for k in range(TOPK):
                            dve.wait_ge(s["urow_used"], chunk * TOPK + k + USLOTS - 1)
                            dve.wait_ge(urow_full[k % USLOTS], 16 * (chunk * (TOPK // USLOTS) + k // USLOTS + 1))
                            V.tensor_tensor_reduce(out=junku[k % 2], in0=uslot[k % USLOTS], in1=h2cur, scale=1.0, scalar=0.0,
                                                   op0=ALU.mult, op1=ALU.add, accum_out=dots[par][:, k:k + 1]).then_inc(
                                s["urow_used"], 1)
                        dve.wait_ge(s["gelu_ready"], chunk + 1)
                        dve.sem_inc(s["pool_go"], 1)
                        V.tensor_tensor(wgt[par], gelu[par], GATEF[:, bass.ds((b * PH + hp * 2 + par) * TOPK, TOPK)],
                                        ALU.mult).then_inc(s["wgt_ready"], 1)
            chain[0] += NB
            dve.wait_ge(s["acc_free"], NB + 1)
            dve.wait_ge(s["mod3_loaded"], 48)
            for b in range(NB):
                link(V.tensor_tensor(moe[:, b, :], moe[:, b, :], gt2[min(b, 1)], ALU.mult))
                V.tensor_tensor(X[:, b, :], X[:, b, :], moe[:, b, :], ALU.add).then_inc(s["norm2_started"], 1)
                dve.wait_ge(s["ssf_ready"], b + 1)
                V.tensor_scalar(varf[:, b:b + 1], ssf[:, b:b + 1], 1.0 / D, EPS, ALU.mult, ALU.add).then_inc(s["varf_ready"], 1)
                dve.wait_ge(s["sdf_ready"], b + 1)
                link(V.reciprocal(rsf[:, b:b + 1], sdf[:, b:b + 1]))
                V.scalar_tensor_tensor(moe[:, b, :], X[:, b, :], rsf[:, b:b + 1], fing, ALU.mult, ALU.mult).then_inc(
                    s["y_ready"], 1)

        @block.tensor
        def _(pe):
            MM = nc.tensor.matmul

            def done(ins, t):
                ins.then_inc(bank_filled[t % 8], 1)

            def product(out, t, pairs):
                for i, (l, r) in enumerate(pairs):
                    ins = MM(out, l, r, start=(i == 0), stop=(i == len(pairs) - 1))
                done(ins, t)

            def turn(t, tiles, m=P):
                ps = free_bank(pe, t)
                for i, x in enumerate(tiles):
                    n = x.shape[0]
                    ins = nc.tensor.transpose(ps[0:m, i * P:i * P + n], x, ident[0:n, 0:n])
                done(ins, t)

            pe.wait_ge(s["c_loaded"], 32)
            turn(T_COND, [condrows])
            pe.wait_ge(s["conv_loaded"], 16)
            turn(T_CONV, [convrows])
            pe.wait_ge(s["mlp_loaded"], 128)
            for layer, w in enumerate((wf1, wf2, wf3)):
                for i, (lo, n) in enumerate(((0, P), (P, NLAT))):
                    t = T_MLP + 2 * layer + i
                    if layer:
                        pe.wait_ge(s["sin_done"], 2 * layer - 1 + i)
                    src = feat if layer == 0 else hid
                    product(free_bank(pe, t)[0:64, 0:n], t, [(w, src[:, lo:lo + n])])
            readout(pe, T_COND)
            for n in range(NADA):
                w = weight(pe, n)
                t = T_MOD + n
                product(free_bank(pe, t)[0:2, :], t, [(silu_c[:, k:16:8], w[:, k, :]) for k in range(KD)])
                filled(pe, t)
                pe.sem_inc(s["weights_used"], 1)
            for b in range(NB):
                pe.wait_ge(s["h_ready"], b + 1)
                for j in range(2):
                    turn(T_HT + 2 * b + j, [hbuf[b % 2][:, (4 * j + i) * P:(4 * j + i + 1) * P] for i in range(4)])
            for j in range(4):
                w = weight(pe, W_QKVG + j)
                for b in range(NB):
                    if j == 0:
                        readout(pe, T_HT + 2 * b)
                        readout(pe, T_HT + 2 * b + 1)
                    t = T_QKVG + j * NB + b
                    product(free_bank(pe, t)[:, :], t, [(hT[:, k, b * P:(b + 1) * P], w[:, k, :]) for k in range(KD)])
                filled(pe, t)
                pe.sem_inc(s["weights_used"], 1)
            for j, src in enumerate((qt, kt)):
                for b in range(NB):
                    if b == 0:
                        readout(pe, T_QKVG + j * NB)
                    else:
                        pe.wait_ge(s["rope_ready"], 4 * j + b)
                    turn(T_QK + j * NB + b, [src[:, b, h * P:(h + 1) * P] for h in range(NH)])
            for b in range(NB):
                readout(pe, T_QKVG + 2 * NB + b)
            for i, (b, d) in enumerate(KV):
                pe.wait_ge(s["kz_ready"], i + 1)
                ps = free_bank(pe, T_KV + i)
                for h in range(NH):
                    c = slice(h * P, (h + 1) * P)
                    ins = MM(ps[:, c], kz[i % 2][:, c], vt[:, b, c], start=True, stop=True)
                done(ins, T_KV + i)
            for b in range(NB):
                readout(pe, T_QK + b)
                readout(pe, T_QK + NB + b)
                tok = slice(b * P, (b + 1) * P)
                ps = free_bank(pe, t_score(b))
                for h in range(NH):
                    ins = MM(ps[:, h * P:(h + 1) * P], kT[:, h, tok], qT[:, h, tok], start=True, stop=True)
                done(ins, t_score(b))
                if b:
                    if b == 1:
                        for i in range(len(KV)):
                            readout(pe, T_KV + i)
                    for d, S in enumerate((Sf[b - 1], Sb[b - 1])):
                        t = t_cross(b, d)
                        ps = free_bank(pe, t)
                        for h in range(NH):
                            c = slice(h * P, (h + 1) * P)
                            ins = MM(ps[:, c], qT[:, h, tok], S[:, c], start=True, stop=True)
                        done(ins, t)
                readout(pe, t_score(b))
                ps = free_bank(pe, t_intra(b))
                for h in range(NH):
                    c = slice(h * P, (h + 1) * P)
                    ins = MM(ps[:, c], sm[b % 2][:, c], vt[:, b, c], start=True, stop=True)
                done(ins, t_intra(b))

            def rows_back(i):
                u = uT[i % 3]
                readout(pe, t_proj(i, 0))
                readout(pe, t_proj(i, 1))
                turn(t_uback(i, 0), [u[:, (1 + b) * P:(2 + b) * P] for b in range(4)])
                turn(t_uback(i, 1), [u[:, 0:P]])

            for i in range(12):
                w = weight(pe, W_HY + i // 4)
                c = slice((i % 4) * P, (i % 4 + 1) * P)
                for part, lo, n in ((0, P, NLAT), (1, 0, P)):
                    t = t_proj(i, part)
                    product(free_bank(pe, t)[:, 0:n], t, [(w[:, k, c], hT[:, k, lo:lo + n]) for k in range(KD)])
                if i % 4 == 3:
                    filled(pe, t)
                    pe.sem_inc(s["weights_used"], 1)
                if i >= 1:
                    rows_back(i - 1)
            rows_back(11)
            pe.wait_ge(s["filt_loaded"], 48)
            pe.wait_ge(s["sin_done"], 6)
            pe.wait_ge(s["dft_loaded"], 16)
            for i in range(12):
                readout(pe, t_uback(i, 0))
                readout(pe, t_uback(i, 1))
            n_filt = n_freq = n_z = 0
            for sg, (b0, nt) in enumerate(SEGS):
                dft = dftc if sg == 0 else dftl
                for o in range(2):
                    for t in range(nt):
                        tok = slice((b0 + t) * P, (b0 + t + 1) * P)
                        for d in range(2):
                            tk = t_filt(sg, o, t, d)
                            lo = (2 * d + o) * HY
                            product(free_bank(pe, tk)[:, :], tk, [(hid[:, tok], w4[:, lo:lo + HY])])
                    n_filt += nt
                    pe.wait_ge(s["filt_ready"], n_filt)
                    if n_z:
                        pe.wait_ge(s["z_ready"], n_z)
                    for f in range(nt):
                        fc = slice(f * P, (f + 1) * P)
                        for j in range(5 if f == 0 else 4):
                            tk = t_freq(sg, o, f, j)
                            ps = free_bank(pe, tk)
                            if j == 4:
                                product(ps[0:1, :], tk, [(dft[:, 1, t, 0:1], he[:, t, :]) for t in range(nt)])
                            else:
                                mat = dft[:, j % 2]
                                src = [he[:, t, :] if j == 0 else ho[:, t, :] if j == 1 else U[:, b0 + t, 0, :] for t in range(nt)]
                                product(ps[:, :], tk, [(mat[:, t, fc], src[t]) for t in range(nt)])
                    n_freq += nt
                    pe.wait_ge(s["spectrum_ready"], n_freq)
                    for t in range(nt):
                        tc = slice(t * P, (t + 1) * P)
                        tk = t_inv(sg, o, t)
                        product(free_bank(pe, tk)[:, :], tk, [(dft[:, 0, f, tc], Rr[:, f, :]) for f in range(nt)] +
                                [(dft[:, 2, f, tc], Ri[:, f, :]) for f in range(nt)])
                    n_z += nt

            def h2_turn(b):
                pe.wait_ge(s["h2_ready"], b + 1)
                for j in range(2):
                    turn(t_h2T(b, j), [H2[:, b, (4 * j + i) * P:(4 * j + i + 1) * P] for i in range(4)])

            for b in range(NB):
                pe.wait_ge(s["yhy_ready"], b + 1)
                turn(t_yT(b, 0), [U[:, b, 0, i * P:(i + 1) * P] for i in range(4)])
                pe.wait_ge(s["yret_ready"], b + 1)
                turn(t_yT(b, 1), [yret[:, b, i * P:(i + 1) * P] for i in range(4)])
                readout(pe, t_yT(b, 0))
                readout(pe, t_yT(b, 1))
                for j in range(2):
                    w = weight(pe, W_OUT + j)
                    t = t_y(b, j)
                    product(free_bank(pe, t)[:, :], t, [(yT[b % 2][:, k, :], w[:, k, :]) for k in range(KD)])
                if b >= 1:
                    h2_turn(b - 1)
            filled(pe, t)
            pe.sem_inc(s["weights_used"], 2)
            h2_turn(NB - 1)
            pe.wait_ge(s["keys_loaded"], 16)
            for i in range(4):
                turn(T_KEYS + i, [keyraw[:, 4 * i + j, :] for j in range(4)])
            for i in range(4):
                readout(pe, T_KEYS + i)
            for b in range(NB):
                readout(pe, t_h2T(b, 0))
                readout(pe, t_h2T(b, 1))

            def scores(i):
                q = qTb[i % 2]
                readout(pe, t_q(i, 0))
                readout(pe, t_q(i, 1))
                for part, blocks in ((0, range(1, NB)), (1, range(1))):
                    t = t_s(i, part)
                    ps = free_bank(pe, t)
                    for j, b in enumerate(blocks):
                        ins = MM(ps[:, j * P:(j + 1) * P], q[:, b * P:(b + 1) * P], keysT[:, i, :], start=True, stop=True)
                    done(ins, t)

            for i in range(16):
                w = weight(pe, W_Q + i // 4)
                c = slice((i % 4) * P, (i % 4 + 1) * P)
                for part, lo, n in ((0, P, NLAT), (1, 0, P)):
                    t = t_q(i, part)
                    product(free_bank(pe, t)[:, 0:n], t, [(w[:, k, c], h2T[:, k, lo:lo + n]) for k in range(KD)])
                if i % 4 == 3:
                    filled(pe, t)
                    pe.sem_inc(s["weights_used"], 1)
                if i >= 1:
                    scores(i - 1)
            scores(15)
            for t in range(T_PEER - 8, T_PEER):
                readout(pe, t)
            pe.wait_ge(s["zero_ready"], 1)
            pe.sem_inc(s["vrow_used"], VSLOTS + TOPK)
            with pe.Fori(0, NB) as b:
                pe.wait_ge(s["acc_free"], b + 1)
                for j in range(2):
                    MM(bank[j][:, :], zero[:, 0:P], zero, start=True, stop=False)
                with pe.Fori(0, PH // 2) as hp:
                    for par in range(2):
                        chunk = b * PH + hp * 2 + par
                        for k in range(TOPK):
                            pe.wait_ge(s["diag_ready"], chunk * TOPK + k + 1)
                            pe.wait_ge(vrow_full[k % VSLOTS], 16 * (chunk * (TOPK // VSLOTS) + k // VSLOTS + 1))
                            MM(bank[0][:, :], diag[k % DSLOTS], vslot[k % VSLOTS][:, 0:512], start=False, stop=False)
                            MM(bank[1][:, :], diag[k % DSLOTS], vslot[k % VSLOTS][:, 512:D], start=False, stop=False).then_inc(
                                s["vrow_used"], 1)
                for j in range(2):
                    ins = MM(bank[j][:, :], zero[:, 0:P], zero, start=False, stop=True)
                ins.then_inc(s["acc_filled"], 1)


_IN_SHAPED = ["x_prompt", "x_sample", "w_ada", "w_in", "w_out", "peer_wq", "peer_u", "peer_v"]


def kernel(**inputs):
    import concourse.bacc as _bacc
    from concourse.bass_utils import run_bass_kernel_spmd as _run

    nc = _bacc.Bacc("TRN2", target_bir_lowering=False, num_devices=1)
    a = {k: np.asarray(v) for k, v in inputs.items()}
    laid = {
        "x_prompt": a["x_prompt"][0], "x_sample": a["x_sample"][0],
        "conds": np.concatenate([a["c_ctx"].reshape(8, P), a["c"].reshape(8, P)], axis=0),
        "w_ada": a["w_ada"][0], "b_ada": a["b_ada"], "norm1_g": a["norm1_g"], "norm2_g": a["norm2_g"],
        "w_in": a["w_in"][0], "w_out": a["w_out"][0], "peer_wq": a["peer_wq"][0],
        "conv_rows": np.concatenate([a["hy_conv_w"].reshape(36, P), a["hy_conv_b"].reshape(12, P)], axis=0),
        "hy_w1": a["hy_w1"][0], "hy_w2": a["hy_w2"][0], "hy_w3": a["hy_w3"][0], "hy_w4": a["hy_w4"][0],
        "hy_b1": a["hy_b1"].reshape(64, 1), "hy_b2": a["hy_b2"].reshape(64, 1), "hy_b3": a["hy_b3"].reshape(64, 1),
        "hy_freq": a["hy_freq"].reshape(64, 1), "hy_bias": a["hy_bias"].reshape(1, 2 * HY), "hy_norm_g": a["hy_norm_g"],
        "ret_decay_fwd": a["ret_decay_fwd"], "ret_decay_bwd": a["ret_decay_bwd"], "ret_norm_g": a["ret_norm_g"],
        "state_ret_fwd": a["state_ret_fwd"][0, 0].transpose(1, 0, 2), "state_ret_bwd": a["state_ret_bwd"][0, 0].transpose(1, 0, 2),
        "peer_keys": a["peer_keys"].reshape(16, P, P), "peer_u": a["peer_u"][0], "peer_v": a["peer_v"][0],
        "final_g": a["final_g"].reshape(1, D),
    }
    laid.update(shape_constants())
    arrays, io = {}, {}
    for name, x in laid.items():
        x = np.ascontiguousarray(x)
        arrays["in_" + name] = x
        io[name] = nc.dram_tensor("in_" + name, x.shape, mybir.dt.from_np(x.dtype), kind="ExternalInput").ap()
    io["mod_scratch"] = nc.dram_tensor("mod_scratch", (2, 6 * D), F32, kind="Internal").ap()
    outs = {"y_prompt": (P, D), "y_sample": (NLAT, D), "new_fwd": (P, NH, P), "new_bwd": (P, NH, P)}
    for name, shape in outs.items():
        io[name] = nc.dram_tensor("out_" + name, shape, F32, kind="ExternalOutput").ap()
    build_trunk_layer(nc, io)
    r = _run(nc, [arrays], core_ids=[0]).results[0]
    return (r["out_y_prompt"].reshape(1, P, D), r["out_y_sample"].reshape(1, NLAT, D),
            r["out_new_fwd"].transpose(1, 0, 2).reshape(1, 1, NH, P, P), r["out_new_bwd"].transpose(1, 0, 2).reshape(1, 1, NH, P, P))
```

```python
from contextlib import ExitStack
import math

import numpy as np
import concourse.bass as bass
from concourse import mybir

F32 = mybir.dt.float32
U32 = mybir.dt.uint32
ALU = mybir.AluOpType
ACT = mybir.ActivationFunctionType
AX = mybir.AxisListType

P = 128
D = 1024
KD = D // P
NLAT = 512
NB = 5
NT = NB * P
HY = 512
NH = 4
GRID_W = 64
PH = 8
TOPK = 16
NKEYS = 128
NEXP = NKEYS * NKEYS
EPS = 1e-6
NADA = 12
NWSLOT = 3
USLOTS = 8
VSLOTS = 8
PSLOTS = 4
PSTEP = 8
NQ = 2 * PH
NL = NB - 1
DSLOTS = 4
MAGIC = 12582912.0
TWO_PI_PARTS = (6.28125, 0.0019350051879882812, 3.0199159819e-07)
PI_SAFE = 3.1415925
FLOAT_LOW = -3.0e38


def shape_constants():
    f8 = np.float64
    out = {}
    out["ident"] = np.eye(P)
    for name, L in (("lat", NLAT), ("ctx", P)):
        t = np.arange(L, dtype=f8)
        ang = 2.0 * np.pi * ((t[:, None] * t[None, :]) % (2 * L)) / (2 * L)
        c, s = np.cos(ang), np.sin(ang)
        s[:, 0] = (-1.0) ** t
        nt = L // P
        out["dft_" + name] = np.concatenate([
            m.reshape(nt, P, L).transpose(1, 0, 2).reshape(P, nt * L) for m in (c, s, s.T)], axis=1)
    feats, wins = [], []
    for L in (P, NLAT):
        t = np.linspace(0.0, 1.0, L, dtype=np.float32)[:, None]
        w = (np.float32(2.0 * math.pi) * np.arange(L, dtype=np.float32)[:, None] / np.float32(L)).astype(np.float32)
        f = np.linspace(1e-4, 15, 16, dtype=np.float32)[None, :]
        fw = (f * w).astype(np.float32)
        feats.append(np.concatenate([t, np.cos(fw), -np.sin(fw)], axis=-1))
        lo, hi = math.log(1e-2) / 1.5, math.log(1e-2) / 0.3
        deltas = np.abs(np.linspace(lo, hi, HY, dtype=np.float32))
        wins.append(np.exp(-t * deltas[None, :]))
    out["feat_t"] = np.concatenate(feats, axis=0).T
    win = np.concatenate(wins, axis=0).reshape(NB, P, HY)
    out["window"] = win.transpose(1, 0, 2).reshape(P, NB * HY)
    t = np.arange(NLAT)
    inv = (10000.0 ** (-np.arange(32, dtype=np.float32) / np.float32(32))).astype(np.float32)
    ang = np.concatenate([(t // GRID_W).astype(np.float32)[:, None] * inv,
                          (t % GRID_W).astype(np.float32)[:, None] * inv], axis=1)
    rope = np.stack([np.cos(ang), np.sin(ang)], axis=1).reshape(4, P, 2, 64)
    out["rope"] = rope.transpose(1, 2, 0, 3).reshape(P, 2 * 4 * 64)
    m, n = np.arange(P)[:, None], np.arange(P)[None, :]
    out["dist"] = np.concatenate([np.maximum(n - m, 0), np.maximum(m - n, 0), n >= m, m >= n], axis=1)
    cols = np.zeros((P, 8))
    i = np.arange(P)
    cols[:, 0], cols[:, 1], cols[:, 2], cols[:, 3] = i + 1, 127 - i, 128 - i, i
    for j, L in ((4, P), (6, NLAT)):
        cols[:, j] = np.where(i == 0, 1.0 / (2 * L), 2.0 / (2 * L))
        cols[:, j + 1] = np.where(i == 0, 0.0, 2.0 / (2 * L))
    out["cols"] = cols
    out["iota16"] = np.tile(np.arange(TOPK)[None, :], (P, 1))
    return {k: np.ascontiguousarray(v.astype(np.float32)) for k, v in out.items()}


def build_trunk_layer(nc, io):
    ctx = ExitStack()
    with ctx:
        def sb(name, shape, dt=F32):
            return ctx.enter_context(nc.sbuf_tensor(name, shape, dt))

        def sem(name):
            return ctx.enter_context(nc.semaphore(name))

        bank = [ctx.enter_context(nc.psum_tensor(f"bank{i}", [P, 512], F32)) for i in range(8)]

        X = sb("X", [P, NB, D])
        HA = sb("HA", [P, NB * D])
        W = sb("W", [P, NWSLOT * KD * 512])
        DA = sb("DA", [P, 6 * D])
        RA = sb("RA", [P, 15 * D])
        TA = sb("TA", [P, 6 * D])

        ident = sb("ident", [P, P])
        cols = sb("cols", [P, 8])
        iota16 = sb("iota16", [P, TOPK])
        rope = sb("rope", [P, 2, 4, 64])
        mask = sb("mask", [P, NH, P])
        hid = sb("hid", [64, NT])
        hidp = sb("peer_small", [P, 96])
        sml = sb("sml", [P, 256])

        wslot = [W[:, i * KD * 512:(i + 1) * KD * 512].rearrange("p (k n) -> p k n", k=KD) for i in range(NWSLOT)]

        def seg(area, lo, n, pat=None, **kw):
            v = area[:, lo:lo + n]
            return v.rearrange(pat, **kw) if pat else v

        silu_c = sml[:, 0:16]
        convc = sml[:, 16:64]
        bfcol = sml[0:64, 64:68]
        decay = sml[:, 68:76]
        lg = sml[:, 76:84]
        xi = sml[:, 84:92]
        zeta = sml[:, 92:100]
        chunkdec = sml[:, 100:108]
        ss1, var1, sd1, rs1 = (sml[:, 108 + 5 * i:113 + 5 * i] for i in range(4))
        sso, varo, sdo, rso = (sml[:, 128 + 4 * i:132 + 4 * i] for i in range(4))
        ssy, vary, sdy, rsy = (sml[:, 144 + 5 * i:149 + 5 * i] for i in range(4))
        ss2, var2, sd2, rs2 = (sml[:, 164 + 5 * i:169 + 5 * i] for i in range(4))
        ssf, varf, sdf, rsf = (sml[:, 184 + 5 * i:189 + 5 * i] for i in range(4))

        feat = TA[0:33, 0:NT]
        arg = TA[0:64, NT:2 * NT]
        turns = TA[0:64, 2 * NT:3 * NT]
        ef = seg(TA, 2048, 512, "p (h n) -> p h n", h=NH)
        eb = seg(TA, 2560, 512, "p (h n) -> p h n", h=NH)
        dist = seg(TA, 4096, 512, "p (a n) -> p a n", a=4)
        wf1 = TA[0:33, 4608:4672]
        wf2 = TA[0:64, 4672:4736]
        wf3 = TA[0:64, 4736:4800]
        condrows = TA[0:16, 4800:4928]
        convrows = TA[0:48, 4928:5056]
        modrow = RA[0:2, 0:6 * D]
        bada = RA[0:2, 6 * D:12 * D]
        grow = RA[0:2, 12 * D:14 * D]
        mod1 = [(seg(DA, 2 * c * D, D), seg(DA, (2 * c + 1) * D, D)) for c in range(2)]
        hbuf = [seg(TA, 0, D), seg(TA, D, D)]
        ropt1 = seg(TA, 2048, 512, "p (h a c) -> p h a c", h=NH, a=2)
        ropt2 = seg(TA, 2560, 512, "p (h a c) -> p h a c", h=NH, a=2)
        junk1 = seg(TA, 3072, D)
        hT = seg(HA, 0, NB * D, "p (k t) -> p k t", k=KD)
        qT = seg(RA, 0, 2560, "p (h t) -> p h t", h=NH)
        kT = seg(RA, 2560, 2560, "p (h t) -> p h t", h=NH)
        kt = seg(RA, 5120, 2560, "p (b n) -> p b n", b=NB)
        vt = seg(RA, 7680, 2560, "p (b n) -> p b n", b=NB)
        gg = seg(RA, 10240, 2560, "p (b n) -> p b n", b=NB)
        qt = seg(RA, 12800, 2560, "p (b n) -> p b n", b=NB)
        yret = qt
        retg = seg(TA, 4096, 512)
        Sf = [seg(TA, i * 512, 512) for i in range(4)]
        Sb = [seg(TA, (4 + i) * 512, 512) for i in range(4)]
        kz = [seg(TA, 4096, 512), seg(TA, 4608, 512)]
        stout = seg(TA, 5120, 1024, "p (a n) -> p a n", a=2)
        sm = [seg(DA, 0, 512), seg(DA, 512, 512)]
        ob = [seg(DA, 1024, 512), seg(DA, 1536, 512)]
        junko = seg(DA, 2048, 512)
        uT = [seg(TA, i * NT, NT) for i in range(3)]
        U = seg(RA, 0, 7680, "p (b j n) -> p b j n", b=NB, j=3)
        XF = X[:, :, :].rearrange("p b d -> p (b d)")
        window = seg(XF, 0, NB * HY, "p (b n) -> p b n", b=NB)
        w4 = XF[0:64, NB * HY:NB * HY + 4 * HY]
        dftc = seg(XF, 4608, 3 * P, "p (m t n) -> p m t n", m=3, t=1)
        dftl = seg(DA, 0, 6 * D, "p (m t n) -> p m t n", m=3, t=4)
        Ps = [seg(TA, 0, 512), seg(TA, 512, 512)]
        Qs = [seg(TA, 1024, 512), seg(TA, 1536, 512)]
        Pn = seg(TA, 2048, 512)
        tt4 = [seg(TA, 2560 + 512 * i, 512) for i in range(4)]
        fbias = TA[0:1, 4608:4608 + 2 * HY]
        he = seg(RA, 7680, 2048, "p (t n) -> p t n", t=4)
        ho = seg(RA, 9728, 2048, "p (t n) -> p t n", t=4)
        Rr = seg(HA, 0, 2048, "p (t n) -> p t n", t=4)
        Ri = seg(HA, 2048, 2048, "p (t n) -> p t n", t=4)
        mod2 = [(seg(DA, 3 * c * D, D), seg(DA, (3 * c + 1) * D, D), seg(DA, (3 * c + 2) * D, D)) for c in range(2)]
        yT = [seg(TA, i * D, D, "p (k t) -> p k t", k=KD) for i in range(2)]
        junk2 = seg(TA, 2048, D)
        hyg = seg(TA, 3072, 512)
        gy = [seg(TA, 3584, 512), seg(TA, 4096, 512)]
        H2 = seg(HA, 0, NB * D, "p (b d) -> p b d", b=NB)
        h2T = seg(RA, 7680, 5120, "p (k t) -> p k t", k=KD)
        keyraw = seg(HA, D, 2048, "p (i d) -> p i d", i=NQ)
        keysT = [seg(RA, lo, 1024, "p (i n) -> p i n", i=8) for lo in (2048, 3584)]
        qTp = seg(HA, 3 * D, 2048, "p (i t) -> p i t", i=NQ)
        scp = seg(DA, 0, 2048, "p (h a n) -> p h a n", h=PH, a=2)
        qTl = [seg(TA, D + i * NLAT, NLAT) for i in range(2)]
        sc = [seg(DA, i * D, D, "p (b a n) -> p b a n", b=NL, a=2) for i in range(2)]
        topv = seg(TA, 4608, 128, "p (q a k) -> p q a k", q=4, a=2)
        topi = seg(TA, 4736, 128, "p (q a k) -> p q a k", q=4, a=2).bitcast(U32)
        topif = seg(TA, 4864, 128, "p (q a k) -> p q a k", q=4, a=2)
        pairv = seg(TA, 4992, 64, "p (q k) -> p q k", q=4)
        pairp = seg(TA, 5056, 64).bitcast(U32)
        posa = seg(TA, 5120, 64).bitcast(U32)
        posb = seg(TA, 5184, 64).bitcast(U32)
        posaf = seg(TA, 5248, 64)
        posbf = seg(TA, 5312, 64)
        sel1 = seg(TA, 5376, 64)
        sel2 = seg(TA, 5440, 64)
        gsum = seg(TA, 5504, 32)
        grec = seg(TA, 5536, 32)
        cand = seg(DA, 2 * D, D, "p (q i j) -> p q i j", q=4, i=16)
        onehot = seg(RA, 5120, D)
        pdots = seg(TA, 5568, P)
        pgelu = seg(TA, 5568 + P, P)
        pwgt = seg(TA, 5568 + 2 * P, P)
        pu = [seg(RA, 0, D), seg(RA, D, D), seg(RA, 6144, D), seg(RA, 14080, D)]
        pv = [seg(DA, 3 * D, D), seg(DA, 5 * D, D), seg(TA, 2 * D, D), seg(TA, 3 * D, D)]
        IDXP = seg(RA, 12800, P, "p (h k) -> p h k", h=PH).bitcast(U32)
        GATEP = seg(RA, 12928, P, "p (h k) -> p h k", h=PH)
        IDX = seg(RA, 13056, 512, "p (b h k) -> p b h k", b=NL, h=PH).bitcast(U32)
        GATE = seg(RA, 13568, 512, "p (b h k) -> p b h k", b=NL, h=PH)
        uslot = [seg(W, i * D, D) for i in range(USLOTS)]
        vslot = [seg(W, (USLOTS + i) * D, D) for i in range(4)] + [seg(RA, 7680 + i * D, D) for i in range(4)]
        moe = seg(TA, 0, NB * D, "p (b d) -> p b d", b=NB)
        h2cur = seg(TA, 5120, D)
        gt2 = [seg(DA, 0, D), seg(DA, D, D)]
        fing = seg(DA, 2 * D, D)
        junku = [seg(DA, 3 * D, D), seg(DA, 5 * D, D)]
        diag = [seg(DA, 4096 + i * P, P) for i in range(DSLOTS)]
        zero = seg(DA, 4608, 512)
        dots = [seg(sml, 210, TOPK), seg(sml, 226, TOPK)]
        gelu = [seg(hidp, 16 * i, TOPK) for i in range(2)]
        wgt = [seg(hidp, 32 + 16 * i, TOPK) for i in range(2)]
        idxc = [seg(hidp, 64 + 16 * i, TOPK).bitcast(U32) for i in range(2)]

        T_COND, T_CONV, T_MLP = 0, 1, 2
        T_MOD = T_MLP + 6
        T_HT = T_MOD + NADA
        T_QKVG = T_HT + 2 * NB
        T_QK = T_QKVG + 4 * NB
        T_KV = T_QK + 2 * NB
        KV = [(0, 0), (0, 1), (1, 0), (2, 0), (3, 0), (4, 1), (3, 1), (2, 1)]
        T_RET = T_KV + len(KV)

        def t_score(b):
            return T_RET + (0 if b == 0 else 2 + 4 * (b - 1))

        def t_cross(b, d):
            return t_score(b) + 1 + d

        def t_intra(b):
            return t_score(b) + (1 if b == 0 else 3)

        T_HY = T_RET + 2 + 4 * 4

        def t_proj(i, part):
            return T_HY + (0 if i == 0 else 4 * i - 2) + part

        def t_uback(i, part):
            return T_HY + (4 * i + 4 if i < 11 else 46) + part

        T_CONVL = T_HY + 48
        SEGS = [(0, 1), (1, 4)]

        def conv_base(s, o):
            return T_CONVL + (o * 8 if s == 0 else 16 + o * 29)

        def t_filt(s, o, t, d):
            return conv_base(s, o) + 2 * t + d

        def t_freq(s, o, f, j):
            return conv_base(s, o) + 2 * SEGS[s][1] + (j if f == 0 else 1 + 4 * f + j)

        def t_inv(s, o, t):
            return conv_base(s, o) + 6 * SEGS[s][1] + 1 + t

        T_OUT = T_CONVL + 74

        def t_yT(b, j):
            return T_OUT + (0 if b == 0 else 18 if b == 1 else 6 * b + 10) + j

        def t_y(b, j):
            return t_yT(b, 0) + 2 + j

        T_KEYS = T_OUT + 4
        T_QP = T_KEYS + 6

        def t_h2T(b, j):
            return T_KEYS + 4 + j if b == 0 else t_yT(1, 0) + 6 * b - 2 + (4 if b < NL else 0) + j

        def t_qp(g):
            return T_QP + (0 if g == 0 else 2 * g - 1)

        def t_sp(g):
            return T_QP + (2 * g + 2 if g < 3 else 7)

        T_LAT = t_h2T(NL, 1) + 1

        def t_q(i):
            return T_LAT + (0 if i == 0 else 4 * i - 3)

        def t_s(i):
            return T_LAT + (4 * i + 2 if i < NQ - 1 else 4 * i + 1)

        def t_pv(i, j):
            return t_s(i) + 1 + j

        T_PEER = T_LAT + 4 * NQ

        bank_filled = [sem(f"bank_filled{i}") for i in range(8)]
        bank_freed = [sem(f"bank_freed{i}") for i in range(8)]

        def free_bank(pe, t):
            if t >= 8:
                pe.wait_ge(bank_freed[t % 8], t // 8)
            return bank[t % 8]

        def filled(eng, t):
            eng.wait_ge(bank_filled[t % 8], t // 8 + 1)
            return bank[t % 8]

        def readout(eng, t):
            eng.wait_ge(bank_freed[t % 8], t // 8 + 1)

        names = """c_loaded conv_loaded mlp_loaded const_loaded decay_loaded ada_bias_loaded x_loaded x_again
            arg_ready sin_done lg_ready decays_ready masks_ready mod_ready mod_stored mod1_loaded retg_loaded
            ss1_ready var1_ready sd1_ready h_ready rope_ready gate_ready state_loaded kz_ready state_ready
            stout_ready o_ready sso_ready varo_ready sdo_ready yret_ready conv_center dft_loaded filt_loaded
            bias_loaded filt_ready ps_scaled spectrum_ready z_ready mod2_loaded hyg_loaded ssy_ready vary_ready sdy_ready
            yhy_ready x1_ready ss2_ready var2_ready sd2_ready h2_ready keys_loaded scores_out topk_done pair_ready exp_done
            gates_ready mod3_loaded weights_used idx_ready gelu_ready wgt_ready diag_ready acc_filled acc_free
            vrow_used urow_used pool_go zero_ready ssf_ready varf_ready sdf_ready y_ready stored states_stored dve_chain act_chain
            norm2_started prompt_topk prompt_pairs prompt_exp prompt_gates pu_used pv_used pgelu_ready pwgt_ready
            pdiag_ready psum_ready""".split()
        s = {n: sem(n) for n in names}
        w_full = [sem(f"w_full{i}") for i in range(NWSLOT)]
        pu_full = [sem(f"prompt_urow_full{i}") for i in range(PSLOTS)]
        pv_full = [sem(f"prompt_vrow_full{i}") for i in range(PSLOTS)]
        urow_full = [sem(f"urow_full{i}") for i in range(USLOTS)]
        vrow_full = [sem(f"vrow_full{i}") for i in range(VSLOTS)]

        wtiles = [(io["w_ada"], n * 512) for n in range(NADA)]
        W_QKVG = len(wtiles)
        wtiles += [(io["w_in"], 3 * HY + n * 512) for n in range(4)]
        W_HY = len(wtiles)
        wtiles += [(io["w_in"], n * 512) for n in range(3)]
        W_OUT = len(wtiles)
        wtiles += [(io["w_out"], n * 512) for n in range(2)]
        W_QP = len(wtiles)
        wtiles += [(io["peer_wq"], n * 512) for n in range(4)]
        W_OUTL = len(wtiles)
        wtiles += [(io["w_out"], n * 512) for n in range(2)]
        W_Q = len(wtiles)
        wtiles += [(io["peer_wq"], n * 512) for n in range(4)]

        def weight(pe, n):
            pe.wait_ge(w_full[n % NWSLOT], 16 * (n // NWSLOT + 1))
            return wslot[n % NWSLOT]

        block = ctx.enter_context(nc.Block())

        @block.sync
        def _(sp):
            sp.dma_start(condrows, io["conds"]).then_inc(s["c_loaded"], 16)
            sp.dma_start(ident[:, :], io["ident"]).then_inc(s["c_loaded"], 16)
            for i in range(NWSLOT):
                src, lo = wtiles[i]
                sp.dma_start(wslot[i], src[:, lo:lo + 512].rearrange("(k p) n -> p k n", p=P)).then_inc(w_full[i], 16)
            for n in range(NWSLOT, len(wtiles)):
                src, lo = wtiles[n]
                sp.wait_ge(s["weights_used"], n - NWSLOT + 1)
                sp.dma_start(wslot[n % NWSLOT], src[:, lo:lo + 512].rearrange("(k p) n -> p k n", p=P)).then_inc(
                    w_full[n % NWSLOT], 16)
            sp.wait_ge(s["topk_done"], PH)
            for c in range(2):
                sp.dma_start(gt2[c], io["mod_scratch"][c:c + 1, 5 * D:6 * D].to_broadcast([P, D])).then_inc(s["mod3_loaded"], 16)
            sp.dma_start(fing, io["final_g"].to_broadcast([P, D])).then_inc(s["mod3_loaded"], 16)
            for b in range(NB):
                sp.wait_ge(s["y_ready"], b + 1)
                dst = io["y_prompt"] if b == 0 else io["y_sample"][(b - 1) * P:b * P, :]
                sp.dma_start(dst, moe[:, b, :]).then_inc(s["stored"], 16)
            sp.wait_ge(s["stored"], 16 * NB)

        @block.gpsimd
        def _(g):
            g.dma_start(convrows, io["conv_rows"]).then_inc(s["conv_loaded"], 16)
            for dst, name in ((feat, "feat_t"), (wf1, "hy_w1"), (wf2, "hy_w2"), (wf3, "hy_w3")):
                g.dma_start(dst, io[name]).then_inc(s["mlp_loaded"], 16)
            for j, name in enumerate(("hy_b1", "hy_b2", "hy_b3", "hy_freq")):
                g.dma_start(bfcol[:, j:j + 1], io[name]).then_inc(s["mlp_loaded"], 16)
            g.dma_start(dist, io["dist"].rearrange("p (a n) -> p a n", a=4)).then_inc(s["decay_loaded"], 16)
            g.dma_start(cols[:, :], io["cols"]).then_inc(s["decay_loaded"], 16)
            g.dma_start(decay[:, 0:4], io["ret_decay_fwd"].to_broadcast([P, NH])).then_inc(s["decay_loaded"], 16)
            g.dma_start(decay[:, 4:8], io["ret_decay_bwd"].to_broadcast([P, NH])).then_inc(s["decay_loaded"], 16)
            g.dma_start(bada, io["b_ada"].to_broadcast([2, 6 * D])).then_inc(s["ada_bias_loaded"], 16)
            g.dma_start(grow[:, 0:D], io["norm1_g"].to_broadcast([2, D])).then_inc(s["ada_bias_loaded"], 16)
            g.dma_start(grow[:, D:2 * D], io["norm2_g"].to_broadcast([2, D])).then_inc(s["ada_bias_loaded"], 16)
            g.dma_start(X[:, 0, :], io["x_prompt"]).then_inc(s["x_loaded"], 16)
            g.dma_start(X[:, 1:NB, :], io["x_sample"].rearrange("(b p) d -> p b d", p=P)).then_inc(s["x_loaded"], 16)
            g.dma_start(rope[:, :, :, :], io["rope"].rearrange("p (a b c) -> p a b c", a=2, b=4)).then_inc(s["const_loaded"], 16)
            g.dma_start(iota16[:, :], io["iota16"]).then_inc(s["const_loaded"], 16)
            g.wait_ge(s["mod_ready"], 1)
            g.dma_start(io["mod_scratch"], modrow).then_inc(s["mod_stored"], 16)
            g.wait_ge(s["mod_stored"], 16)

            def spread(dst, c, j, done):
                g.dma_start(dst, io["mod_scratch"][c:c + 1, j * D:(j + 1) * D].to_broadcast([P, D])).then_inc(s[done], 16)

            for c in range(2):
                spread(mod1[c][0], c, 1, "mod1_loaded")
                spread(mod1[c][1], c, 0, "mod1_loaded")
            g.wait_ge(s["masks_ready"], 1)
            g.dma_start(retg, io["ret_norm_g"].to_broadcast([P, HY])).then_inc(s["retg_loaded"], 16)
            for b in range(NB):
                for j in range(2):
                    filled(g, T_HT + 2 * b + j)
            g.dma_start(Sf[0].rearrange("p (h e) -> p h e", h=NH), io["state_ret_fwd"]).then_inc(s["state_loaded"], 16)
            g.wait_ge(s["rope_ready"], 8)
            g.wait_ge(s["h_ready"], NB)
            g.dma_start(Sb[3].rearrange("p (h e) -> p h e", h=NH), io["state_ret_bwd"]).then_inc(s["state_loaded"], 16)
            g.dma_start(window, io["window"].rearrange("p (b n) -> p b n", b=NB)).then_inc(s["filt_loaded"], 16)
            g.dma_start(w4, io["hy_w4"]).then_inc(s["filt_loaded"], 16)
            g.dma_start(dftc, io["dft_ctx"].rearrange("p (m t n) -> p m t n", m=3, t=1)).then_inc(s["filt_loaded"], 16)
            g.wait_ge(s["stout_ready"], 2)
            for d, name in ((0, "new_fwd"), (1, "new_bwd")):
                g.dma_start(io[name], stout[:, d, :].rearrange("p (h e) -> p h e", h=NH)).then_inc(s["states_stored"], 16)
            g.wait_ge(s["yret_ready"], NB)
            g.dma_start(dftl, io["dft_lat"].rearrange("p (m t n) -> p m t n", m=3, t=4)).then_inc(s["dft_loaded"], 16)
            g.wait_ge(s["states_stored"], 32)
            g.dma_start(fbias, io["hy_bias"]).then_inc(s["bias_loaded"], 16)
            g.wait_ge(s["spectrum_ready"], 10)
            g.dma_start(hyg, io["hy_norm_g"].to_broadcast([P, HY])).then_inc(s["hyg_loaded"], 16)
            g.dma_start(X[:, 0, :], io["x_prompt"]).then_inc(s["x_again"], 16)
            g.dma_start(X[:, 1:NB, :], io["x_sample"].rearrange("(b p) d -> p b d", p=P)).then_inc(s["x_again"], 16)
            for t in range(4):
                filled(g, t_inv(1, 1, t))
            for i, j in enumerate((2, 4, 3)):
                spread(mod2[0][i], 0, j, "mod2_loaded")
            g.dma_start(keyraw, io["peer_keys"].rearrange("i n d -> n i d")).then_inc(s["keys_loaded"], 16)
            for i, j in enumerate((2, 4, 3)):
                spread(mod2[1][i], 1, j, "mod2_loaded")

            g.wait_ge(s["prompt_topk"], 2)
            g.wait_ge(s["h2_ready"], NB)
            for i in range(NQ + 1):
                for k in range(PSTEP):
                    if i < NQ:
                        n = i * PSTEP + k
                        if n >= PSLOTS:
                            g.wait_ge(s["pu_used"], n - PSLOTS + 1)
                        g.indirect_dma_start(out=pu[n % PSLOTS], out_offset=None, in_=io["peer_u"],
                                             in_offset=bass.IndirectOffsetOnAxis(ap=IDXP[:, n // TOPK, n % TOPK:n % TOPK + 1], axis=0)
                                             ).then_inc(pu_full[n % PSLOTS], 16)
                    if i >= 1:
                        n = (i - 1) * PSTEP + k
                        if n >= PSLOTS:
                            g.wait_ge(s["pv_used"], n - PSLOTS + 1)
                        g.indirect_dma_start(out=pv[n % PSLOTS], out_offset=None, in_=io["peer_v"],
                                             in_offset=bass.IndirectOffsetOnAxis(ap=IDXP[:, n // TOPK, n % TOPK:n % TOPK + 1], axis=0)
                                             ).then_inc(pv_full[n % PSLOTS], 16)

            g.wait_ge(s["weights_used"], len(wtiles))
            with g.Fori(0, NL) as b:
                with g.Fori(0, PH // 2) as hp:
                    for par in range(2):
                        chunk = b * PH + hp * 2 + par
                        g.wait_ge(s["idx_ready"], chunk + 1)
                        for k in range(TOPK):
                            g.wait_ge(s["urow_used"], chunk * TOPK + k + 1)
                            g.sem_inc(s["pool_go"], 1)
                            g.indirect_dma_start(out=uslot[k % USLOTS], out_offset=None, in_=io["peer_u"],
                                                 in_offset=bass.IndirectOffsetOnAxis(ap=idxc[par][:, k:k + 1], axis=0)
                                                 ).then_inc(urow_full[k % USLOTS], 16)
                        for k in range(TOPK):
                            g.wait_ge(s["vrow_used"], chunk * TOPK + TOPK + k + 1)
                            g.sem_inc(s["pool_go"], 1)
                            g.indirect_dma_start(out=vslot[k % VSLOTS], out_offset=None, in_=io["peer_v"],
                                                 in_offset=bass.IndirectOffsetOnAxis(ap=idxc[par][:, k:k + 1], axis=0)
                                                 ).then_inc(vrow_full[k % VSLOTS], 16)

        @block.scalar
        def _(act):
            A = nc.scalar

            def copy_out(t, out, src):
                A.copy(out, src).then_inc(bank_freed[t % 8], 1)

            chain = [0]

            def link(ins):
                chain[0] += 1
                ins.then_inc(s["act_chain"], 1)
                act.wait_ge(s["act_chain"], chain[0])

            ps = filled(act, T_COND)
            A.activation(silu_c, ps[:, 0:16], ACT.Silu).then_inc(bank_freed[T_COND % 8], 1)
            ps = filled(act, T_CONV)
            copy_out(T_CONV, convc, ps[:, 0:48])
            for layer in range(3):
                for i, (lo, n) in enumerate(((0, P), (P, NLAT))):
                    act.wait_ge(s["arg_ready"], 2 * layer + i + 1)
                    A.activation(hid[:, lo:lo + n], arg[:, lo:lo + n], ACT.Sin).then_inc(s["sin_done"], 1)
            act.wait_ge(s["decay_loaded"], 64)
            link(A.activation(decay, decay, ACT.Exp))
            act.wait_ge(s["lg_ready"], 1)
            for h in range(NH):
                A.activation(ef[:, h, :], dist[:, 0, :], ACT.Exp, scale=lg[:, h:h + 1])
                A.activation(eb[:, h, :], dist[:, 1, :], ACT.Exp, scale=lg[:, 4 + h:5 + h])
            A.activation(xi[:, 0:4], lg[:, 0:4], ACT.Exp, scale=cols[:, 0:1])
            A.activation(zeta[:, 0:4], lg[:, 0:4], ACT.Exp, scale=cols[:, 1:2])
            A.activation(xi[:, 4:8], lg[:, 4:8], ACT.Exp, scale=cols[:, 2:3])
            A.activation(zeta[:, 4:8], lg[:, 4:8], ACT.Exp, scale=cols[:, 3:4])
            A.activation(chunkdec, lg, ACT.Exp, scale=float(P)).then_inc(s["decays_ready"], 1)
            act.wait_ge(s["x_loaded"], 32)
            for b in range(NB):
                link(A.activation(junk1, X[:, b, :], ACT.Square, accum_out=ss1[:, b:b + 1]))
            act.sem_inc(s["ss1_ready"], 1)
            act.wait_ge(s["var1_ready"], 1)
            A.activation(sd1, var1, ACT.Sqrt).then_inc(s["sd1_ready"], 1)
            for b in range(NB):
                for j in range(2):
                    t = T_HT + 2 * b + j
                    ps = filled(act, t)
                    copy_out(t, hT[:, 4 * j:4 * j + 4, b * P:(b + 1) * P], ps[:, :].rearrange("p (k t) -> p k t", k=4))
            t = T_QKVG
            copy_out(t, qt[:, 0, :], filled(act, t)[:, :])
            t = T_QKVG + NB
            copy_out(t, kt[:, 0, :], filled(act, t)[:, :])
            for b in range(NB):
                t = T_QKVG + 2 * NB + b
                copy_out(t, vt[:, b, :], filled(act, t)[:, :])
            for b in range(NB):
                t = T_QKVG + 3 * NB + b
                ps = filled(act, t)
                A.activation(gg[:, b, :], ps[:, :], ACT.Silu).then_inc(bank_freed[t % 8], 1)
            for j, dst in enumerate((qT, kT)):
                for b in range(NB):
                    t = T_QK + j * NB + b
                    ps = filled(act, t)
                    copy_out(t, dst[:, :, b * P:(b + 1) * P], ps[:, :].rearrange("p (h t) -> p h t", h=NH))
            for b in range(NB):
                if b >= 2:
                    act.wait_ge(s["yret_ready"], b - 1)
                copy_out(t_intra(b), ob[b % 2], filled(act, t_intra(b))[:, :])
                act.wait_ge(s["o_ready"], b + 1)
                for h in range(NH):
                    ins = A.activation(junko[:, h * P:(h + 1) * P], ob[b % 2][:, h * P:(h + 1) * P], ACT.Square,
                                       accum_out=sso[:, h:h + 1])
                ins.then_inc(s["sso_ready"], 1)
                act.wait_ge(s["varo_ready"], b + 1)
                A.activation(sdo, varo, ACT.Sqrt).then_inc(s["sdo_ready"], 1)
            def rows_out(i):
                for part in range(2):
                    t = t_uback(i, part)
                    ps = filled(act, t)
                    j, c = i // 4, (i % 4) * P
                    if part == 0:
                        copy_out(t, U[:, 1:NB, j, c:c + P], ps[:, :].rearrange("p (b n) -> p b n", b=4))
                    else:
                        copy_out(t, U[:, 0, j, c:c + P], ps[:, 0:P])

            act.wait_ge(s["stout_ready"], 2)
            act.wait_ge(s["yret_ready"], NB)
            for i in range(12):
                if i >= 3:
                    filled(act, t_uback(i - 3, 1))
                for part, lo, n in ((0, P, NLAT), (1, 0, P)):
                    ps = filled(act, t_proj(i, part))
                    A.activation(uT[i % 3][:, lo:lo + n], ps[:, 0:n], ACT.Identity, bias=convc[:, 36 + i:37 + i],
                                 scale=convc[:, 12 + i:13 + i]).then_inc(s["conv_center"], 1)
                if i >= 1:
                    rows_out(i - 1)
            rows_out(11)
            n_freq = 0
            for sg, (b0, nt) in enumerate(SEGS):
                cp, cq = (cols[:, 4 + 2 * sg:5 + 2 * sg], cols[:, 5 + 2 * sg:6 + 2 * sg])
                wgt2 = 2.0 / (2 * nt * P)
                for o in range(2):
                    for f in range(nt):
                        if n_freq >= 2:
                            act.wait_ge(s["spectrum_ready"], n_freq - 1)
                        if f == 0 and n_freq >= 1:
                            act.wait_ge(s["spectrum_ready"], n_freq)
                        i = n_freq % 2
                        ps = filled(act, t_freq(sg, o, f, 0))
                        if f == 0:
                            link(A.activation(Pn, ps[:, :], ACT.Copy, scale=cp))
                        A.activation(Ps[i], ps[:, :], ACT.Copy, scale=cp if f == 0 else wgt2).then_inc(
                            bank_freed[t_freq(sg, o, f, 0) % 8], 1)
                        ps = filled(act, t_freq(sg, o, f, 1))
                        A.activation(Qs[i], ps[:, :], ACT.Copy, scale=cq if f == 0 else wgt2).then_inc(
                            bank_freed[t_freq(sg, o, f, 1) % 8], 1)
                        if f == 0:
                            t = t_freq(sg, o, 0, 4)
                            ps = filled(act, t)
                            A.activation(Pn[0:1, :], ps[0:1, :], ACT.Copy, scale=0.5 * wgt2).then_inc(bank_freed[t % 8], 1)
                        n_freq += 1
            act.wait_ge(s["z_ready"], 10)
            for b in range(NB):
                link(A.activation(junk2[:, 0:512], U[:, b, 0, :], ACT.Square, accum_out=ssy[:, b:b + 1]))
            act.sem_inc(s["ssy_ready"], 1)
            act.wait_ge(s["vary_ready"], 1)
            A.activation(sdy, vary, ACT.Sqrt).then_inc(s["sdy_ready"], 1)

            def h2T_out(b):
                for j in range(2):
                    t = t_h2T(b, j)
                    ps = filled(act, t)
                    copy_out(t, h2T[:, 4 * j:4 * j + 4, b * P:(b + 1) * P], ps[:, :].rearrange("p (k t) -> p k t", k=4))

            def out_block(b):
                for j in range(2):
                    t = t_yT(b, j)
                    if b >= 2:
                        filled(act, t_y(b - 2, 1))
                    ps = filled(act, t)
                    copy_out(t, yT[b % 2][:, 4 * j:4 * j + 4, :], ps[:, :].rearrange("p (k t) -> p k t", k=4))
                act.wait_ge(s["x1_ready"], b + 1)
                A.activation(junk2, X[:, b, :], ACT.Square, accum_out=ss2[:, b:b + 1]).then_inc(s["ss2_ready"], 1)
                act.wait_ge(s["var2_ready"], b + 1)
                A.activation(sd2[:, b:b + 1], var2[:, b:b + 1], ACT.Sqrt).then_inc(s["sd2_ready"], 1)

            out_block(0)
            for i in range(4):
                t = T_KEYS + i
                copy_out(t, keysT[i // 2][:, 4 * (i % 2):4 * (i % 2) + 4, :],
                         filled(act, t)[:, :].rearrange("p (i n) -> p i n", i=4))
            h2T_out(0)

            def prompt_scores_out(g):
                ps = filled(act, t_sp(g))
                copy_out(t_sp(g), scp[:, 2 * g:2 * g + 2, :, :], ps[:, :].rearrange("p (h a n) -> p h a n", h=2, a=2))

            for g in range(4):
                ps = filled(act, t_qp(g))
                copy_out(t_qp(g), qTp[:, 4 * g:4 * g + 4, :], ps[:, :].rearrange("p (i t) -> p i t", i=4))
                if g >= 1:
                    prompt_scores_out(g - 1)
            prompt_scores_out(3)
            for b in range(1, NB):
                out_block(b)
                if b >= 2:
                    h2T_out(b - 1)
                if b == 2:
                    act.wait_ge(s["prompt_pairs"], 2)
                    A.activation(GATEP, GATEP, ACT.Exp).then_inc(s["prompt_exp"], 1)
            h2T_out(NL)

            act.wait_ge(s["h2_ready"], NB)
            for i in range(NQ + 1):
                for k in range(PSTEP):
                    if i == 0:
                        continue
                    n = (i - 1) * PSTEP + k
                    if k == 0:
                        act.wait_ge(s["pwgt_ready"], i)
                    if n >= DSLOTS:
                        act.wait_ge(s["pv_used"], n - DSLOTS + 1)
                    A.activation(diag[n % DSLOTS], ident[:, :], ACT.Copy, scale=pwgt[:, n:n + 1]).then_inc(s["pdiag_ready"], 1)
                    if k == 2:
                        hd, half = (i - 1) // 2, (i - 1) % 2
                        if half == 0 and hd >= 2:
                            act.wait_ge(s["topk_done"], hd - 1)
                        copy_out(t_s(i - 1), sc[hd % 2][:, :, half, :],
                                 filled(act, t_s(i - 1))[:, :].rearrange("p (b n) -> p b n", b=NL))
                if i < NQ:
                    copy_out(t_q(i), qTl[i % 2], filled(act, t_q(i))[:, :])
                    act.wait_ge(s["pu_used"], (i + 1) * PSTEP)
                    c = slice(i * PSTEP, (i + 1) * PSTEP)
                    A.activation(pgelu[:, c], pdots[:, c], ACT.Gelu_apprx_tanh).then_inc(s["pgelu_ready"], 1)
            act.wait_ge(s["pair_ready"], PH)
            gflat = GATE[:, :, :, :].rearrange("p b h k -> p (b h k)")
            A.activation(gflat, gflat, ACT.Exp).then_inc(s["exp_done"], 1)

            act.wait_ge(s["zero_ready"], 1)
            with act.Fori(0, NL) as b:
                with act.Fori(0, PH // 2) as hp:
                    for par in range(2):
                        chunk = b * PH + hp * 2 + par
                        act.wait_ge(s["urow_used"], chunk * TOPK + USLOTS + TOPK)
                        A.activation(gelu[par], dots[par], ACT.Gelu_apprx_tanh).then_inc(s["gelu_ready"], 1)
                        act.wait_ge(s["wgt_ready"], chunk + 1)
                        for k in range(TOPK):
                            act.wait_ge(s["vrow_used"], chunk * TOPK + TOPK + k + 1 + VSLOTS - DSLOTS)
                            A.activation(diag[k % DSLOTS], ident[:, :], ACT.Copy, scale=wgt[par][:, k:k + 1]).then_inc(
                                s["diag_ready"], 1)
                act.wait_ge(s["acc_filled"], b + 1)
                act.sem_inc(s["act_chain"], 1)
                for j in range(2):
                    ins = A.copy(moe[:, bass.ds(b + 1, 1), j * 512:(j + 1) * 512], bank[j][:, :].unsqueeze(1))
                ins.then_inc(s["acc_free"], 1)
            for b in range(NB):
                act.wait_ge(s["norm2_started"], b + 1)
                A.activation(junku[b % 2], X[:, b, :], ACT.Square, accum_out=ssf[:, b:b + 1]).then_inc(s["ssf_ready"], 1)
                act.wait_ge(s["varf_ready"], b + 1)
                A.activation(sdf[:, b:b + 1], varf[:, b:b + 1], ACT.Sqrt).then_inc(s["sdf_ready"], 1)

        @block.vector
        def _(dve):
            V = nc.vector
            chain = [0]

            def link(ins):
                chain[0] += 1
                ins.then_inc(s["dve_chain"], 1)
                dve.wait_ge(s["dve_chain"], chain[0])

            def frees(ins, t):
                ins.then_inc(bank_freed[t % 8], 1)

            def inverse_root(ss, var, sd, rs, n, got, said, sd_done, count):
                dve.wait_ge(s[got], count)
                V.tensor_scalar(var, ss, 1.0 / n, EPS, ALU.mult, ALU.add).then_inc(s[said], 1)
                dve.wait_ge(s[sd_done], count)
                link(V.reciprocal(rs, sd))

            for layer in range(3):
                for i, (lo, n) in enumerate(((0, P), (P, NLAT))):
                    t = T_MLP + 2 * layer + i
                    if t == T_MLP:
                        dve.wait_ge(s["mlp_loaded"], 128)
                    ps = filled(dve, t)
                    a, k = arg[:, lo:lo + n], turns[:, lo:lo + n]
                    frees(V.tensor_scalar(a, ps[0:64, 0:n], bfcol[:, layer:layer + 1], bfcol[:, 3:4], ALU.add, ALU.mult), t)
                    readout(dve, t)
                    link(V.tensor_scalar(k, a, 1.0 / (2.0 * math.pi), MAGIC, ALU.mult, ALU.add))
                    link(V.tensor_scalar(k, k, MAGIC, None, ALU.subtract))
                    for part in TWO_PI_PARTS:
                        link(V.scalar_tensor_tensor(a, k, -part, a, ALU.mult, ALU.add))
                    V.tensor_scalar(a, a, PI_SAFE, -PI_SAFE, ALU.min, ALU.max).then_inc(s["arg_ready"], 1)
            dve.wait_ge(s["act_chain"], 1)
            V.tensor_scalar(lg, decay, -1.0, None, ALU.mult).then_inc(s["lg_ready"], 1)
            dve.wait_ge(s["decays_ready"], 1)
            V.tensor_tensor(ef, ef, dist[:, 2, :].unsqueeze(1).to_broadcast([P, NH, P]), ALU.mult)
            V.tensor_scalar(zeta, zeta, P ** -0.5, None, ALU.mult)
            link(V.tensor_tensor(eb, eb, dist[:, 3, :].unsqueeze(1).to_broadcast([P, NH, P]), ALU.mult))
            link(V.tensor_tensor(mask[:, :, :], ef, eb, ALU.add))
            V.tensor_scalar(mask[:, :, :], mask[:, :, :], P ** -0.5, None, ALU.mult).then_inc(s["masks_ready"], 1)
            dve.wait_ge(s["ada_bias_loaded"], 48)
            for n in range(NADA):
                ps = filled(dve, T_MOD + n)
                frees(V.tensor_tensor(modrow[:, n * 512:(n + 1) * 512], ps[0:2, :], bada[:, n * 512:(n + 1) * 512], ALU.add),
                      T_MOD + n)
            for n in range(NADA):
                readout(dve, T_MOD + n)
            m = modrow[:, D:2 * D]
            link(V.scalar_tensor_tensor(m, m, 1.0, grow[:, 0:D], ALU.add, ALU.mult))
            m = modrow[:, 4 * D:5 * D]
            V.scalar_tensor_tensor(m, m, 1.0, grow[:, D:2 * D], ALU.add, ALU.mult).then_inc(s["mod_ready"], 1)
            inverse_root(ss1, var1, sd1, rs1, D, "ss1_ready", "var1_ready", "sd1_ready", 1)
            dve.wait_ge(s["mod1_loaded"], 64)
            for b in range(NB):
                scale, shift = mod1[min(b, 1)]
                if b >= 2:
                    filled(dve, T_HT + 2 * (b - 2) + 1)
                link(V.scalar_tensor_tensor(hbuf[b % 2], X[:, b, :], rs1[:, b:b + 1], scale, ALU.mult, ALU.mult))
                V.tensor_tensor(hbuf[b % 2], hbuf[b % 2], shift, ALU.add).then_inc(s["h_ready"], 1)
            dve.wait_ge(s["const_loaded"], 32)
            for j, dst in enumerate((qt, kt)):
                for b in range(1, NB):
                    t = T_QKVG + j * NB + b
                    ps = filled(dve, t)[:, :].rearrange("p (h a c) -> p h a c", h=NH, a=2)
                    out = dst[:, b, :].rearrange("p (h a c) -> p h a c", h=NH, a=2)
                    cos = rope[:, 0, b - 1, :].unsqueeze(1).to_broadcast([P, NH, 64])
                    sin = rope[:, 1, b - 1, :].unsqueeze(1).to_broadcast([P, NH, 64])
                    for a in range(2):
                        V.tensor_tensor(ropt1[:, :, a, :], ps[:, :, a, :], cos, ALU.mult)
                    V.tensor_tensor(ropt2[:, :, 0, :], ps[:, :, 1, :], sin, ALU.mult)
                    frees(V.tensor_tensor(ropt2[:, :, 1, :], ps[:, :, 0, :], sin, ALU.mult), t)
                    readout(dve, t)
                    V.tensor_tensor(out[:, :, 0, :], ropt1[:, :, 0, :], ropt2[:, :, 0, :], ALU.subtract)
                    V.tensor_tensor(out[:, :, 1, :], ropt1[:, :, 1, :], ropt2[:, :, 1, :], ALU.add).then_inc(s["rope_ready"], 1)
                    dve.wait_ge(s["rope_ready"], 4 * j + b)
            dve.wait_ge(s["retg_loaded"], 16)
            for b in range(NB):
                readout(dve, T_QKVG + 3 * NB + b)
                V.tensor_tensor(gg[:, b, :], gg[:, b, :], retg, ALU.mult).then_inc(s["gate_ready"], 1)
            dve.wait_ge(s["gate_ready"], NB)
            dve.wait_ge(s["rope_ready"], 8)
            dve.wait_ge(s["state_loaded"], 32)
            readout(dve, T_QKVG + NB)

            def state(i):
                b, d = KV[i]
                t = T_KV + i
                ps = filled(dve, t)
                if b == 0:
                    V.tensor_copy(stout[:, d, :], ps[:, :]).then_inc(s["stout_ready"], 1)
                    dve.wait_ge(s["stout_ready"], i + 1)
                    dve.sem_inc(bank_freed[t % 8], 1)
                    return
                old, new = (Sf[b - 1], Sf[b]) if d == 0 else (Sb[b - 1], Sb[b - 2])
                for h in range(NH):
                    c = slice(h * P, (h + 1) * P)
                    ins = V.scalar_tensor_tensor(new[:, c], old[:, c], chunkdec[:, 4 * d + h:4 * d + h + 1], ps[:, c],
                                                 ALU.mult, ALU.add)
                frees(ins, t)
                readout(dve, t)

            for i, (b, d) in enumerate(KV):
                if i >= 2:
                    filled(dve, T_KV + i - 2)
                V.tensor_tensor(kz[i % 2].rearrange("p (h e) -> p h e", h=NH), kt[:, b, :].rearrange("p (h e) -> p h e", h=NH),
                                zeta[:, 4 * d:4 * d + 4].unsqueeze(2).to_broadcast([P, NH, P]), ALU.mult).then_inc(s["kz_ready"], 1)
                if i >= 1:
                    state(i - 1)
            state(len(KV) - 1)
            for b in range(NB):
                t = t_score(b)
                if b >= 2:
                    filled(dve, t_intra(b - 2))
                frees(V.tensor_tensor(sm[b % 2], filled(dve, t)[:, :], mask[:, :, :].rearrange("p h n -> p (h n)"), ALU.mult), t)
                o = ob[b % 2]
                readout(dve, t_intra(b))
                if b == 0:
                    dve.sem_inc(s["o_ready"], 1)
                else:
                    for d in range(2):
                        t = t_cross(b, d)
                        ps = filled(dve, t)
                        for h in range(NH):
                            c = slice(h * P, (h + 1) * P)
                            ins = V.scalar_tensor_tensor(o[:, c], ps[:, c], xi[:, 4 * d + h:4 * d + h + 1], o[:, c], ALU.mult, ALU.add)
                        frees(ins, t)
                        readout(dve, t)
                    dve.sem_inc(s["o_ready"], 1)
                inverse_root(sso, varo, sdo, rso, P, "sso_ready", "varo_ready", "sdo_ready", b + 1)
                for h in range(NH):
                    c = slice(h * P, (h + 1) * P)
                    ins = V.scalar_tensor_tensor(yret[:, b, c], o[:, c], rso[:, h:h + 1], gg[:, b, c], ALU.mult, ALU.mult)
                ins.then_inc(s["yret_ready"], 1)
            for i in range(12):
                u = uT[i % 3]
                w0, w2 = convc[:, i:i + 1], convc[:, 24 + i:25 + i]
                dve.wait_ge(s["conv_center"], 2 * i + 2)
                pl, pc = filled(dve, t_proj(i, 0)), filled(dve, t_proj(i, 1))
                V.scalar_tensor_tensor(u[:, P + 1:NT], pl[:, 0:NLAT - 1], w0, u[:, P + 1:NT], ALU.mult, ALU.add)
                link(V.scalar_tensor_tensor(u[:, 1:P], pc[:, 0:P - 1], w0, u[:, 1:P], ALU.mult, ALU.add))
                frees(V.scalar_tensor_tensor(u[:, P:NT - 1], pl[:, 1:NLAT], w2, u[:, P:NT - 1], ALU.mult, ALU.add), t_proj(i, 0))
                frees(V.scalar_tensor_tensor(u[:, 0:P - 1], pc[:, 1:P], w2, u[:, 0:P - 1], ALU.mult, ALU.add), t_proj(i, 1))
            dve.wait_ge(s["filt_loaded"], 48)
            dve.wait_ge(s["bias_loaded"], 16)
            for i in range(12):
                for part in range(2):
                    readout(dve, t_uback(i, part))
            n_freq = n_filt = 0
            for sg, (b0, nt) in enumerate(SEGS):
                for o in range(2):
                    for t in range(nt):
                        hf, hb = tt4[2 * (t % 2)], tt4[2 * (t % 2) + 1]
                        tf, tb = t_filt(sg, o, t, 0), t_filt(sg, o, t, 1)
                        if n_filt >= 2:
                            dve.wait_ge(s["filt_ready"], n_filt - 1)
                        n_filt += 1
                        frees(V.tensor_tensor(hf, filled(dve, tf)[:, :], window[:, b0 + t, :], ALU.mult), tf)
                        frees(V.tensor_tensor(hb, filled(dve, tb)[:, :], window[:, b0 + t, :], ALU.mult), tb)
                        readout(dve, tf)
                        readout(dve, tb)
                        if t == 0:
                            V.tensor_tensor(hf[0:1, :], hf[0:1, :], fbias[:, o * HY:(o + 1) * HY], ALU.add)
                            link(V.memset(hb[0:1, :], 0.0))
                        V.tensor_tensor(he[:, t, :], hf, hb, ALU.add)
                        V.tensor_tensor(ho[:, t, :], hf, hb, ALU.subtract).then_inc(s["filt_ready"], 1)
                    for f in range(nt):
                        i = n_freq % 2
                        readout(dve, t_freq(sg, o, f, 0))
                        readout(dve, t_freq(sg, o, f, 1))
                        if f == 0:
                            readout(dve, t_freq(sg, o, 0, 4))
                        if f == 0:
                            dve.wait_ge(s["filt_ready"], n_filt)
                        else:
                            dve.wait_ge(s["spectrum_ready"], n_freq)
                        a, bb = filled(dve, t_freq(sg, o, f, 2)), filled(dve, t_freq(sg, o, f, 3))
                        V.tensor_tensor(tt4[0], a[:, :], Ps[i], ALU.mult)
                        V.tensor_tensor(tt4[1], bb[:, :], Qs[i], ALU.mult)
                        frees(V.tensor_tensor(tt4[2], a[:, :], Qs[i], ALU.mult), t_freq(sg, o, f, 2))
                        frees(V.tensor_tensor(tt4[3], bb[:, :], Pn if f == 0 else Ps[i], ALU.mult), t_freq(sg, o, f, 3))
                        readout(dve, t_freq(sg, o, f, 3))
                        readout(dve, t_freq(sg, o, f, 2))
                        V.tensor_tensor(Rr[:, f, :], tt4[0], tt4[1], ALU.subtract)
                        V.tensor_tensor(Ri[:, f, :], tt4[2], tt4[3], ALU.add).then_inc(s["spectrum_ready"], 1)
                        n_freq += 1
                    for t in range(nt):
                        ti = t_inv(sg, o, t)
                        ps = filled(dve, ti)
                        V.tensor_tensor(U[:, b0 + t, 0, :], ps[:, :], U[:, b0 + t, 1 + o, :], ALU.mult).then_inc(s["z_ready"], 1)
                        dve.wait_ge(s["z_ready"], {0: o + 1, 1: 2 + 4 * o + t + 1}[sg])
                        dve.sem_inc(bank_freed[ti % 8], 1)
            inverse_root(ssy, vary, sdy, rsy, HY, "ssy_ready", "vary_ready", "sdy_ready", 1)
            dve.wait_ge(s["hyg_loaded"], 16)
            for b in range(NB):
                V.scalar_tensor_tensor(U[:, b, 0, :], U[:, b, 0, :], rsy[:, b:b + 1], hyg, ALU.mult, ALU.mult).then_inc(
                    s["yhy_ready"], 1)
            dve.wait_ge(s["mod2_loaded"], 96)
            dve.wait_ge(s["x_again"], 32)

            def out_rows(b):
                g1, scale, shift = mod2[min(b, 1)]
                for j in range(2):
                    c = slice(j * 512, (j + 1) * 512)
                    t = t_y(b, j)
                    frees(V.tensor_tensor(gy[j], filled(dve, t)[:, :], g1[:, c], ALU.mult), t)
                    readout(dve, t)
                    ins = V.tensor_tensor(X[:, b, c], X[:, b, c], gy[j], ALU.add)
                    if j == 0:
                        link(ins)
                    else:
                        ins.then_inc(s["x1_ready"], 1)
                inverse_root(ss2[:, b:b + 1], var2[:, b:b + 1], sd2[:, b:b + 1], rs2[:, b:b + 1], D,
                             "ss2_ready", "var2_ready", "sd2_ready", b + 1)
                link(V.scalar_tensor_tensor(H2[:, b, :], X[:, b, :], rs2[:, b:b + 1], scale, ALU.mult, ALU.mult))
                V.tensor_tensor(H2[:, b, :], H2[:, b, :], shift, ALU.add).then_inc(s["h2_ready"], 1)
                dve.wait_ge(s["h2_ready"], b + 1)

            def best_eight(vals, outv, outi):
                for v, o in zip(vals, outv):
                    ins = V.max(o[:, 0:8], v)
                link(ins)
                for v, o, x in zip(vals, outv, outi):
                    ins = V.max_index(x[:, 0:8], o[:, 0:8], v)
                link(ins)
                for v, o in zip(vals, outv):
                    ins = V.match_replace(v, o[:, 0:8], v, FLOAT_LOW)
                link(ins)

            def next_eight(vals, outv, outi):
                for v, o in zip(vals, outv):
                    ins = V.max(o[:, 8:16], v)
                link(ins)
                for v, o, x in zip(vals, outv, outi):
                    ins = V.max_index(x[:, 8:16], o[:, 8:16], v)
                link(ins)

            def halves(S):
                return ([S[:, q, a, :] for q in range(4) for a in range(2)], [topv[:, q, a, :] for q in range(4) for a in range(2)],
                        [topi[:, q, a, :] for q in range(4) for a in range(2)])

            pp = pairp.rearrange("p (q k) -> p q k", q=4)
            pairs = ([cand[:, q, :, :].rearrange("p i j -> p (i j)") for q in range(4)],
                     [pairv[:, q, :] for q in range(4)], [pp[:, q, :] for q in range(4)])

            def all_pairs():
                V.tensor_copy(topif, topi)
                link(V.tensor_tensor(cand, topv[:, :, 0, :].unsqueeze(3).to_broadcast([P, 4, 16, 16]),
                                     topv[:, :, 1, :].unsqueeze(2).to_broadcast([P, 4, 16, 16]), ALU.add))

            def experts(idx, gate, done, shifted):
                V.tensor_scalar(posa, pairp, 4, None, ALU.logical_shift_right)
                link(V.tensor_scalar(posb, pairp, 15, None, ALU.bitwise_and))
                V.tensor_copy(posaf, posa)
                link(V.tensor_copy(posbf, posb))
                for half, pos, sel in ((0, posaf, sel1), (1, posbf, sel2)):
                    oh = onehot.rearrange("p (q j) -> p q j", j=TOPK)
                    link(V.tensor_tensor(oh, pos.unsqueeze(2).to_broadcast([P, 64, TOPK]),
                                         iota16[:, :].unsqueeze(1).to_broadcast([P, 64, TOPK]), ALU.is_equal))
                    oh4 = onehot.rearrange("p (b q j) -> p b q j", b=4, j=TOPK)
                    link(V.tensor_tensor(oh4, oh4, topif[:, :, half, :].unsqueeze(2).to_broadcast([P, 4, TOPK, TOPK]), ALU.mult))
                    link(V.tensor_reduce(sel, oh, AX.X, ALU.add))
                V.scalar_tensor_tensor(idx, sel1.rearrange("p (q k) -> p q k", q=4), float(NKEYS),
                                       sel2.rearrange("p (q k) -> p q k", q=4), ALU.mult, ALU.add).then_inc(s[done], 1)
                V.tensor_tensor(gate, pairv, pairv[:, :, 0:1].to_broadcast([P, 4, TOPK]), ALU.subtract).then_inc(s[shifted], 1)

            def prompt_heads(g):
                readout(dve, t_sp(2 * g))
                readout(dve, t_sp(2 * g + 1))
                q = slice(4 * g, 4 * g + 4)
                best_eight(*halves(scp[:, q, :, :]))
                next_eight(*halves(scp[:, q, :, :]))
                all_pairs()
                best_eight(*pairs)
                next_eight(*pairs)
                experts(IDXP[:, q, :], GATEP[:, q, :], "prompt_topk", "prompt_pairs")
                dve.wait_ge(s["prompt_pairs"], g + 1)

            out_rows(0)
            for i in range(4):
                filled(dve, T_KEYS + i)
            prompt_heads(0)
            out_rows(1)
            prompt_heads(1)
            out_rows(2)
            dve.wait_ge(s["prompt_exp"], 1)
            link(V.tensor_reduce(gsum[:, 0:PH], GATEP, AX.X, ALU.add))
            link(V.reciprocal(grec[:, 0:PH], gsum[:, 0:PH]))
            V.tensor_tensor(GATEP, GATEP, grec[:, 0:PH].unsqueeze(2).to_broadcast([P, PH, TOPK]), ALU.mult).then_inc(
                s["prompt_gates"], 1)
            dve.wait_ge(s["prompt_gates"], 1)
            out_rows(3)
            out_rows(4)

            def prompt_dots(i, ks):
                for k in ks:
                    n = i * PSTEP + k
                    dve.wait_ge(pu_full[n % PSLOTS], 16 * (n // PSLOTS + 1))
                    V.tensor_tensor_reduce(out=pu[n % PSLOTS], in0=pu[n % PSLOTS], in1=H2[:, 0, :], scale=1.0, scalar=0.0,
                                           op0=ALU.mult, op1=ALU.add, accum_out=pdots[:, n:n + 1]).then_inc(s["pu_used"], 1)

            def prompt_sum(i):
                for j in range(2):
                    c = slice(j * 512, (j + 1) * 512)
                    t = t_pv(i, j)
                    ps = filled(dve, t)
                    if i:
                        dve.wait_ge(s["psum_ready"], 2 * i)
                        V.tensor_tensor(moe[:, 0, c], moe[:, 0, c], ps[:, :], ALU.add).then_inc(s["psum_ready"], 1)
                    else:
                        V.tensor_copy(moe[:, 0, c], ps[:, :]).then_inc(s["psum_ready"], 1)
                dve.wait_ge(s["psum_ready"], 2 * i + 2)
                dve.sem_inc(bank_freed[t_pv(i, 0) % 8], 1)
                dve.sem_inc(bank_freed[t_pv(i, 1) % 8], 1)

            for i in range(NQ + 2):
                hd = i // 2 - 1
                if i < NQ:
                    prompt_dots(i, range(0, 4))
                if i >= 2:
                    if i % 2 == 0:
                        S = sc[hd % 2]
                        readout(dve, t_s(2 * hd))
                        readout(dve, t_s(2 * hd + 1))
                        best_eight(*halves(S))
                    else:
                        best_eight(*pairs)
                if i < NQ:
                    prompt_dots(i, range(4, 8))
                if i >= 2:
                    prompt_sum(i - 2)
                    if i % 2 == 0:
                        next_eight(*halves(S))
                        all_pairs()
                    else:
                        next_eight(*pairs)
                        experts(IDX[:, :, hd, :], GATE[:, :, hd, :], "topk_done", "pair_ready")
                        dve.wait_ge(s["pair_ready"], hd + 1)
                if i < NQ:
                    c = slice(i * PSTEP, (i + 1) * PSTEP)
                    dve.wait_ge(s["pgelu_ready"], i + 1)
                    V.tensor_tensor(pwgt[:, c], pgelu[:, c], GATEP[:, :, :].rearrange("p h k -> p (h k)")[:, c], ALU.mult).then_inc(
                        s["pwgt_ready"], 1)
            dve.wait_ge(s["exp_done"], 1)
            gh = GATE[:, :, :, :].rearrange("p b h k -> p (b h) k")
            link(V.tensor_reduce(gsum, gh, AX.X, ALU.add))
            link(V.reciprocal(grec, gsum))
            V.tensor_tensor(gh, gh, grec.unsqueeze(2).to_broadcast([P, NL * PH, TOPK]), ALU.mult).then_inc(s["gates_ready"], 1)
            link(V.memset(zero, 0.0))
            filled(dve, t_pv(NQ - 1, 1))
            dve.wait_ge(s["gates_ready"], 1)
            dve.sem_inc(s["zero_ready"], 1)
            dve.sem_inc(s["urow_used"], USLOTS)
            dve.sem_inc(s["acc_free"], 1)
            chain_base = chain[0]
            IDXF = IDX.rearrange("p b h k -> p (b h k)")
            GATEF = GATE.rearrange("p b h k -> p (b h k)")
            H2F = H2.rearrange("p b d -> p (b d)")
            with dve.Fori(0, NL) as b:
                V.tensor_copy(h2cur, H2F[:, bass.ds((b + 1) * D, D)]).then_inc(s["dve_chain"], 1)
                dve.wait_ge(s["dve_chain"], chain_base + 1 + b)
                dve.sem_inc(s["pool_go"], 1)
                with dve.Fori(0, PH // 2) as hp:
                    for par in range(2):
                        chunk = b * PH + hp * 2 + par
                        dve.wait_ge(s["vrow_used"], chunk * TOPK + VSLOTS)
                        dve.sem_inc(s["pool_go"], 1)
                        V.tensor_copy(idxc[par], IDXF[:, bass.ds((b * PH + hp * 2 + par) * TOPK, TOPK)]).then_inc(s["idx_ready"], 1)
                        for k in range(TOPK):
                            dve.wait_ge(urow_full[k % USLOTS], 16 * (chunk * (TOPK // USLOTS) + k // USLOTS + 1))
                            V.tensor_tensor_reduce(out=uslot[k % USLOTS], in0=uslot[k % USLOTS], in1=h2cur, scale=1.0, scalar=0.0,
                                                   op0=ALU.mult, op1=ALU.add, accum_out=dots[par][:, k:k + 1]).then_inc(
                                s["urow_used"], 1)
                        dve.wait_ge(s["gelu_ready"], chunk + 1)
                        dve.sem_inc(s["pool_go"], 1)
                        V.tensor_tensor(wgt[par], gelu[par], GATEF[:, bass.ds((b * PH + hp * 2 + par) * TOPK, TOPK)],
                                        ALU.mult).then_inc(s["wgt_ready"], 1)
            chain[0] += NL
            dve.wait_ge(s["acc_free"], NL + 1)
            dve.wait_ge(s["mod3_loaded"], 48)
            for b in range(NB):
                link(V.tensor_tensor(moe[:, b, :], moe[:, b, :], gt2[min(b, 1)], ALU.mult))
                V.tensor_tensor(X[:, b, :], X[:, b, :], moe[:, b, :], ALU.add).then_inc(s["norm2_started"], 1)
                dve.wait_ge(s["ssf_ready"], b + 1)
                V.tensor_scalar(varf[:, b:b + 1], ssf[:, b:b + 1], 1.0 / D, EPS, ALU.mult, ALU.add).then_inc(s["varf_ready"], 1)
                dve.wait_ge(s["sdf_ready"], b + 1)
                link(V.reciprocal(rsf[:, b:b + 1], sdf[:, b:b + 1]))
                V.scalar_tensor_tensor(moe[:, b, :], X[:, b, :], rsf[:, b:b + 1], fing, ALU.mult, ALU.mult).then_inc(
                    s["y_ready"], 1)

        @block.tensor
        def _(pe):
            MM = nc.tensor.matmul

            def done(ins, t):
                ins.then_inc(bank_filled[t % 8], 1)

            def product(out, t, pairs):
                for i, (l, r) in enumerate(pairs):
                    ins = MM(out, l, r, start=(i == 0), stop=(i == len(pairs) - 1))
                done(ins, t)

            def turn(t, tiles, m=P):
                ps = free_bank(pe, t)
                for i, x in enumerate(tiles):
                    n = x.shape[0]
                    ins = nc.tensor.transpose(ps[0:m, i * P:i * P + n], x, ident[0:n, 0:n])
                done(ins, t)

            pe.wait_ge(s["c_loaded"], 32)
            turn(T_COND, [condrows])
            pe.wait_ge(s["conv_loaded"], 16)
            turn(T_CONV, [convrows])
            pe.wait_ge(s["mlp_loaded"], 128)
            for layer, w in enumerate((wf1, wf2, wf3)):
                for i, (lo, n) in enumerate(((0, P), (P, NLAT))):
                    t = T_MLP + 2 * layer + i
                    if layer:
                        pe.wait_ge(s["sin_done"], 2 * layer - 1 + i)
                    src = feat if layer == 0 else hid
                    product(free_bank(pe, t)[0:64, 0:n], t, [(w, src[:, lo:lo + n])])
            readout(pe, T_COND)
            for n in range(NADA):
                w = weight(pe, n)
                t = T_MOD + n
                product(free_bank(pe, t)[0:2, :], t, [(silu_c[:, k:16:8], w[:, k, :]) for k in range(KD)])
                filled(pe, t)
                pe.sem_inc(s["weights_used"], 1)
            for b in range(NB):
                pe.wait_ge(s["h_ready"], b + 1)
                for j in range(2):
                    turn(T_HT + 2 * b + j, [hbuf[b % 2][:, (4 * j + i) * P:(4 * j + i + 1) * P] for i in range(4)])
            for j in range(4):
                w = weight(pe, W_QKVG + j)
                for b in range(NB):
                    if j == 0:
                        readout(pe, T_HT + 2 * b)
                        readout(pe, T_HT + 2 * b + 1)
                    t = T_QKVG + j * NB + b
                    product(free_bank(pe, t)[:, :], t, [(hT[:, k, b * P:(b + 1) * P], w[:, k, :]) for k in range(KD)])
                filled(pe, t)
                pe.sem_inc(s["weights_used"], 1)
            for j, src in enumerate((qt, kt)):
                for b in range(NB):
                    if b == 0:
                        readout(pe, T_QKVG + j * NB)
                    else:
                        pe.wait_ge(s["rope_ready"], 4 * j + b)
                    turn(T_QK + j * NB + b, [src[:, b, h * P:(h + 1) * P] for h in range(NH)])
            for b in range(NB):
                readout(pe, T_QKVG + 2 * NB + b)
            for i, (b, d) in enumerate(KV):
                pe.wait_ge(s["kz_ready"], i + 1)
                ps = free_bank(pe, T_KV + i)
                for h in range(NH):
                    c = slice(h * P, (h + 1) * P)
                    ins = MM(ps[:, c], kz[i % 2][:, c], vt[:, b, c], start=True, stop=True)
                done(ins, T_KV + i)
            for b in range(NB):
                readout(pe, T_QK + b)
                readout(pe, T_QK + NB + b)
                tok = slice(b * P, (b + 1) * P)
                ps = free_bank(pe, t_score(b))
                for h in range(NH):
                    ins = MM(ps[:, h * P:(h + 1) * P], kT[:, h, tok], qT[:, h, tok], start=True, stop=True)
                done(ins, t_score(b))
                if b:
                    if b == 1:
                        for i in range(len(KV)):
                            readout(pe, T_KV + i)
                    for d, S in enumerate((Sf[b - 1], Sb[b - 1])):
                        t = t_cross(b, d)
                        ps = free_bank(pe, t)
                        for h in range(NH):
                            c = slice(h * P, (h + 1) * P)
                            ins = MM(ps[:, c], qT[:, h, tok], S[:, c], start=True, stop=True)
                        done(ins, t)
                readout(pe, t_score(b))
                ps = free_bank(pe, t_intra(b))
                for h in range(NH):
                    c = slice(h * P, (h + 1) * P)
                    ins = MM(ps[:, c], sm[b % 2][:, c], vt[:, b, c], start=True, stop=True)
                done(ins, t_intra(b))

            def rows_back(i):
                u = uT[i % 3]
                readout(pe, t_proj(i, 0))
                readout(pe, t_proj(i, 1))
                turn(t_uback(i, 0), [u[:, (1 + b) * P:(2 + b) * P] for b in range(4)])
                turn(t_uback(i, 1), [u[:, 0:P]])

            for i in range(12):
                w = weight(pe, W_HY + i // 4)
                c = slice((i % 4) * P, (i % 4 + 1) * P)
                for part, lo, n in ((0, P, NLAT), (1, 0, P)):
                    t = t_proj(i, part)
                    product(free_bank(pe, t)[:, 0:n], t, [(w[:, k, c], hT[:, k, lo:lo + n]) for k in range(KD)])
                if i % 4 == 3:
                    filled(pe, t)
                    pe.sem_inc(s["weights_used"], 1)
                if i >= 1:
                    rows_back(i - 1)
            rows_back(11)
            pe.wait_ge(s["filt_loaded"], 48)
            pe.wait_ge(s["sin_done"], 6)
            pe.wait_ge(s["dft_loaded"], 16)
            for i in range(12):
                readout(pe, t_uback(i, 0))
                readout(pe, t_uback(i, 1))
            n_filt = n_freq = n_z = 0
            for sg, (b0, nt) in enumerate(SEGS):
                dft = dftc if sg == 0 else dftl
                for o in range(2):
                    for t in range(nt):
                        tok = slice((b0 + t) * P, (b0 + t + 1) * P)
                        for d in range(2):
                            tk = t_filt(sg, o, t, d)
                            lo = (2 * d + o) * HY
                            product(free_bank(pe, tk)[:, :], tk, [(hid[:, tok], w4[:, lo:lo + HY])])
                    n_filt += nt
                    pe.wait_ge(s["filt_ready"], n_filt)
                    if n_z:
                        pe.wait_ge(s["z_ready"], n_z)
                    for f in range(nt):
                        fc = slice(f * P, (f + 1) * P)
                        for j in range(5 if f == 0 else 4):
                            tk = t_freq(sg, o, f, j)
                            ps = free_bank(pe, tk)
                            if j == 4:
                                product(ps[0:1, :], tk, [(dft[:, 1, t, 0:1], he[:, t, :]) for t in range(nt)])
                            else:
                                mat = dft[:, j % 2]
                                src = [he[:, t, :] if j == 0 else ho[:, t, :] if j == 1 else U[:, b0 + t, 0, :] for t in range(nt)]
                                product(ps[:, :], tk, [(mat[:, t, fc], src[t]) for t in range(nt)])
                    n_freq += nt
                    pe.wait_ge(s["spectrum_ready"], n_freq)
                    for t in range(nt):
                        tc = slice(t * P, (t + 1) * P)
                        tk = t_inv(sg, o, t)
                        product(free_bank(pe, tk)[:, :], tk, [(dft[:, 0, f, tc], Rr[:, f, :]) for f in range(nt)] +
                                [(dft[:, 2, f, tc], Ri[:, f, :]) for f in range(nt)])
                    n_z += nt

            def h2_turn(b):
                pe.wait_ge(s["h2_ready"], b + 1)
                for j in range(2):
                    turn(t_h2T(b, j), [H2[:, b, (4 * j + i) * P:(4 * j + i + 1) * P] for i in range(4)])

            def out_block(b, w_first):
                pe.wait_ge(s["yhy_ready"], b + 1)
                turn(t_yT(b, 0), [U[:, b, 0, i * P:(i + 1) * P] for i in range(4)])
                pe.wait_ge(s["yret_ready"], b + 1)
                turn(t_yT(b, 1), [yret[:, b, i * P:(i + 1) * P] for i in range(4)])
                readout(pe, t_yT(b, 0))
                readout(pe, t_yT(b, 1))
                for j in range(2):
                    w = weight(pe, w_first + j)
                    t = t_y(b, j)
                    product(free_bank(pe, t)[:, :], t, [(yT[b % 2][:, k, :], w[:, k, :]) for k in range(KD)])

            out_block(0, W_OUT)
            filled(pe, t_y(0, 1))
            pe.sem_inc(s["weights_used"], 2)
            pe.wait_ge(s["keys_loaded"], 16)
            for i in range(4):
                turn(T_KEYS + i, [keyraw[:, 4 * i + j, :] for j in range(4)])
            h2_turn(0)
            for i in range(4):
                readout(pe, T_KEYS + i)
            readout(pe, t_h2T(0, 0))
            readout(pe, t_h2T(0, 1))

            def prompt_scores(g):
                readout(pe, t_qp(g))
                ps = free_bank(pe, t_sp(g))
                for j in range(4):
                    i = 4 * g + j
                    ins = MM(ps[:, j * P:(j + 1) * P], qTp[:, i, :], keysT[i // 8][:, i % 8, :], start=True, stop=True)
                done(ins, t_sp(g))

            for g in range(4):
                w = weight(pe, W_QP + g)
                ps = free_bank(pe, t_qp(g))
                for j in range(4):
                    for k in range(KD):
                        ins = MM(ps[:, j * P:(j + 1) * P], w[:, k, j * P:(j + 1) * P], h2T[:, k, 0:P],
                                 start=(k == 0), stop=(k == KD - 1))
                done(ins, t_qp(g))
                filled(pe, t_qp(g))
                pe.sem_inc(s["weights_used"], 1)
                if g >= 1:
                    prompt_scores(g - 1)
            prompt_scores(3)
            for b in range(1, NB):
                out_block(b, W_OUTL)
                if b >= 2:
                    h2_turn(b - 1)
            filled(pe, t_y(NL, 1))
            pe.sem_inc(s["weights_used"], 2)
            h2_turn(NL)
            for b in range(1, NB):
                readout(pe, t_h2T(b, 0))
                readout(pe, t_h2T(b, 1))

            def prompt_row(n):
                pe.wait_ge(s["pdiag_ready"], n + 1)
                pe.wait_ge(pv_full[n % PSLOTS], 16 * (n // PSLOTS + 1))
                i, k = n // PSTEP, n % PSTEP
                for j in range(2):
                    t = t_pv(i, j)
                    ps = free_bank(pe, t) if k == 0 else bank[t % 8]
                    ins = MM(ps[:, :], diag[n % DSLOTS], pv[n % PSLOTS][:, j * 512:(j + 1) * 512],
                             start=(k == 0), stop=(k == PSTEP - 1))
                    if k == PSTEP - 1 and j == 0:
                        done(ins, t)
                ins.then_inc(s["pv_used"], 1)
                if k == PSTEP - 1:
                    pe.wait_ge(s["pv_used"], n + 1)
                    pe.sem_inc(bank_filled[t_pv(i, 1) % 8], 1)

            for i in range(NQ + 1):
                if i < NQ:
                    w = weight(pe, W_Q + i // 4)
                    ps = free_bank(pe, t_q(i))
                c = slice((i % 4) * P, (i % 4 + 1) * P)
                for k in range(KD):
                    if i < NQ:
                        ins = MM(ps[:, :], w[:, k, c], h2T[:, k, P:NT], start=(k == 0), stop=(k == KD - 1))
                        if k == KD - 1:
                            done(ins, t_q(i))
                    if i >= 1 and k == 2:
                        readout(pe, t_q(i - 1))
                        pss = free_bank(pe, t_s(i - 1))
                        for j in range(NL):
                            ins = MM(pss[:, j * P:(j + 1) * P], qTl[(i - 1) % 2][:, j * P:(j + 1) * P],
                                     keysT[(i - 1) // 8][:, (i - 1) % 8, :], start=True, stop=True)
                        done(ins, t_s(i - 1))
                    if i >= 1 and k >= 1:
                        prompt_row((i - 1) * PSTEP + k - 1)
                if i < NQ and i % 4 == 3:
                    filled(pe, t_q(i))
                    pe.sem_inc(s["weights_used"], 1)
                if i >= 1:
                    prompt_row(i * PSTEP - 1)
            for t in range(T_PEER - 8, T_PEER):
                readout(pe, t)
            pe.wait_ge(s["zero_ready"], 1)
            pe.sem_inc(s["vrow_used"], VSLOTS + TOPK)
            with pe.Fori(0, NL) as b:
                pe.wait_ge(s["acc_free"], b + 1)
                for j in range(2):
                    MM(bank[j][:, :], zero[:, 0:P], zero, start=True, stop=False)
                with pe.Fori(0, PH // 2) as hp:
                    for par in range(2):
                        chunk = b * PH + hp * 2 + par
                        for k in range(TOPK):
                            pe.wait_ge(s["diag_ready"], chunk * TOPK + k + 1)
                            pe.wait_ge(vrow_full[k % VSLOTS], 16 * (chunk * (TOPK // VSLOTS) + k // VSLOTS + 1))
                            MM(bank[0][:, :], diag[k % DSLOTS], vslot[k % VSLOTS][:, 0:512], start=False, stop=False)
                            MM(bank[1][:, :], diag[k % DSLOTS], vslot[k % VSLOTS][:, 512:D], start=False, stop=False).then_inc(
                                s["vrow_used"], 1)
                for j in range(2):
                    ins = MM(bank[j][:, :], zero[:, 0:P], zero, start=False, stop=True)
                ins.then_inc(s["acc_filled"], 1)


_IN_SHAPED = ["x_prompt", "x_sample", "w_ada", "w_in", "w_out", "peer_wq", "peer_u", "peer_v"]


def kernel(**inputs):
    import concourse.bacc as _bacc
    from concourse.bass_utils import run_bass_kernel_spmd as _run

    nc = _bacc.Bacc("TRN2", target_bir_lowering=False, num_devices=1)
    a = {k: np.asarray(v) for k, v in inputs.items()}
    laid = {
        "x_prompt": a["x_prompt"][0], "x_sample": a["x_sample"][0],
        "conds": np.concatenate([a["c_ctx"].reshape(8, P), a["c"].reshape(8, P)], axis=0),
        "w_ada": a["w_ada"][0], "b_ada": a["b_ada"], "norm1_g": a["norm1_g"], "norm2_g": a["norm2_g"],
        "w_in": a["w_in"][0], "w_out": a["w_out"][0], "peer_wq": a["peer_wq"][0],
        "conv_rows": np.concatenate([a["hy_conv_w"].reshape(36, P), a["hy_conv_b"].reshape(12, P)], axis=0),
        "hy_w1": a["hy_w1"][0], "hy_w2": a["hy_w2"][0], "hy_w3": a["hy_w3"][0], "hy_w4": a["hy_w4"][0],
        "hy_b1": a["hy_b1"].reshape(64, 1), "hy_b2": a["hy_b2"].reshape(64, 1), "hy_b3": a["hy_b3"].reshape(64, 1),
        "hy_freq": a["hy_freq"].reshape(64, 1), "hy_bias": a["hy_bias"].reshape(1, 2 * HY), "hy_norm_g": a["hy_norm_g"],
        "ret_decay_fwd": a["ret_decay_fwd"], "ret_decay_bwd": a["ret_decay_bwd"], "ret_norm_g": a["ret_norm_g"],
        "state_ret_fwd": a["state_ret_fwd"][0, 0].transpose(1, 0, 2), "state_ret_bwd": a["state_ret_bwd"][0, 0].transpose(1, 0, 2),
        "peer_keys": a["peer_keys"].reshape(16, P, P), "peer_u": a["peer_u"][0], "peer_v": a["peer_v"][0],
        "final_g": a["final_g"].reshape(1, D),
    }
    laid.update(shape_constants())
    arrays, io = {}, {}
    for name, x in laid.items():
        x = np.ascontiguousarray(x)
        arrays["in_" + name] = x
        io[name] = nc.dram_tensor("in_" + name, x.shape, mybir.dt.from_np(x.dtype), kind="ExternalInput").ap()
    io["mod_scratch"] = nc.dram_tensor("mod_scratch", (2, 6 * D), F32, kind="Internal").ap()
    outs = {"y_prompt": (P, D), "y_sample": (NLAT, D), "new_fwd": (P, NH, P), "new_bwd": (P, NH, P)}
    for name, shape in outs.items():
        io[name] = nc.dram_tensor("out_" + name, shape, F32, kind="ExternalOutput").ap()
    build_trunk_layer(nc, io)
    r = _run(nc, [arrays], core_ids=[0]).results[0]
    return (r["out_y_prompt"].reshape(1, P, D), r["out_y_sample"].reshape(1, NLAT, D),
            r["out_new_fwd"].transpose(1, 0, 2).reshape(1, 1, NH, P, P), r["out_new_bwd"].transpose(1, 0, 2).reshape(1, 1, NH, P, P))
```

```python
from contextlib import ExitStack
import math

import numpy as np
import concourse.bass as bass
from concourse import mybir

F32 = mybir.dt.float32
U32 = mybir.dt.uint32
ALU = mybir.AluOpType
ACT = mybir.ActivationFunctionType
AX = mybir.AxisListType

P = 128
D = 1024
KD = D // P
NLAT = 512
NB = 5
NT = NB * P
HY = 512
NH = 4
GRID_W = 64
PH = 8
TOPK = 16
NKEYS = 128
NEXP = NKEYS * NKEYS
EPS = 1e-6
NWSLOT = 3
USLOTS = 8
VSLOTS = 8
PSLOTS = 6
PSTEP = 8
NQ = 2 * PH
NL = NB - 1
DSLOTS = 4
MAGIC = 12582912.0
TWO_PI_PARTS = (6.28125, 0.0019350051879882812, 3.0199159819e-07)
PI_SAFE = 3.1415925
FLOAT_LOW = -3.0e38


def shape_constants():
    f8 = np.float64
    out = {}
    out["ident"] = np.eye(P)
    for name, L in (("lat", NLAT), ("ctx", P)):
        t = np.arange(L, dtype=f8)
        ang = 2.0 * np.pi * ((t[:, None] * t[None, :]) % (2 * L)) / (2 * L)
        c, s = np.cos(ang), np.sin(ang)
        s[:, 0] = (-1.0) ** t
        nt = L // P
        out["dft_" + name] = np.concatenate([
            m.reshape(nt, P, L).transpose(1, 0, 2).reshape(P, nt * L) for m in (c, s, s.T)], axis=1)
    feats, wins = [], []
    for L in (P, NLAT):
        t = np.linspace(0.0, 1.0, L, dtype=np.float32)[:, None]
        w = (np.float32(2.0 * math.pi) * np.arange(L, dtype=np.float32)[:, None] / np.float32(L)).astype(np.float32)
        f = np.linspace(1e-4, 15, 16, dtype=np.float32)[None, :]
        fw = (f * w).astype(np.float32)
        feats.append(np.concatenate([t, np.cos(fw), -np.sin(fw)], axis=-1))
        lo, hi = math.log(1e-2) / 1.5, math.log(1e-2) / 0.3
        deltas = np.abs(np.linspace(lo, hi, HY, dtype=np.float32))
        wins.append(np.exp(-t * deltas[None, :]))
    out["feat_t"] = np.concatenate(feats, axis=0).T
    win = np.concatenate(wins, axis=0).reshape(NB, P, HY)
    out["window"] = win.transpose(1, 0, 2).reshape(P, NB * HY)
    t = np.arange(NLAT)
    inv = (10000.0 ** (-np.arange(32, dtype=np.float32) / np.float32(32))).astype(np.float32)
    ang = np.concatenate([(t // GRID_W).astype(np.float32)[:, None] * inv,
                          (t % GRID_W).astype(np.float32)[:, None] * inv], axis=1)
    rope = np.stack([np.cos(ang), np.sin(ang)], axis=1).reshape(4, P, 2, 64)
    out["rope"] = rope.transpose(1, 2, 0, 3).reshape(P, 2 * 4 * 64)
    m, n = np.arange(P)[:, None], np.arange(P)[None, :]
    out["dist"] = np.concatenate([np.maximum(n - m, 0), np.maximum(m - n, 0), n >= m, m >= n], axis=1)
    cols = np.zeros((P, 8))
    i = np.arange(P)
    cols[:, 0], cols[:, 1], cols[:, 2], cols[:, 3] = i + 1, 127 - i, 128 - i, i
    for j, L in ((4, P), (6, NLAT)):
        cols[:, j] = np.where(i == 0, 1.0 / (2 * L), 2.0 / (2 * L))
        cols[:, j + 1] = np.where(i == 0, 0.0, 2.0 / (2 * L))
    out["cols"] = cols
    out["iota16"] = np.tile(np.arange(TOPK)[None, :], (P, 1))
    return {k: np.ascontiguousarray(v.astype(np.float32)) for k, v in out.items()}


def build_trunk_layer(nc, io):
    ctx = ExitStack()
    with ctx:
        def sb(name, shape, dt=F32):
            return ctx.enter_context(nc.sbuf_tensor(name, shape, dt))

        def sem(name):
            return ctx.enter_context(nc.semaphore(name))

        bank = [ctx.enter_context(nc.psum_tensor(f"bank{i}", [P, 512], F32)) for i in range(8)]

        X = sb("X", [P, NB, D])
        HA = sb("HA", [P, NB * D])
        W = sb("W", [P, NWSLOT * KD * 512])
        DA = sb("DA", [P, 6 * D])
        RA = sb("RA", [P, 15 * D])
        TA = sb("TA", [P, 6 * D])

        ident = sb("ident", [P, P])
        cols = sb("cols", [P, 8])
        iota16 = sb("iota16", [P, TOPK])
        rope = sb("rope", [P, 2, 4, 64])
        mask = sb("mask", [P, NH, P])
        hid = sb("hid", [64, NT])
        hidp = sb("peer_small", [P, 96])
        sml = sb("sml", [P, 256])

        wslot = [W[:, i * KD * 512:(i + 1) * KD * 512].rearrange("p (k n) -> p k n", k=KD) for i in range(NWSLOT)]

        def seg(area, lo, n, pat=None, **kw):
            v = area[:, lo:lo + n]
            return v.rearrange(pat, **kw) if pat else v

        silu_c = sml[:, 0:16]
        convc = sml[:, 16:64]
        bfcol = sml[0:64, 64:68]
        decay = sml[:, 68:76]
        lg = sml[:, 76:84]
        xi = sml[:, 84:92]
        zeta = sml[:, 92:100]
        chunkdec = sml[:, 100:108]
        ss1, var1, sd1, rs1 = (sml[:, 108 + 5 * i:113 + 5 * i] for i in range(4))
        sso, varo, sdo, rso = (sml[:, 128 + 4 * i:132 + 4 * i] for i in range(4))
        ssy, vary, sdy, rsy = (sml[:, 144 + 5 * i:149 + 5 * i] for i in range(4))
        ss2, var2, sd2, rs2 = (sml[:, 164 + 5 * i:169 + 5 * i] for i in range(4))
        ssf, varf, sdf, rsf = (sml[:, 184 + 5 * i:189 + 5 * i] for i in range(4))

        feat = TA[0:33, 0:NT]
        arg = TA[0:64, NT:2 * NT]
        turns = TA[0:64, 2 * NT:3 * NT]
        ef = seg(TA, 2048, 512, "p (h n) -> p h n", h=NH)
        eb = seg(TA, 2560, 512, "p (h n) -> p h n", h=NH)
        dist = seg(TA, 4096, 512, "p (a n) -> p a n", a=4)
        wf1 = TA[0:33, 4608:4672]
        wf2 = TA[0:64, 4672:4736]
        wf3 = TA[0:64, 4736:4800]
        condrows = TA[0:16, 4800:4928]
        convrows = TA[0:48, 4928:5056]
        adarows = DA[0:64, 3072:3072 + P]
        adac = seg(DA, 3200, 64)
        modc = seg(DA, 3264, 96, "p (c m) -> p c m", c=2)
        modt = DA[0:96, 3360:3360 + P]
        modrow = [DA[0:2, 3584 + 512 * i:4096 + 512 * i] for i in (0, 1, 2, 3, 0, 1, 0, 1, 0, 1, 0, 1)]
        modsum = [seg(DA, lo, D, "p (c n) -> p c n", c=2) for lo in (2 * D, 4608)]
        pick_row = sml[:, 204:208]
        hbuf = [seg(DA, 0, D), seg(DA, D, D)]
        ropt1 = seg(TA, 2048, 512, "p (h a c) -> p h a c", h=NH, a=2)
        ropt2 = seg(TA, 2560, 512, "p (h a c) -> p h a c", h=NH, a=2)
        junk1 = seg(TA, 3072, D)
        hT = seg(HA, 0, NB * D, "p (k t) -> p k t", k=KD)
        qT = seg(RA, 0, 2560, "p (h t) -> p h t", h=NH)
        kT = seg(RA, 2560, 2560, "p (h t) -> p h t", h=NH)
        kt = seg(RA, 5120, 2560, "p (b n) -> p b n", b=NB)
        vt = seg(RA, 7680, 2560, "p (b n) -> p b n", b=NB)
        gg = seg(RA, 10240, 2560, "p (b n) -> p b n", b=NB)
        qt = seg(RA, 12800, 2560, "p (b n) -> p b n", b=NB)
        yret = qt
        retg = seg(TA, 4096, 512)
        Sf = [seg(TA, i * 512, 512) for i in range(4)]
        Sb = [seg(TA, (4 + i) * 512, 512) for i in range(4)]
        kz = [seg(TA, 4096, 512), seg(TA, 4608, 512)]
        stout = seg(TA, 5120, 1024, "p (a n) -> p a n", a=2)
        sm = [seg(DA, 0, 512), seg(DA, 512, 512)]
        ob = [seg(DA, 1024, 512), seg(DA, 1536, 512)]
        junko = seg(DA, 2048, 512)
        uT = [seg(TA, i * NT, NT) for i in range(3)]
        U = seg(RA, 0, 7680, "p (b j n) -> p b j n", b=NB, j=3)
        XF = X[:, :, :].rearrange("p b d -> p (b d)")
        window = seg(XF, 0, NB * HY, "p (b n) -> p b n", b=NB)
        w4 = XF[0:64, NB * HY:NB * HY + 4 * HY]
        dftc = seg(XF, 4608, 3 * P, "p (m t n) -> p m t n", m=3, t=1)
        dftl = seg(DA, 0, 6 * D, "p (m t n) -> p m t n", m=3, t=4)
        Ps = [seg(TA, 0, 512), seg(TA, 512, 512)]
        Qs = [seg(TA, 1024, 512), seg(TA, 1536, 512)]
        Pn = seg(TA, 2048, 512)
        tt4 = [seg(TA, 2560 + 512 * i, 512) for i in range(4)]
        fbias = TA[0:1, 4608:4608 + 2 * HY]
        he = seg(RA, 7680, 2048, "p (t n) -> p t n", t=4)
        ho = seg(RA, 9728, 2048, "p (t n) -> p t n", t=4)
        Rr = seg(HA, 0, 2048, "p (t n) -> p t n", t=4)
        Ri = seg(HA, 2048, 2048, "p (t n) -> p t n", t=4)
        mod2 = [(seg(DA, 3 * c * D, D), seg(DA, (3 * c + 1) * D, D), seg(DA, (3 * c + 2) * D, D)) for c in range(2)]
        yT = [seg(TA, i * D, D, "p (k t) -> p k t", k=KD) for i in range(2)]
        junk2 = seg(TA, 2048, D)
        hyg = seg(TA, 3072, 512)
        gy = [seg(TA, 3584, 512), seg(TA, 4096, 512)]
        H2 = seg(HA, 0, NB * D, "p (b d) -> p b d", b=NB)
        h2T = seg(RA, 7680, 5120, "p (k t) -> p k t", k=KD)
        keyraw = seg(HA, D, 2048, "p (i d) -> p i d", i=NQ)
        keysT = [seg(RA, lo, 1024, "p (i n) -> p i n", i=8) for lo in (2048, 3584)]
        qTp = seg(HA, 3 * D, 2048, "p (i t) -> p i t", i=NQ)
        scp = seg(DA, 0, 2048, "p (h a n) -> p h a n", h=PH, a=2)
        qTl = [seg(TA, D + i * NLAT, NLAT) for i in range(2)]
        sc = [seg(DA, i * D, D, "p (b a n) -> p b a n", b=NL, a=2) for i in range(2)]
        topv = seg(TA, 4608, 128, "p (q a k) -> p q a k", q=4, a=2)
        topi = seg(TA, 4736, 128, "p (q a k) -> p q a k", q=4, a=2).bitcast(U32)
        topif = seg(TA, 4864, 128, "p (q a k) -> p q a k", q=4, a=2)
        pairv = seg(TA, 4992, 64, "p (q k) -> p q k", q=4)
        pairp = seg(TA, 5056, 64).bitcast(U32)
        posa = seg(TA, 5120, 64).bitcast(U32)
        posb = seg(TA, 5184, 64).bitcast(U32)
        posaf = seg(TA, 5248, 64)
        posbf = seg(TA, 5312, 64)
        sel1 = seg(TA, 5376, 64)
        sel2 = seg(TA, 5440, 64)
        gsum = seg(TA, 5504, 32)
        grec = seg(TA, 5536, 32)
        cand = seg(DA, 2 * D, D, "p (q i j) -> p q i j", q=4, i=16)
        onehot = seg(RA, 5120, D)
        pdots = seg(TA, 5568, P)
        pgelu = seg(TA, 5568 + P, P)
        pwgt = seg(TA, 5568 + 2 * P, P)
        pu = [seg(RA, 0, D), seg(RA, 6656, D), seg(RA, D, D), seg(RA, 14080, D), seg(W, 8 * D, D), seg(W, 9 * D, D)]
        pv = [seg(DA, 3 * D, D), seg(DA, 5 * D, D), seg(TA, 2 * D, D), seg(TA, 3 * D, D), seg(W, 10 * D, D), seg(W, 11 * D, D)]
        IDXP = seg(RA, 12800, P, "p (h k) -> p h k", h=PH).bitcast(U32)
        GATEP = seg(RA, 12928, P, "p (h k) -> p h k", h=PH)
        IDX = seg(RA, 13056, 512, "p (b h k) -> p b h k", b=NL, h=PH).bitcast(U32)
        GATE = seg(RA, 13568, 512, "p (b h k) -> p b h k", b=NL, h=PH)
        uslot = [seg(W, i * D, D) for i in range(USLOTS)]
        vslot = [seg(W, (USLOTS + i) * D, D) for i in range(4)] + [seg(RA, 7680 + i * D, D) for i in range(4)]
        moe = seg(TA, 0, NB * D, "p (b d) -> p b d", b=NB)
        h2cur = seg(TA, 5120, D)
        gt2 = [seg(DA, 0, D), seg(DA, D, D)]
        fing = seg(DA, 2 * D, D)
        junku = [seg(DA, 3 * D, D), seg(DA, 5 * D, D)]
        diag = [seg(DA, 4096 + i * P, P) for i in range(DSLOTS)]
        zero = seg(DA, 4608, 512)
        dots = [seg(sml, 210, TOPK), seg(sml, 226, TOPK)]
        gelu = [seg(hidp, 16 * i, TOPK) for i in range(2)]
        wgt = [seg(hidp, 32 + 16 * i, TOPK) for i in range(2)]
        idxc = [seg(hidp, 64 + 16 * i, TOPK).bitcast(U32) for i in range(2)]

        order = [("cond",), ("row", 0), ("row", 1), ("conv",), ("ada",), ("row", 2)]
        order += [("hT", b, j) for b in range(NB) for j in range(2)] + [("row", 3), ("mod1",)]
        for j in range(4):
            for b in range(NB):
                order.append(("pr", j, b))
                if j >= 2 and b == 0:
                    order.append(("mod", j - 2))
            if j >= 1:
                order += [("row", 2 + 2 * j), ("row", 3 + 2 * j)]
            if j < 3:
                order += [("mlp", j, 0), ("mlp", j, 1)]
        order += [("mod", 2)] + [("qk", j, b) for j in range(2) for b in range(NB)]
        order += [("row", 10), ("row", 11), ("mod", 3), ("modT",)]
        ticket = {name: t for t, name in enumerate(order)}
        T_COND, T_CONV, T_ADAR, T_MOD1, T_MODT = (ticket[name,] for name in ("cond", "conv", "ada", "mod1", "modT"))
        T_HT = ticket["hT", 0, 0]

        def t_row(n):
            return ticket["row", n]

        def t_pr(j, b):
            return ticket["pr", j, b]

        def t_mod(j):
            return ticket["mod", j]

        def t_mlp(layer, i):
            return ticket["mlp", layer, i]

        T_QK = ticket["qk", 0, 0]
        T_KV = len(order)
        KV = [(0, 0), (0, 1), (1, 0), (2, 0), (3, 0), (4, 1), (3, 1), (2, 1)]
        T_RET = T_KV + len(KV)

        ret_order = [("score", 0)]
        for b in range(NB):
            ret_order += [("score", b + 1)] if b + 1 < NB else []
            ret_order += [("intra", b)]
            ret_order += [("cross", b + 1, 0), ("cross", b + 1, 1)] if b + 1 < NB else []
        ret_ticket = {name: T_RET + t for t, name in enumerate(ret_order)}

        def t_score(b):
            return ret_ticket["score", b]

        def t_cross(b, d):
            return ret_ticket["cross", b, d]

        def t_intra(b):
            return ret_ticket["intra", b]

        T_HY = T_RET + len(ret_order)

        def t_proj(i, part):
            return T_HY + (0 if i == 0 else 4 * i - 2) + part

        def t_uback(i, part):
            return T_HY + (4 * i + 4 if i < 11 else 46) + part

        T_CONVL = T_HY + 48
        SEGS = [(0, 1), (1, 4)]

        STAGES = [(sg, o) for sg in range(2) for o in range(2)]
        conv_order = [("filt", 0, 0, t, d) for t in range(SEGS[0][1]) for d in range(2)]
        for n, (sg, o) in enumerate(STAGES):
            conv_order += [("freq", sg, o, f, j) for f in range(SEGS[sg][1]) for j in range(5 if f == 0 else 4)]
            if n + 1 < len(STAGES):
                s2, o2 = STAGES[n + 1]
                conv_order += [("filt", s2, o2, t, d) for t in range(SEGS[s2][1]) for d in range(2)]
            conv_order += [("inv", sg, o, t) for t in range(SEGS[sg][1])]
        conv_ticket = {name: T_CONVL + t for t, name in enumerate(conv_order)}

        def t_filt(s, o, t, d):
            return conv_ticket["filt", s, o, t, d]

        def t_freq(s, o, f, j):
            return conv_ticket["freq", s, o, f, j]

        def t_inv(s, o, t):
            return conv_ticket["inv", s, o, t]

        T_OUT = T_CONVL + len(conv_order)

        def t_yT(b, j):
            return T_OUT + (0 if b == 0 else 18 if b == 1 else 6 * b + 10) + j

        def t_y(b, j):
            return t_yT(b, 0) + 2 + j

        T_KEYS = T_OUT + 4
        T_QP = T_KEYS + 6

        def t_h2T(b, j):
            return T_KEYS + 4 + j if b == 0 else t_yT(1, 0) + 6 * b - 2 + (4 if b < NL else 0) + j

        def t_qp(g):
            return T_QP + (0 if g == 0 else 2 * g - 1)

        def t_sp(g):
            return T_QP + (2 * g + 2 if g < 3 else 7)

        T_LAT = t_h2T(NL, 1) + 1

        lat_order = [("q", 0)]
        for i in range(NQ + 1):
            lat_order += [("q", i + 1)] if i + 1 < NQ else []
            lat_order += [("s", i)] if i < NQ else []
            lat_order += [("pv", i - 1, 0), ("pv", i - 1, 1)] if i >= 1 else []
        lat_ticket = {name: T_LAT + t for t, name in enumerate(lat_order)}

        def t_q(i):
            return lat_ticket["q", i]

        def t_s(i):
            return lat_ticket["s", i]

        def t_pv(i, j):
            return lat_ticket["pv", i, j]

        T_PEER = T_LAT + len(lat_order)

        bank_filled = [sem(f"bank_filled{i}") for i in range(8)]
        bank_freed = [sem(f"bank_freed{i}") for i in range(8)]

        def free_bank(pe, t):
            if t >= 8:
                pe.wait_ge(bank_freed[t % 8], t // 8)
            return bank[t % 8]

        def filled(eng, t):
            eng.wait_ge(bank_filled[t % 8], t // 8 + 1)
            return bank[t % 8]

        def readout(eng, t):
            eng.wait_ge(bank_freed[t % 8], t // 8 + 1)

        names = """c_loaded conv_loaded mlp_loaded const_loaded decay_loaded ada_bias_loaded x_loaded x_again arg_ready
            sin_done lg_ready decays_ready masks_ready decay_exp mod1_ready mod_ready mod_stored hT_dve_ready
            hT_act_ready retg_loaded ss1_ready var1_ready sd1_ready h_ready rope_ready gate_ready state_loaded
            kz_ready stout_ready o_ready sso_ready varo_ready sdo_ready yret_ready conv_center dft_loaded filt_loaded
            bias_loaded filt_ready spectrum_ready z_ready mod2_loaded hyg_loaded ssy_ready vary_ready sdy_ready
            yhy_ready x1_ready ss2_ready var2_ready sd2_ready h2_ready keys_loaded topk_done pair_ready exp_done
            gates_ready mod3_loaded idx_ready gelu_ready wgt_ready diag_ready acc_filled acc_free vrow_used urow_used
            pool_go zero_ready mod_sum_ready varf_ready sdf_ready y_ready stored states_stored dve_chain act_chain
            prompt_topk prompt_pairs prompt_exp prompt_gates pu_used pv_used pgelu_ready pwgt_ready pdiag_ready
            psum_ready""".split()
        s = {n: sem(n) for n in names}
        w_full = [sem(f"w_full{i}") for i in range(NWSLOT)]
        w_used = [sem(f"w_used{i}") for i in range(NWSLOT)]
        pu_full = [sem(f"prompt_urow_full{i}") for i in range(PSLOTS)]
        pv_full = [sem(f"prompt_vrow_full{i}") for i in range(PSLOTS)]
        urow_full = [sem(f"urow_full{i}") for i in range(USLOTS)]
        vrow_full = [sem(f"vrow_full{i}") for i in range(VSLOTS)]

        wtiles = [(io["w_ada"], n * 512) for n in range(4)]
        w_pr, w_ada = {}, {n: n for n in range(4)}
        for what in ("q", 4, "k", 5, "v", 6, 7, "g", 8, 9):
            if isinstance(what, str):
                w_pr["qkvg".index(what)] = len(wtiles)
                wtiles.append((io["w_in"], 3 * HY + "qkvg".index(what) * 512))
            else:
                w_ada[what] = len(wtiles)
                wtiles.append((io["w_ada"], what * 512))
        w_hy = [len(wtiles), len(wtiles) + 3, len(wtiles) + 4]
        w_ada[10], w_ada[11] = len(wtiles) + 1, len(wtiles) + 2
        wtiles += [(io["w_in"], 0), (io["w_ada"], 10 * 512), (io["w_ada"], 11 * 512), (io["w_in"], 512), (io["w_in"], 2 * 512)]
        W_OUT = len(wtiles)
        wtiles += [(io["w_out"], n * 512) for n in range(2)]
        W_QP = len(wtiles)
        wtiles += [(io["peer_wq"], n * 512) for n in range(4)]
        W_OUTL = len(wtiles)
        wtiles += [(io["w_out"], n * 512) for n in range(2)]
        W_Q = len(wtiles)
        wtiles += [(io["peer_wq"], n * 512) for n in range(4)]

        slot_of = [n % NWSLOT if n < W_Q else (n - W_Q) % 2 for n in range(len(wtiles))]
        for n in range(4, 12):
            slot_of[w_ada[n]] = 2 if n < 11 else 0
        for j in range(4):
            slot_of[w_pr[j]] = (1, 0)[j % 2]
        for n in range(3):
            slot_of[w_hy[n]] = (1, 0, 2)[n]

        def weight(pe, n):
            pe.wait_ge(w_full[slot_of[n]], 16 * slot_of[:n + 1].count(slot_of[n]))
            return wslot[slot_of[n]]

        def used(eng, n):
            eng.sem_inc(w_used[slot_of[n]], 1)

        block = ctx.enter_context(nc.Block())

        @block.sync
        def _(sp):
            sp.dma_start(condrows, io["conds"]).then_inc(s["c_loaded"], 16)
            sp.dma_start(ident[:, :], io["ident"]).then_inc(s["c_loaded"], 16)
            for n, (src, lo) in enumerate(wtiles):
                i = slot_of[n]
                if i in slot_of[:n]:
                    sp.wait_ge(w_used[i], slot_of[:n].count(i))
                sp.dma_start(wslot[i], src[:, lo:lo + 512].rearrange("(k p) n -> p k n", p=P)).then_inc(w_full[i], 16)
            sp.wait_ge(s["topk_done"], PH)
            for c in range(2):
                sp.dma_start(gt2[c], io["mod_scratch"][c:c + 1, 5 * D:6 * D].to_broadcast([P, D])).then_inc(s["mod3_loaded"], 16)
            sp.dma_start(fing, io["final_g"].to_broadcast([P, D])).then_inc(s["mod3_loaded"], 16)
            for b in range(NB):
                sp.wait_ge(s["y_ready"], b + 1)
                dst = io["y_prompt"] if b == 0 else io["y_sample"][(b - 1) * P:b * P, :]
                sp.dma_start(dst, moe[:, b, :]).then_inc(s["stored"], 16)
            sp.wait_ge(s["stored"], 16 * NB)

        @block.gpsimd
        def _(g):
            g.dma_start(convrows, io["conv_rows"]).then_inc(s["conv_loaded"], 16)
            g.dma_start(adarows, io["ada_rows"]).then_inc(s["ada_bias_loaded"], 16)
            g.dma_start(X[:, 0, :], io["x_prompt"]).then_inc(s["x_loaded"], 16)
            g.dma_start(X[:, 1:NB, :], io["x_sample"].rearrange("(b p) d -> p b d", p=P)).then_inc(s["x_loaded"], 16)
            g.dma_start(dist, io["dist"].rearrange("p (a n) -> p a n", a=4)).then_inc(s["decay_loaded"], 16)
            g.dma_start(cols[:, :], io["cols"]).then_inc(s["decay_loaded"], 16)
            g.dma_start(decay[:, 0:4], io["ret_decay_fwd"].to_broadcast([P, NH])).then_inc(s["decay_loaded"], 16)
            g.dma_start(decay[:, 4:8], io["ret_decay_bwd"].to_broadcast([P, NH])).then_inc(s["decay_loaded"], 16)
            g.dma_start(rope[:, :, :, :], io["rope"].rearrange("p (a b c) -> p a b c", a=2, b=4)).then_inc(s["const_loaded"], 16)
            g.dma_start(iota16[:, :], io["iota16"]).then_inc(s["const_loaded"], 16)
            for dst, name in ((feat, "feat_t"), (wf1, "hy_w1"), (wf2, "hy_w2"), (wf3, "hy_w3")):
                g.dma_start(dst, io[name]).then_inc(s["mlp_loaded"], 16)
            for j, name in enumerate(("hy_b1", "hy_b2", "hy_b3", "hy_freq")):
                g.dma_start(bfcol[:, j:j + 1], io[name]).then_inc(s["mlp_loaded"], 16)

            def spread(dst, c, j, done):
                g.dma_start(dst, io["mod_scratch"][c:c + 1, j * D:(j + 1) * D].to_broadcast([P, D])).then_inc(s[done], 16)

            g.wait_ge(s["masks_ready"], 1)
            g.dma_start(retg, io["ret_norm_g"].to_broadcast([P, HY])).then_inc(s["retg_loaded"], 16)
            g.wait_ge(s["sin_done"], 6)
            g.dma_start(Sf[0].rearrange("p (h e) -> p h e", h=NH), io["state_ret_fwd"]).then_inc(s["state_loaded"], 16)
            g.wait_ge(s["rope_ready"], 8)
            g.wait_ge(s["h_ready"], NB)
            g.dma_start(Sb[3].rearrange("p (h e) -> p h e", h=NH), io["state_ret_bwd"]).then_inc(s["state_loaded"], 16)
            g.dma_start(window, io["window"].rearrange("p (b n) -> p b n", b=NB)).then_inc(s["filt_loaded"], 16)
            g.dma_start(w4, io["hy_w4"]).then_inc(s["filt_loaded"], 16)
            g.dma_start(dftc, io["dft_ctx"].rearrange("p (m t n) -> p m t n", m=3, t=1)).then_inc(s["filt_loaded"], 16)
            readout(g, T_MODT)
            g.dma_start(io["mod_scratch"].rearrange("c (m p) -> (c m) p", p=P), modt).then_inc(s["mod_stored"], 16)
            g.wait_ge(s["mod_stored"], 16)
            g.wait_ge(s["stout_ready"], 2)
            for d, name in ((0, "new_fwd"), (1, "new_bwd")):
                g.dma_start(io[name], stout[:, d, :].rearrange("p (h e) -> p h e", h=NH)).then_inc(s["states_stored"], 16)
            g.wait_ge(s["yret_ready"], NB)
            g.dma_start(dftl, io["dft_lat"].rearrange("p (m t n) -> p m t n", m=3, t=4)).then_inc(s["dft_loaded"], 16)
            g.wait_ge(s["states_stored"], 32)
            g.dma_start(fbias, io["hy_bias"]).then_inc(s["bias_loaded"], 16)
            g.wait_ge(s["spectrum_ready"], 10)
            g.dma_start(hyg, io["hy_norm_g"].to_broadcast([P, HY])).then_inc(s["hyg_loaded"], 16)
            g.dma_start(X[:, 0, :], io["x_prompt"]).then_inc(s["x_again"], 16)
            g.dma_start(X[:, 1:NB, :], io["x_sample"].rearrange("(b p) d -> p b d", p=P)).then_inc(s["x_again"], 16)
            for t in range(4):
                filled(g, t_inv(1, 1, t))
            for i, j in enumerate((2, 4, 3)):
                spread(mod2[0][i], 0, j, "mod2_loaded")
            g.dma_start(keyraw, io["peer_keys"].rearrange("i n d -> n i d")).then_inc(s["keys_loaded"], 16)
            for i, j in enumerate((2, 4, 3)):
                spread(mod2[1][i], 1, j, "mod2_loaded")

            g.wait_ge(s["prompt_topk"], 1)
            for i in range(NQ + 1):
                if i == NQ // 2:
                    g.wait_ge(s["prompt_topk"], 2)
                for k in range(PSTEP):
                    if i < NQ:
                        n = i * PSTEP + k
                        if n == 2:
                            g.wait_ge(s["h2_ready"], NB)
                        if n >= PSLOTS:
                            g.wait_ge(s["pu_used"], n - PSLOTS + 1)
                        g.indirect_dma_start(out=pu[n % PSLOTS], out_offset=None, in_=io["peer_u"],
                                             in_offset=bass.IndirectOffsetOnAxis(ap=IDXP[:, n // TOPK, n % TOPK:n % TOPK + 1], axis=0)
                                             ).then_inc(pu_full[n % PSLOTS], 16)
                    if i >= 1:
                        n = (i - 1) * PSTEP + k
                        if n >= PSLOTS:
                            g.wait_ge(s["pv_used"], n - PSLOTS + 1)
                        g.indirect_dma_start(out=pv[n % PSLOTS], out_offset=None, in_=io["peer_v"],
                                             in_offset=bass.IndirectOffsetOnAxis(ap=IDXP[:, n // TOPK, n % TOPK:n % TOPK + 1], axis=0)
                                             ).then_inc(pv_full[n % PSLOTS], 16)

            for i in range(NWSLOT):
                g.wait_ge(w_used[i], slot_of.count(i))
            with g.Fori(0, NL) as b:
                with g.Fori(0, PH // 2) as hp:
                    for par in range(2):
                        chunk = b * PH + hp * 2 + par
                        g.wait_ge(s["idx_ready"], chunk + 1)
                        for k in range(TOPK):
                            g.wait_ge(s["urow_used"], chunk * TOPK + k + 1)
                            g.sem_inc(s["pool_go"], 1)
                            g.indirect_dma_start(out=uslot[k % USLOTS], out_offset=None, in_=io["peer_u"],
                                                 in_offset=bass.IndirectOffsetOnAxis(ap=idxc[par][:, k:k + 1], axis=0)
                                                 ).then_inc(urow_full[k % USLOTS], 16)
                        for k in range(TOPK):
                            g.wait_ge(s["vrow_used"], chunk * TOPK + TOPK + k + 1)
                            g.sem_inc(s["pool_go"], 1)
                            g.indirect_dma_start(out=vslot[k % VSLOTS], out_offset=None, in_=io["peer_v"],
                                                 in_offset=bass.IndirectOffsetOnAxis(ap=idxc[par][:, k:k + 1], axis=0)
                                                 ).then_inc(vrow_full[k % VSLOTS], 16)

        @block.scalar
        def _(act):
            A = nc.scalar

            def copy_out(t, out, src):
                A.copy(out, src).then_inc(bank_freed[t % 8], 1)

            chain = [0]

            def link(ins):
                chain[0] += 1
                ins.then_inc(s["act_chain"], 1)
                act.wait_ge(s["act_chain"], chain[0])

            ps = filled(act, T_COND)
            A.activation(silu_c, ps[:, 0:16], ACT.Silu).then_inc(bank_freed[T_COND % 8], 1)
            ps = filled(act, T_CONV)
            copy_out(T_CONV, convc, ps[:, 0:48])
            copy_out(T_ADAR, adac, filled(act, T_ADAR)[:, 0:64])
            act.wait_ge(s["x_loaded"], 32)
            for b in range(NB):
                link(A.activation(junk1, X[:, b, :], ACT.Square, accum_out=ss1[:, b:b + 1]))
            act.sem_inc(s["ss1_ready"], 1)
            act.wait_ge(s["var1_ready"], 1)
            A.activation(sd1, var1, ACT.Sqrt).then_inc(s["sd1_ready"], 1)
            for b in range(NB):
                for j in range(2):
                    t = T_HT + 2 * b + j
                    ps = filled(act, t)
                    copy_out(t, hT[:, 4 * j:4 * j + 4, b * P:(b + 1) * P], ps[:, :].rearrange("p (k t) -> p k t", k=4))
            act.wait_ge(s["mod1_ready"], 1)
            for t in range(T_HT, T_HT + 2 * NB):
                readout(act, t)
            for k in range(KD):
                x = hT[:, k, 0:P]
                ins = A.activation(x, x, ACT.Identity, bias=modc[:, 0, k:k + 1], scale=modc[:, 0, 8 + k:9 + k])
            for k in (6, 7):
                x = hT[:, k, P:NT]
                ins = A.activation(x, x, ACT.Identity, bias=modc[:, 1, k:k + 1], scale=modc[:, 1, 8 + k:9 + k])
            ins.then_inc(s["hT_act_ready"], 1)
            act.wait_ge(s["decay_loaded"], 64)
            A.activation(decay, decay, ACT.Exp).then_inc(s["decay_exp"], 1)
            act.wait_ge(s["lg_ready"], 1)
            for h in range(NH):
                A.activation(ef[:, h, :], dist[:, 0, :], ACT.Exp, scale=lg[:, h:h + 1])
                A.activation(eb[:, h, :], dist[:, 1, :], ACT.Exp, scale=lg[:, 4 + h:5 + h])
            A.activation(xi[:, 0:4], lg[:, 0:4], ACT.Exp, scale=cols[:, 0:1])
            A.activation(zeta[:, 0:4], lg[:, 0:4], ACT.Exp, scale=cols[:, 1:2])
            A.activation(xi[:, 4:8], lg[:, 4:8], ACT.Exp, scale=cols[:, 2:3])
            A.activation(zeta[:, 4:8], lg[:, 4:8], ACT.Exp, scale=cols[:, 3:4])
            A.activation(chunkdec, lg, ACT.Exp, scale=float(P)).then_inc(s["decays_ready"], 1)
            def sines(layer):
                for i, (lo, n) in enumerate(((0, P), (P, NLAT))):
                    act.wait_ge(s["arg_ready"], 2 * layer + i + 1)
                    A.activation(hid[:, lo:lo + n], arg[:, lo:lo + n], ACT.Sin).then_inc(s["sin_done"], 1)

            t = t_pr(0, 0)
            copy_out(t, qt[:, 0, :], filled(act, t)[:, :])
            sines(0)
            t = t_pr(1, 0)
            copy_out(t, kt[:, 0, :], filled(act, t)[:, :])
            sines(1)
            for b in range(NB):
                t = t_pr(2, b)
                copy_out(t, vt[:, b, :], filled(act, t)[:, :])
            sines(2)
            for b in range(NB):
                t = t_pr(3, b)
                ps = filled(act, t)
                A.activation(gg[:, b, :], ps[:, :], ACT.Silu).then_inc(bank_freed[t % 8], 1)
            for j, dst in enumerate((qT, kT)):
                for b in range(NB):
                    t = T_QK + j * NB + b
                    ps = filled(act, t)
                    copy_out(t, dst[:, :, b * P:(b + 1) * P], ps[:, :].rearrange("p (h t) -> p h t", h=NH))
            copy_out(T_MODT, modt, filled(act, T_MODT)[0:96, 0:P])
            for b in range(NB):
                if b >= 2:
                    act.wait_ge(s["yret_ready"], b - 1)
                copy_out(t_intra(b), ob[b % 2], filled(act, t_intra(b))[:, :])
                act.wait_ge(s["o_ready"], b + 1)
                for h in range(NH):
                    ins = A.activation(junko[:, h * P:(h + 1) * P], ob[b % 2][:, h * P:(h + 1) * P], ACT.Square,
                                       accum_out=sso[:, h:h + 1])
                ins.then_inc(s["sso_ready"], 1)
                act.wait_ge(s["varo_ready"], b + 1)
                A.activation(sdo, varo, ACT.Sqrt).then_inc(s["sdo_ready"], 1)
            def rows_out(i):
                for part in range(2):
                    t = t_uback(i, part)
                    ps = filled(act, t)
                    j, c = i // 4, (i % 4) * P
                    if part == 0:
                        copy_out(t, U[:, 1:NB, j, c:c + P], ps[:, :].rearrange("p (b n) -> p b n", b=4))
                    else:
                        copy_out(t, U[:, 0, j, c:c + P], ps[:, 0:P])

            act.wait_ge(s["stout_ready"], 2)
            act.wait_ge(s["yret_ready"], NB)
            for i in range(12):
                if i >= 3:
                    filled(act, t_uback(i - 3, 1))
                for part, lo, n in ((0, P, NLAT), (1, 0, P)):
                    ps = filled(act, t_proj(i, part))
                    A.activation(uT[i % 3][:, lo:lo + n], ps[:, 0:n], ACT.Identity, bias=convc[:, 36 + i:37 + i],
                                 scale=convc[:, 12 + i:13 + i]).then_inc(s["conv_center"], 1)
                if i >= 1:
                    rows_out(i - 1)
            rows_out(11)
            n_freq = 0
            for sg, (b0, nt) in enumerate(SEGS):
                cp, cq = (cols[:, 4 + 2 * sg:5 + 2 * sg], cols[:, 5 + 2 * sg:6 + 2 * sg])
                wgt2 = 2.0 / (2 * nt * P)
                for o in range(2):
                    for f in range(nt):
                        if n_freq >= 2:
                            act.wait_ge(s["spectrum_ready"], n_freq - 1)
                        if f == 0 and n_freq >= 1:
                            act.wait_ge(s["spectrum_ready"], n_freq)
                        i = n_freq % 2
                        ps = filled(act, t_freq(sg, o, f, 0))
                        if f == 0:
                            link(A.activation(Pn, ps[:, :], ACT.Copy, scale=cp))
                        A.activation(Ps[i], ps[:, :], ACT.Copy, scale=cp if f == 0 else wgt2).then_inc(
                            bank_freed[t_freq(sg, o, f, 0) % 8], 1)
                        ps = filled(act, t_freq(sg, o, f, 1))
                        A.activation(Qs[i], ps[:, :], ACT.Copy, scale=cq if f == 0 else wgt2).then_inc(
                            bank_freed[t_freq(sg, o, f, 1) % 8], 1)
                        if f == 0:
                            t = t_freq(sg, o, 0, 4)
                            ps = filled(act, t)
                            A.activation(Pn[0:1, :], ps[0:1, :], ACT.Copy, scale=0.5 * wgt2).then_inc(bank_freed[t % 8], 1)
                        n_freq += 1
            act.wait_ge(s["z_ready"], 10)
            for b in range(NB):
                link(A.activation(junk2[:, 0:512], U[:, b, 0, :], ACT.Square, accum_out=ssy[:, b:b + 1]))
            act.sem_inc(s["ssy_ready"], 1)
            act.wait_ge(s["vary_ready"], 1)
            A.activation(sdy, vary, ACT.Sqrt).then_inc(s["sdy_ready"], 1)

            def h2T_out(b):
                for j in range(2):
                    t = t_h2T(b, j)
                    ps = filled(act, t)
                    copy_out(t, h2T[:, 4 * j:4 * j + 4, b * P:(b + 1) * P], ps[:, :].rearrange("p (k t) -> p k t", k=4))

            def out_block(b):
                for j in range(2):
                    t = t_yT(b, j)
                    if b >= 2:
                        filled(act, t_y(b - 2, 1))
                    ps = filled(act, t)
                    copy_out(t, yT[b % 2][:, 4 * j:4 * j + 4, :], ps[:, :].rearrange("p (k t) -> p k t", k=4))
                act.wait_ge(s["x1_ready"], b + 1)
                A.activation(junk2, X[:, b, :], ACT.Square, accum_out=ss2[:, b:b + 1]).then_inc(s["ss2_ready"], 1)
                act.wait_ge(s["var2_ready"], b + 1)
                A.activation(sd2[:, b:b + 1], var2[:, b:b + 1], ACT.Sqrt).then_inc(s["sd2_ready"], 1)

            out_block(0)
            for i in range(4):
                t = T_KEYS + i
                copy_out(t, keysT[i // 2][:, 4 * (i % 2):4 * (i % 2) + 4, :],
                         filled(act, t)[:, :].rearrange("p (i n) -> p i n", i=4))
            h2T_out(0)

            def prompt_scores_out(g):
                ps = filled(act, t_sp(g))
                copy_out(t_sp(g), scp[:, 2 * g:2 * g + 2, :, :], ps[:, :].rearrange("p (h a n) -> p h a n", h=2, a=2))

            for g in range(4):
                ps = filled(act, t_qp(g))
                copy_out(t_qp(g), qTp[:, 4 * g:4 * g + 4, :], ps[:, :].rearrange("p (i t) -> p i t", i=4))
                if g >= 1:
                    prompt_scores_out(g - 1)
            prompt_scores_out(3)

            def prompt_exp(g):
                act.wait_ge(s["prompt_pairs"], g + 1)
                A.activation(GATEP[:, 4 * g:4 * g + 4, :], GATEP[:, 4 * g:4 * g + 4, :], ACT.Exp).then_inc(s["prompt_exp"], 1)

            for b in range(1, NB):
                out_block(b)
                if b >= 2:
                    h2T_out(b - 1)
                if b == 3:
                    prompt_exp(0)
            h2T_out(NL)

            act.wait_ge(s["h2_ready"], NB)
            copy_out(t_q(0), qTl[0], filled(act, t_q(0))[:, :])
            for i in range(NQ + 1):
                for k in range(PSTEP):
                    if i >= 1:
                        n = (i - 1) * PSTEP + k
                        if k == 0:
                            act.wait_ge(s["pwgt_ready"], i)
                        if n >= DSLOTS:
                            act.wait_ge(s["pv_used"], n - DSLOTS + 1)
                        A.activation(diag[n % DSLOTS], ident[:, :], ACT.Copy, scale=pwgt[:, n:n + 1]).then_inc(s["pdiag_ready"], 1)
                    if k == 2 and i < NQ:
                        hd, half = i // 2, i % 2
                        if half == 0 and hd >= 2:
                            act.wait_ge(s["topk_done"], hd - 1)
                        copy_out(t_s(i), sc[hd % 2][:, :, half, :],
                                 filled(act, t_s(i))[:, :].rearrange("p (b n) -> p b n", b=NL))
                if i == 2:
                    prompt_exp(1)
                if i < NQ:
                    act.wait_ge(s["pu_used"], (i + 1) * PSTEP)
                    c = slice(i * PSTEP, (i + 1) * PSTEP)
                    A.activation(pgelu[:, c], pdots[:, c], ACT.Gelu_apprx_tanh).then_inc(s["pgelu_ready"], 1)
                if i + 1 < NQ:
                    copy_out(t_q(i + 1), qTl[(i + 1) % 2], filled(act, t_q(i + 1))[:, :])
            act.wait_ge(s["pair_ready"], PH)
            gflat = GATE[:, :, :, :].rearrange("p b h k -> p (b h k)")
            A.activation(gflat, gflat, ACT.Exp).then_inc(s["exp_done"], 1)

            act.wait_ge(s["zero_ready"], 1)
            def expert_gates(b, hp, par):
                chunk = b * PH + hp * 2 + par
                act.wait_ge(s["urow_used"], chunk * TOPK + USLOTS + TOPK)
                A.activation(gelu[par], dots[par], ACT.Gelu_apprx_tanh).then_inc(s["gelu_ready"], 1)
                act.wait_ge(s["wgt_ready"], chunk + 1)
                for k in range(TOPK):
                    act.wait_ge(s["vrow_used"], chunk * TOPK + TOPK + k + 1 + VSLOTS - DSLOTS)
                    A.activation(diag[k % DSLOTS], ident[:, :], ACT.Copy, scale=wgt[par][:, k:k + 1]).then_inc(
                        s["diag_ready"], 1)

            def final_root(blocks, n):
                act.wait_ge(s["varf_ready"], n)
                A.activation(sdf[:, blocks], varf[:, blocks], ACT.Sqrt).then_inc(s["sdf_ready"], 1)

            with act.Fori(0, NL - 1) as b:
                with act.Fori(0, PH // 2) as hp:
                    for par in range(2):
                        expert_gates(b, hp, par)
                act.wait_ge(s["acc_filled"], b + 1)
                act.sem_inc(s["act_chain"], 1)
                for j in range(2):
                    ins = A.copy(moe[:, bass.ds(b + 1, 1), j * 512:(j + 1) * 512], bank[j][:, :].unsqueeze(1))
                ins.then_inc(s["acc_free"], 1)
            expert_gates(NL - 1, 0, 0)
            final_root(slice(0, NL), 1)
            expert_gates(NL - 1, 0, 1)
            with act.Fori(1, PH // 2) as hp:
                for par in range(2):
                    expert_gates(NL - 1, hp, par)
            final_root(slice(NL, NB), 2)

        @block.vector
        def _(dve):
            V = nc.vector
            chain = [0]

            def link(ins):
                chain[0] += 1
                ins.then_inc(s["dve_chain"], 1)
                dve.wait_ge(s["dve_chain"], chain[0])

            def frees(ins, t):
                ins.then_inc(bank_freed[t % 8], 1)

            def inverse_root(ss, var, sd, rs, n, got, said, sd_done, count):
                dve.wait_ge(s[got], count)
                V.tensor_scalar(var, ss, 1.0 / n, EPS, ALU.mult, ALU.add).then_inc(s[said], 1)
                dve.wait_ge(s[sd_done], count)
                link(V.reciprocal(rs, sd))

            def mod_rows(*tiles):
                for n in tiles:
                    frees(V.tensor_copy(modrow[n], filled(dve, t_row(n))[0:2, :]), t_row(n))

            def mod_sums(n):
                w = weight(dve, w_ada[n])
                if n >= 6:
                    filled(dve, t_row(n - 2))
                acc = modsum[n % 2]
                for k in range(KD):
                    for c in range(2):
                        x = silu_c[:, 8 * c + k:8 * c + k + 1]
                        if k == 0:
                            ins = V.tensor_scalar(acc[:, c, :], w[:, k, :], x, None, ALU.mult)
                        else:
                            ins = V.scalar_tensor_tensor(acc[:, c, :], w[:, k, :], x, acc[:, c, :], ALU.mult, ALU.add)
                    link(ins)
                used(dve, w_ada[n])
                dve.sem_inc(s["mod_sum_ready"], 1)

            def mod_columns(t, first, n):
                ps = filled(dve, t)[:, 0:2 * n].rearrange("p (m c) -> p c m", c=2)
                frees(V.tensor_tensor(modc[:, :, first:first + n], ps, adac[:, first:first + n].unsqueeze(1).to_broadcast([P, 2, n]),
                                      ALU.add), t)
                readout(dve, t)

            def gain_columns(first, gain):
                m = modc[:, :, first:first + 8]
                link(V.scalar_tensor_tensor(m, m, 1.0, adac[:, gain:gain + 8].unsqueeze(1).to_broadcast([P, 2, 8]), ALU.add, ALU.mult))

            inverse_root(ss1, var1, sd1, rs1, D, "ss1_ready", "var1_ready", "sd1_ready", 1)
            mod_rows(0, 1)
            for b in range(NB):
                if b >= 2:
                    filled(dve, T_HT + 2 * (b - 2) + 1)
                V.tensor_scalar(hbuf[b % 2], X[:, b, :], rs1[:, b:b + 1], None, ALU.mult).then_inc(s["h_ready"], 1)
                if b == 1:
                    mod_rows(2)
            mod_rows(3)
            readout(dve, T_ADAR)
            mod_columns(T_MOD1, 0, 16)
            gain_columns(8, 48)
            dve.sem_inc(s["mod1_ready"], 1)
            for t in range(T_HT, T_HT + 2 * NB):
                readout(dve, t)
            for k in range(6):
                x = hT[:, k, P:NT]
                ins = V.tensor_scalar(x, x, modc[:, 1, 8 + k:9 + k], modc[:, 1, k:k + 1], ALU.mult, ALU.add)
            ins.then_inc(s["hT_dve_ready"], 1)
            def sine_argument(layer):
                for i, (lo, n) in enumerate(((0, P), (P, NLAT))):
                    t = t_mlp(layer, i)
                    if layer == 0:
                        dve.wait_ge(s["mlp_loaded"], 128)
                    ps = filled(dve, t)
                    a, k = arg[:, lo:lo + n], turns[:, lo:lo + n]
                    frees(V.tensor_scalar(a, ps[0:64, 0:n], bfcol[:, layer:layer + 1], bfcol[:, 3:4], ALU.add, ALU.mult), t)
                    readout(dve, t)
                    link(V.tensor_scalar(k, a, 1.0 / (2.0 * math.pi), MAGIC, ALU.mult, ALU.add))
                    link(V.tensor_scalar(k, k, MAGIC, None, ALU.subtract))
                    for part in TWO_PI_PARTS:
                        link(V.scalar_tensor_tensor(a, k, -part, a, ALU.mult, ALU.add))
                    V.tensor_scalar(a, a, PI_SAFE, -PI_SAFE, ALU.min, ALU.max).then_inc(s["arg_ready"], 1)
            dve.wait_ge(s["decay_exp"], 1)
            V.tensor_scalar(lg, decay, -1.0, None, ALU.mult).then_inc(s["lg_ready"], 1)
            dve.wait_ge(s["decays_ready"], 1)
            V.tensor_tensor(ef, ef, dist[:, 2, :].unsqueeze(1).to_broadcast([P, NH, P]), ALU.mult)
            V.tensor_scalar(zeta, zeta, P ** -0.5, None, ALU.mult)
            link(V.tensor_tensor(eb, eb, dist[:, 3, :].unsqueeze(1).to_broadcast([P, NH, P]), ALU.mult))
            link(V.tensor_tensor(mask[:, :, :], ef, eb, ALU.add))
            V.tensor_scalar(mask[:, :, :], mask[:, :, :], P ** -0.5, None, ALU.mult).then_inc(s["masks_ready"], 1)
            link(V.memset(pick_row, 0.0))
            V.memset(pick_row[:, 0:1], 1.0)
            link(V.memset(pick_row[:, 3:4], 1.0))
            dve.wait_ge(s["const_loaded"], 32)
            for j, dst in enumerate((qt, kt)):
                for b in range(1, NB):
                    t = t_pr(j, b)
                    ps = filled(dve, t)[:, :].rearrange("p (h a c) -> p h a c", h=NH, a=2)
                    out = dst[:, b, :].rearrange("p (h a c) -> p h a c", h=NH, a=2)
                    cos = rope[:, 0, b - 1, :].unsqueeze(1).to_broadcast([P, NH, 64])
                    sin = rope[:, 1, b - 1, :].unsqueeze(1).to_broadcast([P, NH, 64])
                    for a in range(2):
                        V.tensor_tensor(ropt1[:, :, a, :], ps[:, :, a, :], cos, ALU.mult)
                    V.tensor_tensor(ropt2[:, :, 0, :], ps[:, :, 1, :], sin, ALU.mult)
                    frees(V.tensor_tensor(ropt2[:, :, 1, :], ps[:, :, 0, :], sin, ALU.mult), t)
                    readout(dve, t)
                    V.tensor_tensor(out[:, :, 0, :], ropt1[:, :, 0, :], ropt2[:, :, 0, :], ALU.subtract)
                    V.tensor_tensor(out[:, :, 1, :], ropt1[:, :, 1, :], ropt2[:, :, 1, :], ALU.add).then_inc(s["rope_ready"], 1)
                    dve.wait_ge(s["rope_ready"], 4 * j + b)
                if j == 0:
                    mod_sums(4)
                    sine_argument(0)
                    mod_sums(5)
            mod_rows(4, 5)
            mod_sums(6)
            sine_argument(1)
            mod_sums(7)
            mod_columns(t_mod(0), 16, 8)
            mod_rows(6, 7)
            sine_argument(2)
            mod_sums(8)
            mod_sums(9)
            mod_columns(t_mod(1), 24, 8)
            mod_rows(8, 9)
            dve.wait_ge(s["retg_loaded"], 16)
            for b in range(NB):
                readout(dve, t_pr(3, b))
                V.tensor_tensor(gg[:, b, :], gg[:, b, :], retg, ALU.mult).then_inc(s["gate_ready"], 1)
            mod_columns(t_mod(2), 32, 8)
            gain_columns(32, 56)
            mod_rows(10, 11)
            mod_columns(t_mod(3), 40, 8)
            dve.sem_inc(s["mod_ready"], 1)
            dve.wait_ge(s["gate_ready"], NB)
            dve.wait_ge(s["rope_ready"], 8)
            dve.wait_ge(s["state_loaded"], 32)
            readout(dve, t_pr(1, 0))

            def state(i):
                b, d = KV[i]
                t = T_KV + i
                ps = filled(dve, t)
                if b == 0:
                    V.tensor_copy(stout[:, d, :], ps[:, :]).then_inc(s["stout_ready"], 1)
                    dve.wait_ge(s["stout_ready"], i + 1)
                    dve.sem_inc(bank_freed[t % 8], 1)
                    return
                old, new = (Sf[b - 1], Sf[b]) if d == 0 else (Sb[b - 1], Sb[b - 2])
                for h in range(NH):
                    c = slice(h * P, (h + 1) * P)
                    ins = V.scalar_tensor_tensor(new[:, c], old[:, c], chunkdec[:, 4 * d + h:4 * d + h + 1], ps[:, c],
                                                 ALU.mult, ALU.add)
                frees(ins, t)
                readout(dve, t)

            for i, (b, d) in enumerate(KV):
                if i >= 2:
                    filled(dve, T_KV + i - 2)
                V.tensor_tensor(kz[i % 2].rearrange("p (h e) -> p h e", h=NH), kt[:, b, :].rearrange("p (h e) -> p h e", h=NH),
                                zeta[:, 4 * d:4 * d + 4].unsqueeze(2).to_broadcast([P, NH, P]), ALU.mult).then_inc(s["kz_ready"], 1)
                if i >= 1:
                    state(i - 1)
            state(len(KV) - 1)
            def masked(b):
                if b >= 2:
                    filled(dve, t_intra(b - 2))
                t = t_score(b)
                frees(V.tensor_tensor(sm[b % 2], filled(dve, t)[:, :], mask[:, :, :].rearrange("p h n -> p (h n)"), ALU.mult), t)

            masked(0)
            for b in range(NB):
                if b + 1 < NB:
                    masked(b + 1)
                o = ob[b % 2]
                readout(dve, t_intra(b))
                if b == 0:
                    dve.sem_inc(s["o_ready"], 1)
                else:
                    for d in range(2):
                        t = t_cross(b, d)
                        ps = filled(dve, t)
                        for h in range(NH):
                            c = slice(h * P, (h + 1) * P)
                            ins = V.scalar_tensor_tensor(o[:, c], ps[:, c], xi[:, 4 * d + h:4 * d + h + 1], o[:, c], ALU.mult, ALU.add)
                        frees(ins, t)
                        readout(dve, t)
                    dve.sem_inc(s["o_ready"], 1)
                inverse_root(sso, varo, sdo, rso, P, "sso_ready", "varo_ready", "sdo_ready", b + 1)
                for h in range(NH):
                    c = slice(h * P, (h + 1) * P)
                    ins = V.scalar_tensor_tensor(yret[:, b, c], o[:, c], rso[:, h:h + 1], gg[:, b, c], ALU.mult, ALU.mult)
                ins.then_inc(s["yret_ready"], 1)
            for i in range(12):
                u = uT[i % 3]
                w0, w2 = convc[:, i:i + 1], convc[:, 24 + i:25 + i]
                dve.wait_ge(s["conv_center"], 2 * i + 2)
                pl, pc = filled(dve, t_proj(i, 0)), filled(dve, t_proj(i, 1))
                V.scalar_tensor_tensor(u[:, P + 1:NT], pl[:, 0:NLAT - 1], w0, u[:, P + 1:NT], ALU.mult, ALU.add)
                link(V.scalar_tensor_tensor(u[:, 1:P], pc[:, 0:P - 1], w0, u[:, 1:P], ALU.mult, ALU.add))
                frees(V.scalar_tensor_tensor(u[:, P:NT - 1], pl[:, 1:NLAT], w2, u[:, P:NT - 1], ALU.mult, ALU.add), t_proj(i, 0))
                frees(V.scalar_tensor_tensor(u[:, 0:P - 1], pc[:, 1:P], w2, u[:, 0:P - 1], ALU.mult, ALU.add), t_proj(i, 1))
            dve.wait_ge(s["filt_loaded"], 48)
            dve.wait_ge(s["bias_loaded"], 16)
            for i in range(12):
                for part in range(2):
                    readout(dve, t_uback(i, part))
            n_freq = n_filt = 0

            def filters(sg, o):
                nonlocal n_filt
                b0, nt = SEGS[sg]
                if n_freq:
                    dve.wait_ge(s["spectrum_ready"], n_freq)
                for t in range(nt):
                    hf, hb = tt4[2 * (t % 2)], tt4[2 * (t % 2) + 1]
                    tf, tb = t_filt(sg, o, t, 0), t_filt(sg, o, t, 1)
                    if n_filt >= 2:
                        dve.wait_ge(s["filt_ready"], n_filt - 1)
                    n_filt += 1
                    frees(V.tensor_tensor(hf, filled(dve, tf)[:, :], window[:, b0 + t, :], ALU.mult), tf)
                    frees(V.tensor_tensor(hb, filled(dve, tb)[:, :], window[:, b0 + t, :], ALU.mult), tb)
                    readout(dve, tf)
                    readout(dve, tb)
                    if t == 0:
                        V.tensor_tensor(hf[0:1, :], hf[0:1, :], fbias[:, o * HY:(o + 1) * HY], ALU.add)
                        link(V.memset(hb[0:1, :], 0.0))
                    V.tensor_tensor(he[:, t, :], hf, hb, ALU.add)
                    V.tensor_tensor(ho[:, t, :], hf, hb, ALU.subtract).then_inc(s["filt_ready"], 1)

            filters(*STAGES[0])
            for n, (sg, o) in enumerate(STAGES):
                b0, nt = SEGS[sg]
                for f in range(nt):
                    i = n_freq % 2
                    readout(dve, t_freq(sg, o, f, 0))
                    readout(dve, t_freq(sg, o, f, 1))
                    if f == 0:
                        readout(dve, t_freq(sg, o, 0, 4))
                        dve.wait_ge(s["filt_ready"], n_filt)
                    else:
                        dve.wait_ge(s["spectrum_ready"], n_freq)
                    a, bb = filled(dve, t_freq(sg, o, f, 2)), filled(dve, t_freq(sg, o, f, 3))
                    V.tensor_tensor(tt4[0], a[:, :], Ps[i], ALU.mult)
                    V.tensor_tensor(tt4[1], bb[:, :], Qs[i], ALU.mult)
                    frees(V.tensor_tensor(tt4[2], a[:, :], Qs[i], ALU.mult), t_freq(sg, o, f, 2))
                    frees(V.tensor_tensor(tt4[3], bb[:, :], Pn if f == 0 else Ps[i], ALU.mult), t_freq(sg, o, f, 3))
                    readout(dve, t_freq(sg, o, f, 3))
                    readout(dve, t_freq(sg, o, f, 2))
                    V.tensor_tensor(Rr[:, f, :], tt4[0], tt4[1], ALU.subtract)
                    V.tensor_tensor(Ri[:, f, :], tt4[2], tt4[3], ALU.add).then_inc(s["spectrum_ready"], 1)
                    n_freq += 1
                if n + 1 < len(STAGES):
                    filters(*STAGES[n + 1])
                for t in range(nt):
                    ti = t_inv(sg, o, t)
                    ps = filled(dve, ti)
                    V.tensor_tensor(U[:, b0 + t, 0, :], ps[:, :], U[:, b0 + t, 1 + o, :], ALU.mult).then_inc(s["z_ready"], 1)
                    dve.wait_ge(s["z_ready"], {0: o + 1, 1: 2 + 4 * o + t + 1}[sg])
                    dve.sem_inc(bank_freed[ti % 8], 1)
            inverse_root(ssy, vary, sdy, rsy, HY, "ssy_ready", "vary_ready", "sdy_ready", 1)
            dve.wait_ge(s["hyg_loaded"], 16)
            for b in range(NB):
                V.scalar_tensor_tensor(U[:, b, 0, :], U[:, b, 0, :], rsy[:, b:b + 1], hyg, ALU.mult, ALU.mult).then_inc(
                    s["yhy_ready"], 1)
            dve.wait_ge(s["mod2_loaded"], 96)
            dve.wait_ge(s["x_again"], 32)

            def out_rows(b):
                g1, scale, shift = mod2[min(b, 1)]
                for j in range(2):
                    c = slice(j * 512, (j + 1) * 512)
                    t = t_y(b, j)
                    frees(V.tensor_tensor(gy[j], filled(dve, t)[:, :], g1[:, c], ALU.mult), t)
                    readout(dve, t)
                    ins = V.tensor_tensor(X[:, b, c], X[:, b, c], gy[j], ALU.add)
                    if j == 0:
                        link(ins)
                    else:
                        ins.then_inc(s["x1_ready"], 1)
                inverse_root(ss2[:, b:b + 1], var2[:, b:b + 1], sd2[:, b:b + 1], rs2[:, b:b + 1], D,
                             "ss2_ready", "var2_ready", "sd2_ready", b + 1)
                link(V.scalar_tensor_tensor(H2[:, b, :], X[:, b, :], rs2[:, b:b + 1], scale, ALU.mult, ALU.mult))
                V.tensor_tensor(H2[:, b, :], H2[:, b, :], shift, ALU.add).then_inc(s["h2_ready"], 1)
                dve.wait_ge(s["h2_ready"], b + 1)

            def best_eight(vals, outv, outi):
                for v, o in zip(vals, outv):
                    ins = V.max(o[:, 0:8], v)
                link(ins)
                for v, o, x in zip(vals, outv, outi):
                    ins = V.max_index(x[:, 0:8], o[:, 0:8], v)
                link(ins)
                for v, o in zip(vals, outv):
                    ins = V.match_replace(v, o[:, 0:8], v, FLOAT_LOW)
                link(ins)

            def next_eight(vals, outv, outi):
                for v, o in zip(vals, outv):
                    ins = V.max(o[:, 8:16], v)
                link(ins)
                for v, o, x in zip(vals, outv, outi):
                    ins = V.max_index(x[:, 8:16], o[:, 8:16], v)
                link(ins)

            def halves(S):
                return ([S[:, q, a, :] for q in range(4) for a in range(2)], [topv[:, q, a, :] for q in range(4) for a in range(2)],
                        [topi[:, q, a, :] for q in range(4) for a in range(2)])

            pp = pairp.rearrange("p (q k) -> p q k", q=4)
            pairs = ([cand[:, q, :, :].rearrange("p i j -> p (i j)") for q in range(4)],
                     [pairv[:, q, :] for q in range(4)], [pp[:, q, :] for q in range(4)])

            def all_pairs():
                V.tensor_copy(topif, topi)
                link(V.tensor_tensor(cand, topv[:, :, 0, :].unsqueeze(3).to_broadcast([P, 4, 16, 16]),
                                     topv[:, :, 1, :].unsqueeze(2).to_broadcast([P, 4, 16, 16]), ALU.add))

            def pick(half, pos, sel):
                oh = onehot.rearrange("p (q j) -> p q j", j=TOPK)
                link(V.tensor_tensor(oh, pos.unsqueeze(2).to_broadcast([P, 64, TOPK]),
                                     iota16[:, :].unsqueeze(1).to_broadcast([P, 64, TOPK]), ALU.is_equal))
                oh4 = onehot.rearrange("p (b q j) -> p b q j", b=4, j=TOPK)
                link(V.tensor_tensor(oh4, oh4, topif[:, :, half, :].unsqueeze(2).to_broadcast([P, 4, TOPK, TOPK]), ALU.mult))
                link(V.tensor_reduce(sel, oh, AX.X, ALU.add))

            def first_keys():
                V.tensor_scalar(posa, pairp, 4, None, ALU.logical_shift_right)
                link(V.tensor_scalar(posb, pairp, 15, None, ALU.bitwise_and))
                V.tensor_copy(posaf, posa)
                link(V.tensor_copy(posbf, posb))
                pick(0, posaf, sel1)

            def experts(idx, gate, done, shifted):
                pick(1, posbf, sel2)
                V.scalar_tensor_tensor(idx, sel1.rearrange("p (q k) -> p q k", q=4), float(NKEYS),
                                       sel2.rearrange("p (q k) -> p q k", q=4), ALU.mult, ALU.add).then_inc(s[done], 1)
                V.tensor_tensor(gate, pairv, pairv[:, :, 0:1].to_broadcast([P, 4, TOPK]), ALU.subtract).then_inc(s[shifted], 1)

            def prompt_softmax(g):
                gates = GATEP[:, 4 * g:4 * g + 4, :]
                dve.wait_ge(s["prompt_exp"], g + 1)
                link(V.tensor_reduce(gsum[:, 0:4], gates, AX.X, ALU.add))
                link(V.reciprocal(grec[:, 0:4], gsum[:, 0:4]))
                V.tensor_tensor(gates, gates, grec[:, 0:4].unsqueeze(2).to_broadcast([P, 4, TOPK]), ALU.mult).then_inc(
                    s["prompt_gates"], 1)
                dve.wait_ge(s["prompt_gates"], g + 1)

            out_rows(0)
            for i in range(4):
                filled(dve, T_KEYS + i)
            readout(dve, t_sp(0))
            readout(dve, t_sp(1))
            best_eight(*halves(scp[:, 0:4, :, :]))
            next_eight(*halves(scp[:, 0:4, :, :]))
            out_rows(1)
            all_pairs()
            best_eight(*pairs)
            out_rows(2)
            next_eight(*pairs)
            first_keys()
            experts(IDXP[:, 0:4, :], GATEP[:, 0:4, :], "prompt_topk", "prompt_pairs")
            dve.wait_ge(s["prompt_pairs"], 1)
            out_rows(3)
            readout(dve, t_sp(2))
            readout(dve, t_sp(3))
            best_eight(*halves(scp[:, 4:8, :, :]))
            next_eight(*halves(scp[:, 4:8, :, :]))
            all_pairs()
            out_rows(4)
            prompt_softmax(0)

            IDXF = seg(RA, 13056, 512 + TOPK).bitcast(U32)

            def prompt_dots(i, ks):
                for k in ks:
                    n = i * PSTEP + k
                    dve.wait_ge(pu_full[n % PSLOTS], 16 * (n // PSLOTS + 1))
                    V.tensor_tensor_reduce(out=pu[n % PSLOTS], in0=pu[n % PSLOTS], in1=H2[:, 0, :], scale=1.0, scalar=0.0,
                                           op0=ALU.mult, op1=ALU.add, accum_out=pdots[:, n:n + 1]).then_inc(s["pu_used"], 1)

            def prompt_sum(i):
                for j in range(2):
                    c = slice(j * 512, (j + 1) * 512)
                    t = t_pv(i, j)
                    ps = filled(dve, t)
                    if i:
                        dve.wait_ge(s["psum_ready"], 2 * i)
                        V.tensor_tensor(moe[:, 0, c], moe[:, 0, c], ps[:, :], ALU.add).then_inc(s["psum_ready"], 1)
                    else:
                        V.tensor_copy(moe[:, 0, c], ps[:, :]).then_inc(s["psum_ready"], 1)
                dve.wait_ge(s["psum_ready"], 2 * i + 2)
                dve.sem_inc(bank_freed[t_pv(i, 0) % 8], 1)
                dve.sem_inc(bank_freed[t_pv(i, 1) % 8], 1)

            for i in range(NQ + 2):
                hd = (i - 1) // 2
                if i < NQ:
                    prompt_dots(i, range(0, 3))
                if i % 2 == 1 and hd < PH:
                    readout(dve, t_s(2 * hd))
                    readout(dve, t_s(2 * hd + 1))
                    best_eight(*halves(sc[hd % 2]))
                elif i % 2 == 0:
                    best_eight(*pairs)
                if i < NQ:
                    prompt_dots(i, range(3, 6))
                if i % 2 == 1 and hd < PH:
                    next_eight(*halves(sc[hd % 2]))
                elif i % 2 == 0:
                    next_eight(*pairs)
                    first_keys()
                if i < NQ:
                    prompt_dots(i, range(6, 8))
                    c = slice(i * PSTEP, (i + 1) * PSTEP)
                    dve.wait_ge(s["pgelu_ready"], i + 1)
                    V.tensor_tensor(pwgt[:, c], pgelu[:, c], GATEP[:, :, :].rearrange("p h k -> p (h k)")[:, c], ALU.mult).then_inc(
                        s["pwgt_ready"], 1)
                if i == NQ - 1:
                    V.tensor_copy(idxc[0], IDXF[:, 0:TOPK]).then_inc(s["idx_ready"], 1)
                    dve.sem_inc(s["urow_used"], USLOTS)
                if i >= 2:
                    prompt_sum(i - 2)
                if i == 3:
                    prompt_softmax(1)
                if i % 2 == 1 and hd < PH:
                    all_pairs()
                elif i == 0:
                    experts(IDXP[:, 4:8, :], GATEP[:, 4:8, :], "prompt_topk", "prompt_pairs")
                    dve.wait_ge(s["prompt_pairs"], 2)
                elif i % 2 == 0:
                    experts(IDX[:, :, hd, :], GATE[:, :, hd, :], "topk_done", "pair_ready")
                    dve.wait_ge(s["pair_ready"], hd + 1)
            dve.wait_ge(s["exp_done"], 1)
            gh = GATE[:, :, :, :].rearrange("p b h k -> p (b h) k")
            link(V.tensor_reduce(gsum, gh, AX.X, ALU.add))
            link(V.reciprocal(grec, gsum))
            V.tensor_tensor(gh, gh, grec.unsqueeze(2).to_broadcast([P, NL * PH, TOPK]), ALU.mult).then_inc(s["gates_ready"], 1)
            link(V.memset(zero, 0.0))
            filled(dve, t_pv(NQ - 1, 1))
            dve.wait_ge(s["gates_ready"], 1)
            dve.sem_inc(s["zero_ready"], 1)
            dve.sem_inc(s["acc_free"], 1)
            chain_base = chain[0]
            GATEF = GATE.rearrange("p b h k -> p (b h k)")
            H2F = H2.rearrange("p b d -> p (b d)")
            def expert_rows(b):
                V.tensor_copy(h2cur, H2F[:, bass.ds((b + 1) * D, D)]).then_inc(s["dve_chain"], 1)
                dve.wait_ge(s["dve_chain"], chain_base + 1 + b)
                dve.sem_inc(s["pool_go"], 1)

            def expert_dots(b, hp, par):
                chunk = b * PH + hp * 2 + par
                for k in range(TOPK):
                    dve.wait_ge(urow_full[k % USLOTS], 16 * (chunk * (TOPK // USLOTS) + k // USLOTS + 1))
                    V.tensor_tensor_reduce(out=uslot[k % USLOTS], in0=uslot[k % USLOTS], in1=h2cur, scale=1.0, scalar=0.0,
                                           op0=ALU.mult, op1=ALU.add, accum_out=dots[par][:, k:k + 1]).then_inc(
                        s["urow_used"], 1)
                dve.wait_ge(s["gelu_ready"], chunk + 1)
                dve.sem_inc(s["pool_go"], 1)
                V.tensor_tensor(wgt[par], gelu[par], GATEF[:, bass.ds((b * PH + hp * 2 + par) * TOPK, TOPK)],
                                ALU.mult).then_inc(s["wgt_ready"], 1)
                dve.wait_ge(s["vrow_used"], chunk * TOPK + TOPK + VSLOTS)
                dve.sem_inc(s["pool_go"], 1)
                V.tensor_copy(idxc[1 - par], IDXF[:, bass.ds((b * PH + hp * 2 + par + 1) * TOPK, TOPK)]).then_inc(
                    s["idx_ready"], 1)

            def final_variance(blocks):
                for b in blocks:
                    ins = V.tensor_tensor(X[:, b, :], X[:, b, :], moe[:, b, :], ALU.add)
                link(ins)
                for b in blocks:
                    link(V.tensor_tensor_reduce(out=junku[b % 2], in0=X[:, b, :], in1=X[:, b, :], scale=1.0, scalar=0.0,
                                                op0=ALU.mult, op1=ALU.add, accum_out=ssf[:, b:b + 1]))
                c = slice(blocks[0], blocks[-1] + 1)
                V.tensor_scalar(varf[:, c], ssf[:, c], 1.0 / D, EPS, ALU.mult, ALU.add).then_inc(s["varf_ready"], 1)

            def final_rows(blocks, n):
                c = slice(blocks[0], blocks[-1] + 1)
                dve.wait_ge(s["sdf_ready"], n)
                link(V.reciprocal(rsf[:, c], sdf[:, c]))
                for b in blocks:
                    V.scalar_tensor_tensor(moe[:, b, :], X[:, b, :], rsf[:, b:b + 1], fing, ALU.mult, ALU.mult).then_inc(
                        s["y_ready"], 1)

            with dve.Fori(0, NL - 1) as b:
                expert_rows(b)
                with dve.Fori(0, PH // 2) as hp:
                    for par in range(2):
                        expert_dots(b, hp, par)
            expert_rows(NL - 1)
            chain[0] += NL
            expert_dots(NL - 1, 0, 0)
            dve.wait_ge(s["acc_free"], NL)
            dve.wait_ge(s["mod3_loaded"], 48)
            for b in range(NL):
                ins = V.tensor_tensor(moe[:, b, :], moe[:, b, :], gt2[min(b, 1)], ALU.mult)
            link(ins)
            final_variance(range(NL))
            expert_dots(NL - 1, 0, 1)
            final_rows(range(NL), 1)
            with dve.Fori(1, PH // 2) as hp:
                for par in range(2):
                    expert_dots(NL - 1, hp, par)
            dve.wait_ge(s["acc_filled"], NL)
            for j in range(2):
                c = slice(j * 512, (j + 1) * 512)
                ins = V.tensor_tensor(moe[:, NL, c], bank[j][:, :], gt2[1][:, c], ALU.mult)
            link(ins)
            final_variance(range(NL, NB))
            final_rows(range(NL, NB), 2)

        @block.tensor
        def _(pe):
            MM = nc.tensor.matmul

            def done(ins, t):
                ins.then_inc(bank_filled[t % 8], 1)

            def product(out, t, pairs):
                for i, (l, r) in enumerate(pairs):
                    ins = MM(out, l, r, start=(i == 0), stop=(i == len(pairs) - 1))
                done(ins, t)

            def turn(t, tiles, m=P):
                ps = free_bank(pe, t)
                for i, x in enumerate(tiles):
                    n = x.shape[0]
                    ins = nc.tensor.transpose(ps[0:m, i * P:i * P + n], x, ident[0:n, 0:n])
                done(ins, t)

            pe.wait_ge(s["c_loaded"], 32)
            turn(T_COND, [condrows])
            def mod_row(n):
                t = t_row(n)
                if n not in range(4, 10):
                    w = weight(pe, w_ada[n])
                    product(free_bank(pe, t)[0:2, :], t, [(silu_c[:, k:16:8], w[:, k, :]) for k in range(KD)])
                    filled(pe, t)
                    used(pe, w_ada[n])
                else:
                    pe.wait_ge(s["mod_sum_ready"], n - 3)
                    product(free_bank(pe, t)[0:2, :], t, [(pick_row[:, 2 * c:2 * c + 2], modsum[n % 2][:, c, :]) for c in range(2)])

            def mod_turn(t, tiles):
                ps = free_bank(pe, t)
                for i, n in enumerate(tiles):
                    readout(pe, t_row(n))
                    for j in range(4):
                        m = 4 * i + j
                        ins = nc.tensor.transpose(ps[:, 2 * m:2 * m + 2], modrow[n][:, j * P:(j + 1) * P], ident[0:2, 0:2])
                done(ins, t)

            readout(pe, T_COND)
            mod_row(0)
            mod_row(1)
            pe.wait_ge(s["conv_loaded"], 16)
            turn(T_CONV, [convrows])
            pe.wait_ge(s["ada_bias_loaded"], 16)
            turn(T_ADAR, [adarows])
            mod_row(2)
            for b in range(NB):
                pe.wait_ge(s["h_ready"], b + 1)
                for j in range(2):
                    turn(T_HT + 2 * b + j, [hbuf[b % 2][:, (4 * j + i) * P:(4 * j + i + 1) * P] for i in range(4)])
            mod_row(3)
            mod_turn(T_MOD1, range(4))
            pe.wait_ge(s["hT_act_ready"], 1)
            pe.wait_ge(s["hT_dve_ready"], 1)
            for j in range(4):
                w = weight(pe, w_pr[j])
                for b in range(NB):
                    t = t_pr(j, b)
                    product(free_bank(pe, t)[:, :], t, [(hT[:, k, b * P:(b + 1) * P], w[:, k, :]) for k in range(KD)])
                    if j >= 2 and b == 0:
                        mod_turn(t_mod(j - 2), (2 * j, 2 * j + 1))
                filled(pe, t)
                used(pe, w_pr[j])
                if j >= 1:
                    mod_row(2 + 2 * j)
                    mod_row(3 + 2 * j)
                if j < 3:
                    pe.wait_ge(s["mlp_loaded"], 128)
                    for i, (lo, n) in enumerate(((0, P), (P, NLAT))):
                        t = t_mlp(j, i)
                        if j:
                            pe.wait_ge(s["sin_done"], 2 * j - 1 + i)
                        src = feat if j == 0 else hid
                        product(free_bank(pe, t)[0:64, 0:n], t, [((wf1, wf2, wf3)[j], src[:, lo:lo + n])])
            mod_turn(t_mod(2), (8, 9))
            for j, src in enumerate((qt, kt)):
                for b in range(NB):
                    if b == 0:
                        readout(pe, t_pr(j, 0))
                    else:
                        pe.wait_ge(s["rope_ready"], 4 * j + b)
                    turn(T_QK + j * NB + b, [src[:, b, h * P:(h + 1) * P] for h in range(NH)])
            mod_row(10)
            mod_row(11)
            mod_turn(t_mod(3), (10, 11))
            pe.wait_ge(s["mod_ready"], 1)
            turn(T_MODT, [modc.rearrange("p c m -> p (c m)")], m=96)
            for b in range(NB):
                readout(pe, t_pr(2, b))
            for i, (b, d) in enumerate(KV):
                pe.wait_ge(s["kz_ready"], i + 1)
                ps = free_bank(pe, T_KV + i)
                for h in range(NH):
                    c = slice(h * P, (h + 1) * P)
                    ins = MM(ps[:, c], kz[i % 2][:, c], vt[:, b, c], start=True, stop=True)
                done(ins, T_KV + i)
            def retention_scores(b):
                readout(pe, T_QK + b)
                readout(pe, T_QK + NB + b)
                tok = slice(b * P, (b + 1) * P)
                ps = free_bank(pe, t_score(b))
                for h in range(NH):
                    ins = MM(ps[:, h * P:(h + 1) * P], kT[:, h, tok], qT[:, h, tok], start=True, stop=True)
                done(ins, t_score(b))

            retention_scores(0)
            for b in range(NB):
                if b + 1 < NB:
                    retention_scores(b + 1)
                readout(pe, t_score(b))
                ps = free_bank(pe, t_intra(b))
                for h in range(NH):
                    c = slice(h * P, (h + 1) * P)
                    ins = MM(ps[:, c], sm[b % 2][:, c], vt[:, b, c], start=True, stop=True)
                done(ins, t_intra(b))
                if b == 0:
                    for i in range(len(KV)):
                        readout(pe, T_KV + i)
                if b + 1 < NB:
                    tok = slice((b + 1) * P, (b + 2) * P)
                    for d, S in enumerate((Sf[b], Sb[b])):
                        t = t_cross(b + 1, d)
                        ps = free_bank(pe, t)
                        for h in range(NH):
                            c = slice(h * P, (h + 1) * P)
                            ins = MM(ps[:, c], qT[:, h, tok], S[:, c], start=True, stop=True)
                        done(ins, t)

            def rows_back(i):
                u = uT[i % 3]
                readout(pe, t_proj(i, 0))
                readout(pe, t_proj(i, 1))
                turn(t_uback(i, 0), [u[:, (1 + b) * P:(2 + b) * P] for b in range(4)])
                turn(t_uback(i, 1), [u[:, 0:P]])

            for i in range(12):
                w = weight(pe, w_hy[i // 4])
                c = slice((i % 4) * P, (i % 4 + 1) * P)
                for part, lo, n in ((0, P, NLAT), (1, 0, P)):
                    t = t_proj(i, part)
                    product(free_bank(pe, t)[:, 0:n], t, [(w[:, k, c], hT[:, k, lo:lo + n]) for k in range(KD)])
                if i % 4 == 3:
                    filled(pe, t)
                    used(pe, w_hy[i // 4])
                if i >= 1:
                    rows_back(i - 1)
            rows_back(11)
            pe.wait_ge(s["filt_loaded"], 48)
            pe.wait_ge(s["sin_done"], 6)
            pe.wait_ge(s["dft_loaded"], 16)
            for i in range(12):
                readout(pe, t_uback(i, 0))
                readout(pe, t_uback(i, 1))
            n_filt = n_freq = n_z = 0

            def filters(sg, o):
                b0, nt = SEGS[sg]
                for t in range(nt):
                    tok = slice((b0 + t) * P, (b0 + t + 1) * P)
                    for d in range(2):
                        tk = t_filt(sg, o, t, d)
                        lo = (2 * d + o) * HY
                        product(free_bank(pe, tk)[:, :], tk, [(hid[:, tok], w4[:, lo:lo + HY])])

            filters(*STAGES[0])
            for n, (sg, o) in enumerate(STAGES):
                b0, nt = SEGS[sg]
                dft = dftc if sg == 0 else dftl
                n_filt += nt
                pe.wait_ge(s["filt_ready"], n_filt)
                if o:
                    pe.wait_ge(s["z_ready"], n_z)
                for f in range(nt):
                    fc = slice(f * P, (f + 1) * P)
                    for j in range(5 if f == 0 else 4):
                        tk = t_freq(sg, o, f, j)
                        ps = free_bank(pe, tk)
                        if j == 4:
                            product(ps[0:1, :], tk, [(dft[:, 1, t, 0:1], he[:, t, :]) for t in range(nt)])
                        else:
                            mat = dft[:, j % 2]
                            src = [he[:, t, :] if j == 0 else ho[:, t, :] if j == 1 else U[:, b0 + t, 0, :] for t in range(nt)]
                            product(ps[:, :], tk, [(mat[:, t, fc], src[t]) for t in range(nt)])
                n_freq += nt
                if n + 1 < len(STAGES):
                    filters(*STAGES[n + 1])
                pe.wait_ge(s["spectrum_ready"], n_freq)
                for t in range(nt):
                    tc = slice(t * P, (t + 1) * P)
                    tk = t_inv(sg, o, t)
                    product(free_bank(pe, tk)[:, :], tk, [(dft[:, 0, f, tc], Rr[:, f, :]) for f in range(nt)] +
                            [(dft[:, 2, f, tc], Ri[:, f, :]) for f in range(nt)])
                n_z += nt

            def h2_turn(b):
                pe.wait_ge(s["h2_ready"], b + 1)
                for j in range(2):
                    turn(t_h2T(b, j), [H2[:, b, (4 * j + i) * P:(4 * j + i + 1) * P] for i in range(4)])

            def out_block(b, w_first):
                pe.wait_ge(s["yhy_ready"], b + 1)
                turn(t_yT(b, 0), [U[:, b, 0, i * P:(i + 1) * P] for i in range(4)])
                pe.wait_ge(s["yret_ready"], b + 1)
                turn(t_yT(b, 1), [yret[:, b, i * P:(i + 1) * P] for i in range(4)])
                readout(pe, t_yT(b, 0))
                readout(pe, t_yT(b, 1))
                for j in range(2):
                    w = weight(pe, w_first + j)
                    t = t_y(b, j)
                    product(free_bank(pe, t)[:, :], t, [(yT[b % 2][:, k, :], w[:, k, :]) for k in range(KD)])

            out_block(0, W_OUT)
            filled(pe, t_y(0, 1))
            used(pe, W_OUT)
            used(pe, W_OUT + 1)
            pe.wait_ge(s["keys_loaded"], 16)
            for i in range(4):
                turn(T_KEYS + i, [keyraw[:, 4 * i + j, :] for j in range(4)])
            h2_turn(0)
            for i in range(4):
                readout(pe, T_KEYS + i)
            readout(pe, t_h2T(0, 0))
            readout(pe, t_h2T(0, 1))

            def prompt_scores(g):
                readout(pe, t_qp(g))
                ps = free_bank(pe, t_sp(g))
                for j in range(4):
                    i = 4 * g + j
                    ins = MM(ps[:, j * P:(j + 1) * P], qTp[:, i, :], keysT[i // 8][:, i % 8, :], start=True, stop=True)
                done(ins, t_sp(g))

            for g in range(4):
                w = weight(pe, W_QP + g)
                ps = free_bank(pe, t_qp(g))
                for j in range(4):
                    for k in range(KD):
                        ins = MM(ps[:, j * P:(j + 1) * P], w[:, k, j * P:(j + 1) * P], h2T[:, k, 0:P],
                                 start=(k == 0), stop=(k == KD - 1))
                done(ins, t_qp(g))
                filled(pe, t_qp(g))
                used(pe, W_QP + g)
                if g >= 1:
                    prompt_scores(g - 1)
            prompt_scores(3)
            for b in range(1, NB):
                out_block(b, W_OUTL)
                if b >= 2:
                    h2_turn(b - 1)
            filled(pe, t_y(NL, 1))
            used(pe, W_OUTL)
            used(pe, W_OUTL + 1)
            h2_turn(NL)
            for b in range(1, NB):
                readout(pe, t_h2T(b, 0))
                readout(pe, t_h2T(b, 1))

            def prompt_row(n):
                pe.wait_ge(s["pdiag_ready"], n + 1)
                pe.wait_ge(pv_full[n % PSLOTS], 16 * (n // PSLOTS + 1))
                i, k = n // PSTEP, n % PSTEP
                for j in range(2):
                    t = t_pv(i, j)
                    ps = free_bank(pe, t) if k == 0 else bank[t % 8]
                    ins = MM(ps[:, :], diag[n % DSLOTS], pv[n % PSLOTS][:, j * 512:(j + 1) * 512],
                             start=(k == 0), stop=(k == PSTEP - 1))
                    if k == PSTEP - 1 and j == 0:
                        done(ins, t)
                ins.then_inc(s["pv_used"], 1)
                if k == PSTEP - 1:
                    pe.wait_ge(s["pv_used"], n + 1)
                    pe.sem_inc(bank_filled[t_pv(i, 1) % 8], 1)

            w = weight(pe, W_Q)
            product(free_bank(pe, t_q(0))[:, :], t_q(0), [(w[:, k, 0:P], h2T[:, k, P:NT]) for k in range(KD)])
            for i in range(NQ + 1):
                q = i + 1
                if q < NQ:
                    w = weight(pe, W_Q + q // 4)
                    ps = free_bank(pe, t_q(q))
                c = slice((q % 4) * P, (q % 4 + 1) * P)
                for k in range(KD):
                    if q < NQ:
                        ins = MM(ps[:, :], w[:, k, c], h2T[:, k, P:NT], start=(k == 0), stop=(k == KD - 1))
                        if k == KD - 1:
                            done(ins, t_q(q))
                    if i < NQ and k == 2:
                        readout(pe, t_q(i))
                        pss = free_bank(pe, t_s(i))
                        for j in range(NL):
                            ins = MM(pss[:, j * P:(j + 1) * P], qTl[i % 2][:, j * P:(j + 1) * P],
                                     keysT[i // 8][:, i % 8, :], start=True, stop=True)
                        done(ins, t_s(i))
                    if i >= 1 and k >= 1:
                        prompt_row((i - 1) * PSTEP + k - 1)
                if q < NQ and q % 4 == 3:
                    filled(pe, t_q(q))
                    used(pe, W_Q + q // 4)
                if i >= 1:
                    prompt_row(i * PSTEP - 1)
            for t in range(T_PEER - 8, T_PEER):
                readout(pe, t)
            pe.wait_ge(s["zero_ready"], 1)
            pe.sem_inc(s["vrow_used"], VSLOTS + TOPK)
            with pe.Fori(0, NL) as b:
                pe.wait_ge(s["acc_free"], b + 1)
                for j in range(2):
                    MM(bank[j][:, :], zero[:, 0:P], zero, start=True, stop=False)
                with pe.Fori(0, PH // 2) as hp:
                    for par in range(2):
                        chunk = b * PH + hp * 2 + par
                        for k in range(TOPK):
                            pe.wait_ge(s["diag_ready"], chunk * TOPK + k + 1)
                            pe.wait_ge(vrow_full[k % VSLOTS], 16 * (chunk * (TOPK // VSLOTS) + k // VSLOTS + 1))
                            MM(bank[0][:, :], diag[k % DSLOTS], vslot[k % VSLOTS][:, 0:512], start=False, stop=False)
                            MM(bank[1][:, :], diag[k % DSLOTS], vslot[k % VSLOTS][:, 512:D], start=False, stop=False).then_inc(
                                s["vrow_used"], 1)
                for j in range(2):
                    ins = MM(bank[j][:, :], zero[:, 0:P], zero, start=False, stop=True)
                ins.then_inc(s["acc_filled"], 1)


_IN_SHAPED = ["x_prompt", "x_sample", "w_ada", "w_in", "w_out", "peer_wq", "peer_u", "peer_v"]


def kernel(**inputs):
    import concourse.bacc as _bacc
    from concourse.bass_utils import run_bass_kernel_spmd as _run

    nc = _bacc.Bacc("TRN2", target_bir_lowering=False, num_devices=1)
    a = {k: np.asarray(v) for k, v in inputs.items()}
    laid = {
        "x_prompt": a["x_prompt"][0], "x_sample": a["x_sample"][0],
        "conds": np.concatenate([a["c_ctx"].reshape(8, P), a["c"].reshape(8, P)], axis=0),
        "w_ada": a["w_ada"][0],
        "ada_rows": np.concatenate([a["b_ada"].reshape(48, P), a["norm1_g"].reshape(8, P), a["norm2_g"].reshape(8, P)], axis=0),
        "w_in": a["w_in"][0], "w_out": a["w_out"][0], "peer_wq": a["peer_wq"][0],
        "conv_rows": np.concatenate([a["hy_conv_w"].reshape(36, P), a["hy_conv_b"].reshape(12, P)], axis=0),
        "hy_w1": a["hy_w1"][0], "hy_w2": a["hy_w2"][0], "hy_w3": a["hy_w3"][0], "hy_w4": a["hy_w4"][0],
        "hy_b1": a["hy_b1"].reshape(64, 1), "hy_b2": a["hy_b2"].reshape(64, 1), "hy_b3": a["hy_b3"].reshape(64, 1),
        "hy_freq": a["hy_freq"].reshape(64, 1), "hy_bias": a["hy_bias"].reshape(1, 2 * HY), "hy_norm_g": a["hy_norm_g"],
        "ret_decay_fwd": a["ret_decay_fwd"], "ret_decay_bwd": a["ret_decay_bwd"], "ret_norm_g": a["ret_norm_g"],
        "state_ret_fwd": a["state_ret_fwd"][0, 0].transpose(1, 0, 2), "state_ret_bwd": a["state_ret_bwd"][0, 0].transpose(1, 0, 2),
        "peer_keys": a["peer_keys"].reshape(16, P, P), "peer_u": a["peer_u"][0], "peer_v": a["peer_v"][0],
        "final_g": a["final_g"].reshape(1, D),
    }
    laid.update(shape_constants())
    arrays, io = {}, {}
    for name, x in laid.items():
        x = np.ascontiguousarray(x)
        arrays["in_" + name] = x
        io[name] = nc.dram_tensor("in_" + name, x.shape, mybir.dt.from_np(x.dtype), kind="ExternalInput").ap()
    io["mod_scratch"] = nc.dram_tensor("mod_scratch", (2, 6 * D), F32, kind="Internal").ap()
    outs = {"y_prompt": (P, D), "y_sample": (NLAT, D), "new_fwd": (P, NH, P), "new_bwd": (P, NH, P)}
    for name, shape in outs.items():
        io[name] = nc.dram_tensor("out_" + name, shape, F32, kind="ExternalOutput").ap()
    build_trunk_layer(nc, io)
    r = _run(nc, [arrays], core_ids=[0]).results[0]
    return (r["out_y_prompt"].reshape(1, P, D), r["out_y_sample"].reshape(1, NLAT, D),
            r["out_new_fwd"].transpose(1, 0, 2).reshape(1, 1, NH, P, P), r["out_new_bwd"].transpose(1, 0, 2).reshape(1, 1, NH, P, P))
```
